# Optimizing a Trainium2 kernel written in Bass

```python
import jax, jax.numpy as jnp
from jax import lax
import numpy as np

D_MODEL = 1024
BATCH = 1
SEQ = 256
DEPTH = 1

N_META = 16
EPS = 1e-6

SB_HEADS = 8
SB_HEAD_DIM = D_MODEL // 16
SB_WIDTH = SB_HEADS * SB_HEAD_DIM
SB_BLOCK = 128

GLA_HEADS = 4
GLA_DV = D_MODEL // 8
GLA_DK = GLA_DV // 2
GLA_WIDTH = GLA_HEADS * GLA_DV
GLA_KW = GLA_HEADS * GLA_DK
GLA_GATE_RANK = 16
GLA_TAU = 16.0
GLA_CHUNK = 64

MIX_WIDTH = SB_WIDTH + GLA_WIDTH
IN_SPLITS = [SB_WIDTH, SB_WIDTH, SB_WIDTH, GLA_KW, GLA_KW, GLA_WIDTH, GLA_WIDTH, GLA_GATE_RANK]
IN_COLS = sum(IN_SPLITS)

PEER_HEADS = 8
PEER_NKEYS = 128
PEER_TOPK = 16
PEER_QDIM = 128
PEER_HALF = PEER_QDIM // 2
N_EXPERTS = PEER_NKEYS * PEER_NKEYS
PEER_BLOCK = 256


def rmsnorm(x, g):
    xf = x.astype(jnp.float32)
    y = xf * lax.rsqrt(jnp.mean(xf * xf, axis=-1, keepdims=True) + EPS)
    return (y * g.astype(jnp.float32)).astype(x.dtype)

def split_heads(t, n):
    b, l, _ = t.shape
    return t.reshape(b, l, n, -1).transpose(0, 2, 1, 3)

def merge_heads(t):
    b, h, l, d = t.shape
    return t.transpose(0, 2, 1, 3).reshape(b, l, h * d)

def sb_query_block(q_blk, q_pos, k, v):
    L = k.shape[2]
    z = jnp.einsum('bhqd,bhkd->bhqk', q_blk, k).astype(jnp.float32) * (SB_HEAD_DIM ** -0.5)
    mask = jnp.arange(L)[None, :] < q_pos[:, None]
    log_1m = jnp.where(mask, jax.nn.log_sigmoid(-z), 0.0)
    between = lax.cumsum(log_1m, axis=3, reverse=True) - log_1m
    a = jnp.where(mask, jnp.exp(jax.nn.log_sigmoid(z) + between), 0.0)
    return jnp.einsum('bhqk,bhkd->bhqd', a, v.astype(jnp.float32)).astype(v.dtype)

def stick_breaking_attention(q, k, v):
    b, h, L, d = q.shape
    n_real = L - N_META
    o_meta = sb_query_block(q[:, :, :N_META], jnp.arange(N_META), k, v)
    starts = N_META + jnp.arange(n_real // SB_BLOCK) * SB_BLOCK

    def body(start):
        qb = lax.dynamic_slice_in_dim(q, start, SB_BLOCK, axis=2)
        return sb_query_block(qb, start + jnp.arange(SB_BLOCK), k, v)

    o_real = lax.map(body, starts)
    o_real = jnp.moveaxis(o_real, 0, 2).reshape(b, h, n_real, d)
    return jnp.concatenate([o_meta, o_real], axis=2)

def gla_chunk(state, xs):
    q, k, v, lg = xs
    C = q.shape[2]
    bcum = jnp.cumsum(lg, axis=2)
    o_inter = jnp.einsum('bhtd,bhde->bhte', q * jnp.exp(bcum), state)
    causal = (jnp.arange(C)[:, None] >= jnp.arange(C)[None, :])[:, :, None]
    diff = bcum[:, :, :, None, :] - bcum[:, :, None, :, :]
    decay = jnp.where(causal, jnp.exp(jnp.where(causal, diff, 0.0)), 0.0)
    attn = jnp.einsum('bhtd,bhsd,bhtsd->bhts', q, k, decay)
    o = o_inter + jnp.einsum('bhts,bhse->bhte', attn, v)
    b_last = bcum[:, :, -1:, :]
    new_state = jnp.exp(b_last[:, :, 0, :])[..., None] * state + \
        jnp.einsum('bhsd,bhse->bhde', k * jnp.exp(b_last - bcum), v)
    return new_state, o

def gated_linear_attention(q, k, v, lg):
    out_dtype = v.dtype
    q, k, v, lg = (t.astype(jnp.float32) for t in (q, k, v, lg))
    b, h, L, dk = q.shape
    dv = v.shape[-1]
    n_real = L - N_META
    n_chunks = n_real // GLA_CHUNK
    state0 = jnp.zeros((b, h, dk, dv), jnp.float32)
    state, o_meta = gla_chunk(state0, (q[:, :, :N_META], k[:, :, :N_META], v[:, :, :N_META], lg[:, :, :N_META]))

    def to_chunks(t):
        return jnp.moveaxis(t[:, :, N_META:].reshape(b, h, n_chunks, GLA_CHUNK, t.shape[-1]), 2, 0)

    _, o_real = lax.scan(gla_chunk, state, (to_chunks(q), to_chunks(k), to_chunks(v), to_chunks(lg)))
    o_real = jnp.moveaxis(o_real, 0, 2).reshape(b, h, n_real, dv)
    return jnp.concatenate([o_meta, o_real], axis=2).astype(out_dtype)

def hybrid_mixer(hn, w_in, w_gate_up, b_gate_up, sb_norm_g, gla_norm_g, w_out):
    proj = hn @ w_in
    offsets = list(np.cumsum(IN_SPLITS)[:-1])
    sbq, sbk, sbv, gq, gk, gv, gr, glr = jnp.split(proj, offsets, axis=-1)
    sb_o = stick_breaking_attention(split_heads(sbq, SB_HEADS), split_heads(sbk, SB_HEADS),
                                    split_heads(sbv, SB_HEADS))
    sb_o = merge_heads(rmsnorm(sb_o, sb_norm_g.reshape(SB_HEADS, 1, SB_HEAD_DIM)))
    lg = jax.nn.log_sigmoid((glr @ w_gate_up + b_gate_up).astype(jnp.float32)) / GLA_TAU
    gla_o = gated_linear_attention(split_heads(gq, GLA_HEADS) * (GLA_DK ** -0.5),
                                   split_heads(gk, GLA_HEADS), split_heads(gv, GLA_HEADS),
                                   split_heads(lg, GLA_HEADS))
    gla_o = merge_heads(rmsnorm(gla_o, gla_norm_g.reshape(GLA_HEADS, 1, GLA_DV))) * jax.nn.silu(gr)
    return jnp.concatenate([sb_o, gla_o], axis=-1) @ w_out

def peer_ffn(hn, w_peer_q, sub_keys1, sub_keys2, expert_u, expert_v):
    b, L, d = hn.shape
    t = hn.reshape(b * L, d)
    T = t.shape[0]
    q = (t @ w_peer_q).reshape(T, PEER_HEADS, 2, PEER_HALF)
    s1 = jnp.einsum('thd,hkd->thk', q[:, :, 0], sub_keys1).astype(jnp.float32)
    s2 = jnp.einsum('thd,hkd->thk', q[:, :, 1], sub_keys2).astype(jnp.float32)
    v1, i1 = lax.top_k(s1, PEER_TOPK)
    v2, i2 = lax.top_k(s2, PEER_TOPK)
    cand = (v1[..., :, None] + v2[..., None, :]).reshape(T, PEER_HEADS, PEER_TOPK * PEER_TOPK)
    cidx = (i1[..., :, None] * PEER_NKEYS + i2[..., None, :]).reshape(T, PEER_HEADS, PEER_TOPK * PEER_TOPK)
    sc, pos = lax.top_k(cand, PEER_TOPK)
    eidx = jnp.take_along_axis(cidx, pos, axis=-1).reshape(T, PEER_HEADS * PEER_TOPK)
    gates = jax.nn.softmax(sc, axis=-1).reshape(T, PEER_HEADS * PEER_TOPK).astype(hn.dtype)
    n_blocks = -(-T // PEER_BLOCK)
    pad = n_blocks * PEER_BLOCK - T
    tb = jnp.pad(t, ((0, pad), (0, 0))).reshape(n_blocks, PEER_BLOCK, d)
    eb = jnp.pad(eidx, ((0, pad), (0, 0))).reshape(n_blocks, PEER_BLOCK, -1)
    gb = jnp.pad(gates, ((0, pad), (0, 0))).reshape(n_blocks, PEER_BLOCK, -1)

    def block(args):
        xt, e, g = args
        act = jax.nn.gelu(jnp.einsum('nkd,nd->nk', expert_u[e], xt), approximate=False)
        return jnp.einsum('nk,nkd->nd', g * act, expert_v[e])

    y = lax.map(block, (tb, eb, gb)).reshape(n_blocks * PEER_BLOCK, d)[:T]
    return y.reshape(b, L, d)

def first_inputs(seed: int = 0) -> dict:
    key = jax.random.key(seed)
    ks = jax.random.split(key, 20)
    n = jax.random.normal
    f = jnp.float32
    return {
        "x": n(ks[0], (BATCH, SEQ, D_MODEL), f),
        "meta_tokens": n(ks[1], (N_META, D_MODEL), f),
        "norm1_g": 1.0 + 0.02 * n(ks[2], (DEPTH, D_MODEL), f),
        "w_in": n(ks[3], (DEPTH, D_MODEL, IN_COLS), f) * D_MODEL ** -0.5,
        "w_gate_up": n(ks[4], (DEPTH, GLA_GATE_RANK, GLA_KW), f) * GLA_GATE_RANK ** -0.5,
        "b_gate_up": 0.1 * n(ks[5], (DEPTH, GLA_KW), f),
        "sb_norm_g": 1.0 + 0.02 * n(ks[6], (DEPTH, SB_WIDTH), f),
        "gla_norm_g": 1.0 + 0.02 * n(ks[7], (DEPTH, GLA_WIDTH), f),
        "w_out": n(ks[8], (DEPTH, MIX_WIDTH, D_MODEL), f) * MIX_WIDTH ** -0.5,
        "norm2_g": 1.0 + 0.02 * n(ks[9], (DEPTH, D_MODEL), f),
        "w_peer_q": n(ks[10], (DEPTH, D_MODEL, PEER_HEADS * PEER_QDIM), f) * D_MODEL ** -0.5,
        "sub_keys1": n(ks[11], (DEPTH, PEER_HEADS, PEER_NKEYS, PEER_HALF), f) * PEER_HALF ** -0.5,
        "sub_keys2": n(ks[12], (DEPTH, PEER_HEADS, PEER_NKEYS, PEER_HALF), f) * PEER_HALF ** -0.5,
        "expert_u": n(ks[13], (DEPTH, N_EXPERTS, D_MODEL), f) * D_MODEL ** -0.5,
        "expert_v": n(ks[14], (DEPTH, N_EXPERTS, D_MODEL), f) * PEER_HEADS ** -0.5,
        "norm_f_g": 1.0 + 0.02 * n(ks[15], (D_MODEL,), f),
    }

def first_block(x, meta_tokens, norm1_g, w_in, w_gate_up, b_gate_up, sb_norm_g, gla_norm_g, w_out,
              norm2_g, w_peer_q, sub_keys1, sub_keys2, expert_u, expert_v, norm_f_g):
    b = x.shape[0]
    meta = jnp.broadcast_to(meta_tokens.astype(x.dtype)[None], (b, N_META, x.shape[-1]))
    h = jnp.concatenate([meta, x], axis=1)
    for l in range(DEPTH):
        h = h + hybrid_mixer(rmsnorm(h, norm1_g[l]), w_in[l], w_gate_up[l], b_gate_up[l],
                             sb_norm_g[l], gla_norm_g[l], w_out[l])
        h = h + peer_ffn(rmsnorm(h, norm2_g[l]), w_peer_q[l], sub_keys1[l], sub_keys2[l],
                         expert_u[l], expert_v[l])
    return rmsnorm(h, norm_f_g)[:, N_META:]


HEAD_DIM = 64
ATTN_HEADS = (D_MODEL // 2) // HEAD_DIM
KV_HEADS = 2
GQA_GROUP = ATTN_HEADS // KV_HEADS
ATTN_WIDTH = ATTN_HEADS * HEAD_DIM
KV_WIDTH = KV_HEADS * HEAD_DIM
LRU_WIDTH = D_MODEL // 2
LRU_BLOCKS = 8
LRU_BLOCK = LRU_WIDTH // LRU_BLOCKS
LRU_C = 8.0
CONV_WIDTH = 4
WINDOW = 128
BLOCK = 128
PAD = BLOCK - N_META
MIX_WIDTH_2 = ATTN_WIDTH + LRU_WIDTH
IN_WIDTH = ATTN_WIDTH + 2 * KV_WIDTH + 2 * LRU_WIDTH
D_FF = 4 * D_MODEL
NEG = -1e30


def rmsnorm_2(x, g):
    xf = x.astype(jnp.float32)
    y = xf * lax.rsqrt(jnp.mean(xf * xf, axis=-1, keepdims=True) + EPS)
    return (y * g.astype(jnp.float32)).astype(x.dtype)

def causal_depthwise_conv(x, w, b):
    c = x.shape[-1]
    y = lax.conv_general_dilated(
        x, w[:, None, :].astype(x.dtype), window_strides=(1,),
        padding=[(CONV_WIDTH - 1, 0)],
        dimension_numbers=("NWC", "WIO", "NWC"), feature_group_count=c)
    return y + b.astype(x.dtype)

def rg_lru(x, w_a, b_a, w_x, b_x, lam):
    bsz, t, _ = x.shape
    xb = x.reshape(bsz, t, LRU_BLOCKS, LRU_BLOCK)
    gate_r = jnp.einsum("btnc,ncd->btnd", xb, w_a).reshape(bsz, t, LRU_WIDTH) + b_a
    gate_i = jnp.einsum("btnc,ncd->btnd", xb, w_x).reshape(bsz, t, LRU_WIDTH) + b_x
    r = jax.nn.sigmoid(gate_r.astype(jnp.float32))
    i = jax.nn.sigmoid(gate_i.astype(jnp.float32))
    log_a = -LRU_C * r * jax.nn.softplus(-lam.astype(jnp.float32))
    a = jnp.exp(log_a)
    mult = jnp.sqrt(-jnp.expm1(2.0 * log_a))
    u = mult * (i * x.astype(jnp.float32))

    def combine(left, right):
        a_l, b_l = left
        a_r, b_r = right
        return a_l * a_r, a_r * b_l + b_r

    _, h = lax.associative_scan(combine, (a, u), axis=1)
    return h

def sliding_window_attention_with_sinks(q, k, v, sinks):
    bsz, t, _, _ = q.shape
    pad_cfg = ((0, 0), (PAD, 0), (0, 0), (0, 0))
    qp, kp, vp = jnp.pad(q, pad_cfg), jnp.pad(k, pad_cfg), jnp.pad(v, pad_cfg)
    tp = t + PAD
    nb = tp // BLOCK
    qb = qp.reshape(bsz, nb, BLOCK, KV_HEADS, GQA_GROUP, HEAD_DIM)
    kb = kp.reshape(bsz, nb, BLOCK, KV_HEADS, HEAD_DIM)
    vb = vp.reshape(bsz, nb, BLOCK, KV_HEADS, HEAD_DIM)
    blk_pad = ((0, 0), (1, 0), (0, 0), (0, 0), (0, 0))
    kk = jnp.concatenate([jnp.pad(kb, blk_pad)[:, :-1], kb], axis=2)
    vv = jnp.concatenate([jnp.pad(vb, blk_pad)[:, :-1], vb], axis=2)
    scale = HEAD_DIM ** -0.5
    s = jnp.einsum("bnqkgd,bnskd->bnkgqs", qb, kk,
                   preferred_element_type=jnp.float32) * scale
    blk = jnp.arange(nb)[:, None] * BLOCK
    qpos = blk + jnp.arange(BLOCK)[None, :]
    kpos = blk - BLOCK + jnp.arange(2 * BLOCK)[None, :]
    diff = qpos[:, :, None] - kpos[:, None, :]
    valid = (diff >= 0) & (diff < WINDOW) & (kpos[:, None, :] >= PAD)
    s = jnp.where(valid[None, :, None, None], s, NEG)
    sink = sinks.astype(jnp.float32).reshape(1, 1, KV_HEADS, GQA_GROUP, 1, 1)
    m = jnp.maximum(jnp.max(s, axis=-1, keepdims=True), sink)
    p = jnp.exp(s - m)
    denom = jnp.sum(p, axis=-1, keepdims=True) + jnp.exp(sink - m)
    o = jnp.einsum("bnkgqs,bnskd->bnqkgd", (p / denom).astype(v.dtype), vv)
    return o.reshape(bsz, tp, ATTN_WIDTH)[:, PAD:]

def second_inputs(seed: int = 0) -> dict:
    key = jax.random.key(seed)
    ks = jax.random.split(key, 20)
    f32 = jnp.float32

    def nrm(k, shape, scale):
        return jax.random.normal(k, shape, f32) * scale

    u = jax.random.uniform(ks[10], (DEPTH, LRU_WIDTH), f32, 0.9, 0.999)
    a0 = u ** (1.0 / LRU_C)
    lru_lambda = jnp.log(a0) - jnp.log1p(-a0)
    return {
        "x": nrm(ks[0], (BATCH, SEQ, D_MODEL), 1.0),
        "meta_tokens": nrm(ks[1], (N_META, D_MODEL), 1.0),
        "g_pre_mix": 1.0 + nrm(ks[2], (DEPTH, D_MODEL), 0.05),
        "w_in": nrm(ks[3], (DEPTH, D_MODEL, IN_WIDTH), D_MODEL ** -0.5),
        "conv_w": nrm(ks[4], (DEPTH, CONV_WIDTH, LRU_WIDTH), CONV_WIDTH ** -0.5),
        "conv_b": nrm(ks[5], (DEPTH, LRU_WIDTH), 0.01),
        "w_a": nrm(ks[6], (DEPTH, LRU_BLOCKS, LRU_BLOCK, LRU_BLOCK), LRU_BLOCK ** -0.5),
        "b_a": nrm(ks[7], (DEPTH, LRU_WIDTH), 0.01),
        "w_x": nrm(ks[8], (DEPTH, LRU_BLOCKS, LRU_BLOCK, LRU_BLOCK), LRU_BLOCK ** -0.5),
        "b_x": nrm(ks[9], (DEPTH, LRU_WIDTH), 0.01),
        "lru_lambda": lru_lambda,
        "attn_sinks": nrm(ks[11], (DEPTH, ATTN_HEADS), 0.5),
        "w_out": nrm(ks[12], (DEPTH, MIX_WIDTH_2, D_MODEL), MIX_WIDTH_2 ** -0.5),
        "g_post_mix": 1.0 + nrm(ks[13], (DEPTH, D_MODEL), 0.05),
        "g_pre_ffn": 1.0 + nrm(ks[14], (DEPTH, D_MODEL), 0.05),
        "w_ff1": nrm(ks[15], (DEPTH, D_MODEL, D_FF), D_MODEL ** -0.5),
        "w_ff2": nrm(ks[16], (DEPTH, D_FF, D_MODEL), D_FF ** -0.5),
        "g_post_ffn": 1.0 + nrm(ks[17], (DEPTH, D_MODEL), 0.05),
    }

def second_block(x, meta_tokens, g_pre_mix, w_in, conv_w, conv_b, w_a, b_a, w_x, b_x,
              lru_lambda, attn_sinks, w_out, g_post_mix, g_pre_ffn, w_ff1, w_ff2,
              g_post_ffn):
    bsz = x.shape[0]
    meta = jnp.broadcast_to(meta_tokens[None].astype(x.dtype), (bsz, N_META, D_MODEL))
    h = jnp.concatenate([meta, x], axis=1)
    t = h.shape[1]
    split_at = [ATTN_WIDTH, ATTN_WIDTH + KV_WIDTH, ATTN_WIDTH + 2 * KV_WIDTH,
                ATTN_WIDTH + 2 * KV_WIDTH + LRU_WIDTH]
    for l in range(DEPTH):
        u = rmsnorm_2(h, g_pre_mix[l])
        z = u @ w_in[l]
        q, k, v, xr, yr = jnp.split(z, split_at, axis=-1)
        attn = sliding_window_attention_with_sinks(
            q.reshape(bsz, t, ATTN_HEADS, HEAD_DIM),
            k.reshape(bsz, t, KV_HEADS, HEAD_DIM),
            v.reshape(bsz, t, KV_HEADS, HEAD_DIM),
            attn_sinks[l])
        xr = causal_depthwise_conv(xr, conv_w[l], conv_b[l])
        hr = rg_lru(xr, w_a[l], b_a[l], w_x[l], b_x[l], lru_lambda[l])
        rec = (jax.nn.gelu(yr.astype(jnp.float32)) * hr).astype(h.dtype)
        mix = jnp.concatenate([attn.astype(h.dtype), rec], axis=-1) @ w_out[l]
        h = h + rmsnorm_2(mix, g_post_mix[l])
        u = rmsnorm_2(h, g_pre_ffn[l])
        f = jnp.square(jax.nn.relu(u @ w_ff1[l])) @ w_ff2[l]
        h = h + rmsnorm_2(f, g_post_ffn[l])
    return h[:, N_META:]


def setup_inputs(seed=0):
    out = dict(first_inputs(seed))
    for name, value in second_inputs(seed + 1).items():
        if name != "x":
            out[name + "_2"] = value
    return out


def reference(
    x, meta_tokens, norm1_g, w_in, w_gate_up, b_gate_up, sb_norm_g, gla_norm_g, w_out, norm2_g,
    w_peer_q, sub_keys1, sub_keys2, expert_u, expert_v, norm_f_g, meta_tokens_2, g_pre_mix_2,
    w_in_2, conv_w_2, conv_b_2, w_a_2, b_a_2, w_x_2, b_x_2, lru_lambda_2, attn_sinks_2, w_out_2,
    g_post_mix_2, g_pre_ffn_2, w_ff1_2, w_ff2_2, g_post_ffn_2,
):
    x = first_block(
        x, meta_tokens, norm1_g, w_in, w_gate_up, b_gate_up, sb_norm_g, gla_norm_g, w_out,
        norm2_g, w_peer_q, sub_keys1, sub_keys2, expert_u, expert_v, norm_f_g,
    )
    return second_block(
        x, meta_tokens_2, g_pre_mix_2, w_in_2, conv_w_2, conv_b_2, w_a_2, b_a_2, w_x_2, b_x_2,
        lru_lambda_2, attn_sinks_2, w_out_2, g_post_mix_2, g_pre_ffn_2, w_ff1_2, w_ff2_2,
        g_post_ffn_2,
    )


_drawn_inputs = setup_inputs


def setup_inputs(seed=0):
    import zlib

    import numpy as np

    out = dict(_drawn_inputs(seed))
    spreads = {}
    factors = {'gla_norm_g': 3.316,
     'b_a_2': 39.052,
     'b_x_2': 25.289,
     'attn_sinks_2': 8.0,
     'sb_norm_g': 3.371,
     'norm2_g': 2.87}
    for name, (base, spread) in spreads.items():
        noise = np.random.default_rng([zlib.crc32(name.encode()), seed]).standard_normal(out[name].shape)
        drawn = base * np.exp(spread * noise) if base else spread * noise
        out[name] = __import__('jax').numpy.asarray(drawn.astype(out[name].dtype))
    for name, factor in factors.items():
        out[name] = (out[name] * factor).astype(out[name].dtype)
    return out
```

```python
from contextlib import ExitStack

import concourse.bass as bass
from concourse import mybir

ALU = mybir.AluOpType
ACT = mybir.ActivationFunctionType
F32 = mybir.dt.float32
U32 = mybir.dt.uint32
AX = mybir.AxisListType.X

P = 128
D = 1024
KD = D // P
SEQ = 256
META = 16
TOK = META + SEQ
EPS = 1e-6
ROWS = [P, P, META]
COL0 = [META, META + P, 0]
REAL = 2

SB_HEADS, SB_DIM = 8, 64
GLA_HEADS, DK, DV, RANK, TAU = 4, 64, 128, 16, 16.0
SUB = 32
NSUB = P // SUB

HEADS, NKEYS, TOPK = 8, 128, 16
RING = 8
UNITS = REAL * HEADS
PASSES = UNITS // 2
RMS_N1, RMS_N2, RMS_NF, RMS_N3, RMS_PM, RMS_N4, RMS_PF = 0, 3, 5, 7, 10, 12, 14
ROUTE_STEPS = 19
V_PRIME = 16

ATT, KVH = 8, 2
CHUNKS_LRU = 4
CONV = 4
LRU_C = 8.0
NEG = -1e30
FF_GROUP = 4
FF_GROUPS = 4 * D // (FF_GROUP * P)
FF_PAIRS = FF_GROUPS // 2

W_COLS = 512
C_NORM1, C_PREMIX, C_PREFFN, C_BG, C_CONVW, C_CONVB, C_BA, C_BX, C_LAM, C_END = (
    0, 8, 16, 24, 26, 42, 46, 50, 54, 58)
R_SB, R_GLA, R_NORM2, R_NORMF, R_POSTMIX, R_POSTFFN, R_SINK, R_END = (
    0, 512, 1024, 2048, 3072, 4096, 5120, 5128)


def proj_plan():
    jobs = []
    for c in range(2):
        jobs.append((("gq", c), "T", 3, c * P, META, SEQ))
    for c in range(2):
        jobs.append((("gk", c), "T", 3, 256 + c * P, 0, TOK))
    jobs.append((("glr", 0), "T", 6, 0, 0, TOK))
    for t in range(3):
        jobs.append((("gv", t), "N", 4, 0, COL0[t], ROWS[t]))
    for t in range(3):
        jobs.append((("sbv", t), "N", 2, 0, COL0[t], ROWS[t]))
    for c in range(4):
        jobs.append((("sbq", c), "T", 0, c * P, META, SEQ))
    for c in range(4):
        jobs.append((("sbk", c), "T", 1, c * P, 0, TOK))
    for t in range(2):
        jobs.append((("gr", t), "N", 5, 0, COL0[t], ROWS[t]))
    return jobs


def proj2_plan():
    jobs = []
    for c in range(4):
        jobs.append((("xr", c), "T", 768 + c * P, 0, TOK))
    for c in range(4):
        jobs.append((("yr", c), "T", 1280 + c * P, META, SEQ))
    for c in range(4):
        jobs.append((("q", c), "T", c * P, META, SEQ))
    jobs.append((("k", 0), "T", 512, 0, TOK))
    for t in range(3):
        jobs.append((("v", t), "N", 640, COL0[t], ROWS[t]))
    return jobs


def evac_plan(jobs, engine_of):
    done = {"v": 0, "a": 0}
    out = {}
    for n, job in enumerate(jobs):
        e = engine_of(job[0])
        done[e] += 1
        out[job[0]] = (n, e, done[e])
    return out


def two_blocks_kernel(nc, x, meta1, meta2, cols, rows, w_in, w_gate, w_out, w_peer_q, keys, expert_u,
                      expert_v, w_in2, w_a, w_x, w_out2, w_ff1, w_ff2, out):
    PJ, PJ2 = proj_plan(), proj2_plan()
    EV = evac_plan(PJ, lambda n: "a" if n[0] in ("gv", "sbq", "sbk", "gr") else "v")
    EV2 = evac_plan(PJ2, lambda n: "a" if n[0] in ("yr", "q") else "v")

    with ExitStack() as ctx:
        sems = {}

        def S(name):
            if name not in sems:
                sems[name] = ctx.enter_context(nc.semaphore(name))
            return sems[name]

        def sb(name, shape, dt=F32):
            return ctx.enter_context(nc.sbuf_tensor(name, shape, dt))

        bank = [ctx.enter_context(nc.psum_tensor(f"bank{i}", [P, 512], F32)) for i in range(4)]
        pairs = [ctx.enter_context(nc.psum_tensor(f"pair{i}", [P, 1024], F32)) for i in range(2)]

        def ps(i):
            return bank[i][:, :] if i < 4 else pairs[(i - 4) // 2][:, (i % 2) * 512:(i % 2) * 512 + 512]

        wblk = sb("wblk", [P, 6, KD * W_COLS])
        wlast = sb("wlast", [P, KD, RANK])
        row = sb("row", [P, R_END])
        col = sb("col", [P, C_END])
        ident = sb("ident", [P, P])
        ntri = sb("ntri", [P, P])
        neg1 = sb("neg1", [P, P])
        causal = sb("causal", [P, P])
        h = sb("h", [P, REAL, D])
        stat = sb("stat", [P, 64])
        epsc = sb("epsc", [P, 1])
        wgate = sb("wgate", [RANK, 2 * P])
        small = sb("small", [P, 256])
        small2 = sb("small2", [P, 256])
        area = sb("area", [P, 76 * 256])

        def at(kb, shape, dt=F32):
            n = 1
            for s in shape:
                n *= s
            a = area[:, int(kb * 256):int(kb * 256) + n]
            if dt is not F32:
                a = a.bitcast(dt)
            if len(shape) == 1:
                return a
            names = "abcd"[:len(shape)]
            return a.rearrange(f"p ({' '.join(names)}) -> p {' '.join(names)}",
                               **{k: s for k, s in zip(names[1:], shape[1:])})

        def blk(i, shape):
            names = "abcd"[:len(shape)]
            return wblk[:, i, :].rearrange(f"p ({' '.join(names)}) -> p {' '.join(names)}",
                                           **{k: s for k, s in zip(names[1:], shape[1:])})

        hM = at(0, [D])
        hnT = at(4, [KD, TOK])
        sbqT = at(12.5, [4, SEQ])
        sbkT = at(16.5, [4, TOK])
        gqT = at(20.75, [2, SEQ])
        gkT = at(22.75, [2, TOK])
        glrT = at(24.875, [TOK])
        nat = at(26, [3, D])
        sbv = at(26, [3, 512])
        gv = at(32, [3, 512])
        gr = at(38, [2, 512])
        sp = at(42, [2, 640])
        aT = at(47, [2, 640])
        tmp = at(52, [2, 640])
        nb = at(57, [2, TOK])
        pb = at(59.125, [2, TOK])
        lgt = at(61.25, [2, TOK])
        gex = at(63.5, [2, 1216])
        state = at(73, [2, DV])
        klnat = at(74, [2, P])
        attT = at(75, [2, P])
        kzpad = at(4, [2, NSUB, P])
        mixn = at(52, [REAL, D])
        sqr = at(60, [512])
        mixT = at(12.5, [KD, SEQ])
        hn2 = at(26, [REAL, D])
        hn2f = at(26, [REAL * D])
        hf = h[:, :, :].rearrange("p a b -> p (a b)")
        hn2T = at(34, [KD, SEQ])
        qpT = at(0, [HEADS, SEQ])
        score = at(8, [UNITS + 1, 2 * NKEYS])
        scoref = at(8, [(UNITS + 1) * 2 * NKEYS])
        keyT = at(42, [HEADS, NKEYS])
        diag = at(34, [TOPK, P])
        cur = at(46, [2, 256])
        cur2 = at(48, [256])
        cand = at(49, [256])
        pick = at(50, [512])
        wtail = at(52, [KD, 768])

        v16 = small[:, 0:32]
        i16 = small[:, 32:64].bitcast(U32)
        if16 = small[:, 64:96]
        sc16 = small[:, 96:112]
        pos = small[:, 112:128].bitcast(U32)
        posij = small[:, 128:160].bitcast(U32)
        posf = small[:, 160:192]
        eij = small[:, 192:224]
        nmx = small[:, 224:225]
        den = small[:, 225:226]
        rden = small[:, 226:227]
        eidx = small2[:, 0:32].bitcast(U32).rearrange("p (a b) -> p a b", a=2)
        dots = small2[:, 32:64].rearrange("p (a b) -> p a b", a=2)
        gate = small2[:, 64:96].rearrange("p (a b) -> p a b", a=2)
        ggel = small2[:, 96:128].rearrange("p (a b) -> p a b", a=2)
        gw = small2[:, 128:160].rearrange("p (a b) -> p a b", a=2)
        ex16 = small2[:, 160:176]
        iota16 = small2[:, 176:192]
        uring = [blk(2 + s // 4, [4, D])[:, s % 4, :] for s in range(RING)]
        vring = [blk(4 + s // 4, [4, D])[:, s % 4, :] for s in range(RING)]

        hM2 = at(0, [D])
        nat2 = at(8, [3, D])
        uT = at(28.5, [KD, TOK])
        q2T = at(37, [4, SEQ])
        k2T = at(41, [TOK])
        v2 = at(42.25, [3, KVH, P])
        xr = at(4, [4, TOK + 3])
        xc = at(20, [4, TOK])
        geluy = at(46, [4, SEQ])
        lr = at(8.5, [4, TOK])
        li = at(12.75, [4, TOK])
        lt = at(68, [4, TOK])
        uF = at(28.5, [KD, SEQ])
        lm = at(24.25, [4, TOK])
        wbd = row[:, 0:1024].rearrange("p (g c n) -> p g c n", g=2, c=4)
        mask2 = row[:, 1024:1536].rearrange("p (t n) -> p t n", t=2)
        mixT2 = at(52, [KD, SEQ])
        S2 = at(60, [4, SEQ])
        pT = at(64, [4, 2, P])
        f1T = at(37, [2, FF_GROUP, SEQ])

        def w_slice(i, c0, n):
            return blk(i, [KD, W_COLS])[:, :, c0:c0 + n]

        def w2_slice(c0):
            if c0 < 1024:
                return blk(c0 // 512, [KD, W_COLS])[:, :, c0 % 512:c0 % 512 + P]
            return wtail[:, :, c0 - 1024:c0 - 1024 + P]

        FF_AT = [4, 0]

        block = ctx.enter_context(nc.Block())

        @block.sync
        def _(sp_q):
            def block_of(src, c0):
                return src.rearrange("(k p) n -> p k n", p=P)[:, :, c0:c0 + W_COLS]

            sp_q.dma_start(h[:, 0, :], x[0:P, :]).then_inc(S("h_loaded0"), 16)
            sp_q.dma_start(h[:, 1, :], x[P:SEQ, :]).then_inc(S("h_loaded1"), 16)
            sp_q.dma_start(hM[0:META, :], meta1).then_inc(S("h_loaded2"), 16)
            sp_q.dma_start(col[:, :], cols).then_inc(S("col_loaded"), 16)
            for i in (3, 4, 2, 0, 1, 5):
                sp_q.dma_start(blk(i, [KD, W_COLS]), block_of(w_in, i * W_COLS)).then_inc(S(f"w_in_loaded{i}"), 16)
                if i == 3:
                    sp_q.dma_start(wlast[:, :, :], w_in.rearrange("(k p) n -> p k n", p=P)[:, :, 6 * W_COLS:])\
                        .then_inc(S("w_in_loaded6"), 16)
            sp_q.wait_ge(S("proj_made"), len(PJ))
            for i in range(2):
                sp_q.dma_start(blk(2 + i, [KD, W_COLS]), block_of(w_out, i * W_COLS)).then_inc(S("w_out_loaded"), 16)
            for i in range(2):
                sp_q.dma_start(blk(i, [KD, W_COLS]), block_of(w_peer_q, i * W_COLS)).then_inc(S("w_pq_loaded"), 16)
            sp_q.wait_ge(S("mix_turned"), 4)
            sp_q.dma_start(keyT[:, :, :], keys).then_inc(S("keys_loaded"), 16)
            sp_q.wait_ge(S("pq_made"), HEADS)
            for i in range(2):
                sp_q.dma_start(blk(i, [KD, W_COLS]), block_of(w_in2, i * W_COLS)).then_inc(S("w_in2_loaded"), 16)
            sp_q.dma_start(wtail[:, :, :], w_in2.rearrange("(k p) n -> p k n", p=P)[:, :, 1024:1792])\
                .then_inc(S("w_in2_loaded"), 16)
            sp_q.wait_ge(S("u_used"), RING + UNITS * TOPK)
            for i in range(2):
                sp_q.dma_start(blk(2 + i, [KD, W_COLS]), block_of(w_out2, i * W_COLS)).then_inc(S("w_out2_loaded"), 16)
            sp_q.dma_start(hM2[0:META, :], meta2).then_inc(S("h2_loaded"), 16)
            w1v = w_ff1.rearrange("(k p) n -> p k n", p=P)
            w2v = w_ff2.rearrange("(g c p) n -> p g c n", p=P, c=FF_GROUP)

            def load_ff1(g, s):
                sp_q.dma_start(blk(FF_AT[s], [KD, W_COLS]), w1v[:, :, bass.ds(g * W_COLS, W_COLS)])\
                    .then_inc(S(f"w_ff1_loaded{s}"), 16)

            def load_ff2(g, s):
                sp_q.dma_start(blk(FF_AT[s] + 1, [FF_GROUP, D]), w2v[:, bass.ds(g, 1), :, :].rearrange("p g c n -> p (g c) n"))\
                    .then_inc(S(f"w_ff2_loaded{s}"), 16)

            sp_q.wait_ge(S("v_used"), V_PRIME + UNITS * TOPK)
            load_ff1(0, 0)
            load_ff2(0, 0)
            sp_q.wait_ge(S("proj2_made"), len(PJ2))
            load_ff1(1, 1)
            load_ff2(1, 1)
            with sp_q.Fori(1, FF_PAIRS) as i:
                for s in range(2):
                    sp_q.wait_ge(S("f1_made"), (i * 2 + s - 1) * FF_GROUP)
                    load_ff1(i * 2 + s, s)
                for s in range(2):
                    sp_q.wait_ge(S("f2_group"), i * 2 + s - 1)
                    load_ff2(i * 2 + s, s)
            for t in range(REAL):
                sp_q.wait_ge(S("out_ready"), t + 1)
                sp_q.dma_start(out[t * P:(t + 1) * P, :], h[:, t, :]).then_inc(S("out_stored"), 16)
            sp_q.wait_ge(S("out_stored"), 16 * REAL)

        @block.gpsimd
        def _(pool):
            nc.gpsimd.memset(ident[:, :], 0.0).then_inc(S("masks_cleared"), 1)
            nc.gpsimd.memset(ntri[:, :], -1.0).then_inc(S("masks_cleared"), 1)
            nc.gpsimd.memset(neg1[:, :], -1.0).then_inc(S("masks_ready"), 1)
            nc.gpsimd.memset(causal[:, :], 1.0).then_inc(S("masks_cleared"), 1)
            pool.wait_ge(S("masks_cleared"), 3)
            nc.gpsimd.affine_select(out=ident[:, :], in_=ident[:, :], compare_op=ALU.not_equal, fill=1.0, base=0,
                                    pattern=[[-1, P]], channel_multiplier=1).then_inc(S("masks_ready"), 1)
            nc.gpsimd.affine_select(out=ntri[:, :], in_=ntri[:, :], compare_op=ALU.is_ge, fill=0.0, base=0,
                                    pattern=[[-1, P]], channel_multiplier=1).then_inc(S("masks_ready"), 1)
            nc.gpsimd.affine_select(out=causal[:, :], in_=causal[:, :], compare_op=ALU.is_ge, fill=0.0, base=0,
                                    pattern=[[1, P]], channel_multiplier=-1).then_inc(S("masks_ready"), 1)
            nc.gpsimd.iota(iota16, pattern=[[1, TOPK]], base=0, channel_multiplier=0,
                           allow_small_or_imprecise_dtypes=True).then_inc(S("iota_ready"), 1)
            pool.wait_ge(S("proj_made"), len(PJ))
            nc.gpsimd.memset(kzpad[:, :, :, :], 0.0).then_inc(S("kz_cleared"), 1)

            def keep_past(view):
                return nc.gpsimd.affine_select(out=view, in_=view, compare_op=ALU.is_gt, fill=0.0, base=0,
                                               pattern=[[1, P]], channel_multiplier=-1)

            for i in range(SB_HEADS + 1):
                if i < SB_HEADS:
                    pool.wait_ge(S("sp_made"), i + 1)
                    keep_past(sp[:, i % 2, 0:P])
                    keep_past(sp[:, i % 2, 512:640]).then_inc(S("sp_masked"), 1)
                if i >= 1:
                    pool.wait_ge(S("aT_made"), i)
                    keep_past(aT[:, (i - 1) % 2, 0:P])
                    keep_past(aT[:, (i - 1) % 2, 512:640]).then_inc(S("aT_masked"), 1)

            pool.wait_ge(S("mix_made"), REAL)
            with pool.Fori(0, PASSES) as b:
                for p in range(2):
                    pool.wait_ge(S("idx_ready"), b * 2 + p + 1)
                    for k in range(TOPK):
                        s, g = k % RING, (b * 2 + p) * TOPK + k
                        pool.wait_ge(S("u_used"), g + 1)
                        pool.sem_inc(S("gather_turn"), 1)
                        nc.gpsimd.indirect_dma_start(
                            out=uring[s], out_offset=None, in_=expert_u,
                            in_offset=bass.IndirectOffsetOnAxis(ap=eidx[:, p, k:k + 1], axis=0),
                        ).then_inc(S(f"u_row{s}"), 16)
                    for k in range(TOPK):
                        s, g = k % RING, (b * 2 + p) * TOPK + k
                        pool.wait_ge(S("v_used"), g + 1 + V_PRIME - RING)
                        pool.sem_inc(S("gather_turn"), 1)
                        nc.gpsimd.indirect_dma_start(
                            out=vring[s], out_offset=None, in_=expert_v,
                            in_offset=bass.IndirectOffsetOnAxis(ap=eidx[:, p, k:k + 1], axis=0),
                        ).then_inc(S(f"v_row{s}"), 16)


            pool.wait_ge(S("hn2_ready"), REAL)
            nc.gpsimd.memset(mask2, 0.0).then_inc(S("mask2_cleared"), 1)
            nc.gpsimd.memset(wbd, 0.0).then_inc(S("wbd_cleared"), 1)
            pool.wait_ge(S("mask2_cleared"), 1)
            nc.gpsimd.affine_select(out=mask2[:, 0, 0:META], in_=mask2[:, 0, 0:META], compare_op=ALU.is_gt, fill=NEG,
                                    base=P - META, pattern=[[1, META]], channel_multiplier=-1).then_inc(S("mask2_ready"), 1)
            nc.gpsimd.affine_select(out=mask2[:, 0, META:META + P], in_=mask2[:, 0, META:META + P], compare_op=ALU.is_ge,
                                    fill=NEG, base=0, pattern=[[-1, P]], channel_multiplier=1).then_inc(S("mask2_ready"), 1)
            nc.gpsimd.affine_select(out=mask2[:, 1, 0:P], in_=mask2[:, 1, 0:P], compare_op=ALU.is_gt, fill=NEG,
                                    base=0, pattern=[[1, P]], channel_multiplier=-1).then_inc(S("mask2_ready"), 1)
            nc.gpsimd.affine_select(out=mask2[:, 1, P:SEQ], in_=mask2[:, 1, P:SEQ], compare_op=ALU.is_ge, fill=NEG,
                                    base=0, pattern=[[-1, P]], channel_multiplier=1).then_inc(S("mask2_ready"), 1)
            pool.wait_ge(S("wbd_cleared"), 1)
            for g, w in enumerate((w_a, w_x)):
                for half in range(2):
                    src = w.rearrange("(c a) i o -> a i c o", a=2)[half]
                    pool.dma_start(wbd[64 * half:64 * half + 64, g, :, 64 * half:64 * half + 64], src)\
                        .then_inc(S("wbd_loaded"), 16)
        @block.scalar
        def _(act):
            linked = [0]

            def link(ins):
                linked[0] += 1
                ins.then_inc(S("scalar_step"), 1)
                act.wait_ge(S("scalar_step"), linked[0])

            act.dma_start(row[:, :], rows.partition_broadcast(P)).then_inc(S("row_loaded"), 16)
            act.dma_start(wgate[:, :], w_gate).then_inc(S("row_loaded"), 16)
            for t in range(3):
                n = ROWS[t]
                src = h[:, t, :] if t < 2 else hM[0:META, :]
                act.wait_ge(S(f"h_loaded{t}"), 16)
                link(nc.scalar.activation(nat[0:n, t, :], src, ACT.Square, accum_out=stat[0:n, t:t + 1]))
            act.wait_ge(S("eps_ready"), 1)
            for t in range(3):
                n = ROWS[t]
                nc.scalar.activation(stat[0:n, 3 + t:4 + t], stat[0:n, t:t + 1], ACT.Sqrt, scale=1.0 / D,
                                     bias=epsc[0:n, :]).then_inc(S("rms_ready"), 1)

            def evac(job):
                name = job[0]
                n, e, k = EV[name]
                if e != "a":
                    return
                b = ps(n % 8)
                act.wait_ge(S("proj_made"), n + 1)
                kind, i = name
                if kind == "gv":
                    r = ROWS[i]
                    ins = nc.scalar.activation(gv[0:r, i, :], b[0:r, :], ACT.Copy)
                elif kind == "gr":
                    ins = nc.scalar.activation(gr[:, i, :], b, ACT.Copy)
                elif kind == "sbq":
                    ins = nc.scalar.activation(sbqT[:, i, :], b[:, 0:SEQ], ACT.Copy, scale=SB_DIM ** -0.5)
                elif kind == "sbk":
                    ins = nc.scalar.activation(sbkT[:, i, :], b[:, 0:TOK], ACT.Copy)
                ins.then_inc(S("evac_a"), 1)

            for job in PJ:
                evac(job)
            act.wait_ge(S("lg_min"), 2)
            link(nc.scalar.activation(lgt[:, 0, :], ps(0)[:, 0:TOK], ACT.Abs, bias=col[:, C_BG:C_BG + 1]))
            link(nc.scalar.activation(lgt[:, 1, :], ps(1)[:, 0:TOK], ACT.Abs, bias=col[:, C_BG + 1:C_BG + 2]))
            link(nc.scalar.activation(lgt[:, :, :], lgt[:, :, :], ACT.Exp, scale=-1.0))
            nc.scalar.activation(lgt[:, :, :], lgt[:, :, :], ACT.Ln, bias=1.0).then_inc(S("lg_ln"), 1)

            def sb_soft(i):
                z = pairs[i % 2][:, 0:640]
                act.wait_ge(S("z_made"), i + 1)
                link(nc.scalar.activation(tmp[:, i % 2, :], z, ACT.Abs))
                link(nc.scalar.activation(tmp[:, i % 2, :], tmp[:, i % 2, :], ACT.Exp, scale=-1.0))
                nc.scalar.activation(tmp[:, i % 2, :], tmp[:, i % 2, :], ACT.Ln, bias=1.0).then_inc(S("z_ln"), 1)

            def sb_weights(i):
                act.wait_ge(S("s_made"), i + 1)
                if i >= 2:
                    act.wait_ge(S("pv_made"), i - 1)
                nc.scalar.activation(aT[:, i % 2, :], pairs[i % 2][:, 0:640], ACT.Exp).then_inc(S("aT_made"), 1)

            for i in range(SB_HEADS + 1):
                if i < SB_HEADS:
                    if i >= 2:
                        act.wait_ge(S("sp_made"), i - 1)
                    sb_soft(i)
                if i >= 1:
                    sb_weights(i - 1)

            act.wait_ge(S("decay_ready"), 2)

            def factors_M(c):
                nc.scalar.activation(gex[:, c, 1200:1216], pb[:, c, 0:META], ACT.Exp, scale=-1.0,
                                     bias=pb[:, c, META - 1:META])
                last = COL0[0] + P - 1
                nc.scalar.activation(stat[:, 42 + c:43 + c], pb[:, c, last:last + 1], ACT.Exp).then_inc(S("gex_made"), 1)

            def factors(t, c):
                u = t * 2 + c
                g = gex[:, u % 2, :]
                o = COL0[t]
                if u >= 2:
                    act.wait_ge(S("o_made"), 2 * u - 2)
                    act.wait_ge(S("klT_made"), u + 1)
                at_ = 0
                for j in range(NSUB):
                    n = P - SUB * j
                    e = o + SUB * j + SUB - 1
                    nc.scalar.activation(g[:, at_:at_ + n], pb[:, c, o + SUB * j:o + P], ACT.Exp,
                                         bias=nb[:, c, e:e + 1])
                    at_ += n
                for j in range(NSUB):
                    e = o + SUB * j + SUB - 1
                    nc.scalar.activation(g[:, 320 + SUB * j:352 + SUB * j], pb[:, c, o + SUB * j:o + SUB * j + SUB],
                                         ACT.Exp, scale=-1.0, bias=pb[:, c, e:e + 1])
                nc.scalar.activation(g[:, 448:576], pb[:, c, o:o + P], ACT.Exp)
                nc.scalar.activation(g[:, 576:704], pb[:, c, o:o + P], ACT.Exp, scale=-1.0,
                                     bias=pb[:, c, o + P - 1:o + P]).then_inc(S("gex_made"), 1)

            factors_M(0)
            factors_M(1)
            for t in range(REAL):
                for c in range(2):
                    factors(t, c)
            act.wait_ge(S("evac_a"), EV[("gr", 1)][2])
            for t in range(REAL):
                nc.scalar.activation(gr[:, t, :], gr[:, t, :], ACT.Silu).then_inc(S("silu_made"), 1)
            for t in range(REAL):
                act.wait_ge(S("ss_made"), 2 * t + 1)
                nc.scalar.activation(stat[:, 16:24], stat[:, 8:16], ACT.Sqrt, scale=1.0 / SB_DIM,
                                     bias=epsc[:, :]).then_inc(S("hrms_made"), 1)
                act.wait_ge(S("ss_made"), 2 * t + 2)
                nc.scalar.activation(stat[:, 28:32], stat[:, 24:28], ACT.Sqrt, scale=1.0 / DV,
                                     bias=epsc[:, :]).then_inc(S("hrms_made"), 1)
            for j in range(4):
                if j % 2 == 1:
                    act.wait_ge(S("mix_turned"), j + 1)
                    nc.scalar.activation(mixT[:, 4:8, (j // 2) * P:(j // 2) * P + P],
                                         ps(4 + j).rearrange("p (a b) -> p a b", a=4), ACT.Copy).then_inc(S("mixT_a"), 1)
            for t in range(REAL):
                act.wait_ge(S("h_mixed"), t + 1)
                link(nc.scalar.activation(hn2[:, t, :], h[:, t, :], ACT.Square, accum_out=stat[:, 32 + t:33 + t]))
                nc.scalar.activation(stat[:, 34 + t:35 + t], stat[:, 32 + t:33 + t], ACT.Sqrt, scale=1.0 / D,
                                     bias=epsc[:, :]).then_inc(S("rms_ready"), 1)
            for c in range(HEADS):
                act.wait_ge(S("pq_made"), c + 1)
                nc.scalar.activation(qpT[:, c, :], ps(c % 4)[:, 0:SEQ], ACT.Copy).then_inc(S("qpT_ready"), 1)
            for u in range(UNITS):
                act.wait_ge(S("score_made"), u + 1)
                nc.scalar.activation(score[:, u, :].rearrange("p (a b) -> p a b", a=2),
                                     pairs[u % 2][:, :].rearrange("p (a b) -> p a b", a=2)[:, :, 0:P], ACT.Copy).then_inc(S("score_ready"), 1)

            act.wait_ge(S("score_ready"), UNITS)
            act.wait_ge(S("score_end_set"), 1)
            nc.scalar.activation(cur[:, 0, :], score[:, 0, :], ACT.Copy).then_inc(S("cur_ready"), 1)
            act.wait_ge(S("sc_ready"), 1)
            nc.scalar.activation(ex16, sc16, ACT.Exp, bias=nmx, accum_out=den).then_inc(S("gex16_ready"), 1)
            with act.Fori(0, PASSES) as b:
                for p in range(2):
                    act.wait_ge(S("cur_used"), b * 2 + p + 1)
                    nc.scalar.activation(cur[:, 1 - p, :], scoref[:, bass.ds((b * 2 + p + 1) * 256, 256)], ACT.Copy)\
                        .then_inc(S("cur_ready"), 1)
                    act.wait_ge(S("u_used"), (b * 2 + p + 1) * TOPK + RING)
                    nc.scalar.activation(ggel[:, p, :], dots[:, p, :], ACT.Gelu).then_inc(S("gelu_ready"), 1)
                    act.wait_ge(S("gw_ready"), b * 2 + p + 1)
                    for k in range(TOPK):
                        act.wait_ge(S("v_used"), (b * 2 + p) * TOPK + k + 1)
                        nc.scalar.activation(diag[:, k, :], ident[:, :], ACT.Copy, scale=gw[:, p, k:k + 1])\
                            .then_inc(S("diag_ready"), 1)
                    act.wait_ge(S("sc_ready"), b * 2 + p + 2)
                    nc.scalar.activation(ex16, sc16, ACT.Exp, bias=nmx, accum_out=den).then_inc(S("gex16_ready"), 1)

            for t in range(REAL):
                act.wait_ge(S("y_added"), 2 + UNITS)
                link(nc.scalar.activation(nat2[:, t, :], h[:, t, :], ACT.Square, accum_out=stat[:, t:t + 1]))
                nc.scalar.activation(stat[:, 2 + t:3 + t], stat[:, t:t + 1], ACT.Sqrt, scale=1.0 / D,
                                     bias=epsc[:, :]).then_inc(S("rms_ready"), 1)
            for t in range(3):
                n = ROWS[t]
                if t < 2:
                    act.wait_ge(S("hf_ready"), t + 1)
                else:
                    act.wait_ge(S("h2_loaded"), 16)
                src = h[:, t, :] if t < 2 else hM2[0:META, :]
                link(nc.scalar.activation(nat2[0:n, t, :], src, ACT.Square, accum_out=stat[0:n, 4 + t:5 + t]))
                nc.scalar.activation(stat[0:n, 7 + t:8 + t], stat[0:n, 4 + t:5 + t], ACT.Sqrt, scale=1.0 / D,
                                     bias=epsc[0:n, :]).then_inc(S("rms_ready"), 1)
            for job in PJ2:
                n, e, k = EV2[job[0]]
                if e != "a":
                    continue
                kind, i = job[0]
                act.wait_ge(S("proj2_made"), n + 1)
                if kind == "yr":
                    nc.scalar.activation(geluy[:, i, :], ps(n % 8)[:, 0:SEQ], ACT.Gelu_apprx_tanh).then_inc(S("evac2_a"), 1)
                else:
                    nc.scalar.activation(q2T[:, i, :], ps(n % 8)[:, 0:SEQ], ACT.Copy, scale=64 ** -0.5)\
                        .then_inc(S("evac2_a"), 1)
            link(nc.scalar.activation(stat[:, 48:52], col[:, C_LAM:C_LAM + 4], ACT.Abs))
            link(nc.scalar.activation(stat[:, 48:52], stat[:, 48:52], ACT.Exp, scale=-1.0))
            nc.scalar.activation(stat[:, 48:52], stat[:, 48:52], ACT.Ln, bias=1.0).then_inc(S("lam_ln"), 1)
            for c in range(4):
                act.wait_ge(S("lru_made"), c + 1)
                b2 = pairs[c % 2]
                nc.scalar.activation(lr[:, c, :], b2[:, 0:TOK], ACT.Sigmoid, bias=col[:, C_BA + c:C_BA + c + 1])
                nc.scalar.activation(li[:, c, :], b2[:, 512:512 + TOK], ACT.Sigmoid, bias=col[:, C_BX + c:C_BX + c + 1])\
                    .then_inc(S("sig_made"), 1)
            act.wait_ge(S("sig_made"), 4)
            act.wait_ge(S("lam_ready"), 2)
            for c in range(4):
                nc.scalar.activation(lm[:, c, :], lr[:, c, :], ACT.Tanh, scale=stat[:, 52 + c:53 + c]).then_inc(S("tanh_made"), 1)
                nc.scalar.activation(lr[:, c, :], lr[:, c, :], ACT.Exp, scale=stat[:, 56 + c:57 + c]).then_inc(S("a_made"), 1)
            act.wait_ge(S("m2_made"), 1)
            nc.scalar.activation(lm[:, :, :], lm[:, :, :], ACT.Sqrt).then_inc(S("root_made"), 1)
            for u in range(4):
                act.wait_ge(S("nm_made"), u + 1)
                nk = META + P if u // 2 == 0 else SEQ
                for j in range(4):
                    nc.scalar.activation(S2[:, j, 0:nk], S2[:, j, 0:nk], ACT.Exp, bias=stat[:, 12 + j:13 + j],
                                         accum_out=stat[:, 16 + j:17 + j])
                nc.scalar.activation(stat[:, 20:24], stat[:, 20:24], ACT.Exp).then_inc(S("p_made"), 1)
            for t in range(REAL):
                act.wait_ge(S("mix2_made"), t + 1)
                link(nc.scalar.activation(nat2[:, t, :], pairs[t][:, :], ACT.Square, accum_out=stat[:, 24 + t:25 + t]))
                nc.scalar.activation(stat[:, 26 + t:27 + t], stat[:, 24 + t:25 + t], ACT.Sqrt, scale=1.0 / D,
                                     bias=epsc[:, :]).then_inc(S("rms_ready"), 1)
            for t in range(REAL):
                act.wait_ge(S("h_mixed2"), t + 1)
                link(nc.scalar.activation(nat2[:, t, :], h[:, t, :], ACT.Square, accum_out=stat[:, 28 + t:29 + t]))
                nc.scalar.activation(stat[:, 30 + t:31 + t], stat[:, 28 + t:29 + t], ACT.Sqrt, scale=1.0 / D,
                                     bias=epsc[:, :]).then_inc(S("rms_ready"), 1)

            def relu_pair(i):
                for s in range(2):
                    if not isinstance(i, int) or i > 0:
                        act.wait_ge(S("f2_group"), i * 2 + s - 1)
                    for c in range(FF_GROUP):
                        act.wait_ge(S("f1_made"), (i * 2 + s) * FF_GROUP + c + 1)
                        nc.scalar.activation(f1T[:, s, c, :], ps(c)[:, 0:SEQ], ACT.Relu).then_inc(S("relu_made"), 1)

            relu_pair(0)
            with act.Fori(1, FF_PAIRS) as i:
                relu_pair(i)
            for t in range(REAL):
                act.wait_ge(S("f2_group"), FF_GROUPS)
                link(nc.scalar.activation(nat2[:, t, :], pairs[t][:, :], ACT.Square, accum_out=stat[:, 32 + t:33 + t]))
                nc.scalar.activation(stat[:, 34 + t:35 + t], stat[:, 32 + t:33 + t], ACT.Sqrt, scale=1.0 / D,
                                     bias=epsc[:, :]).then_inc(S("rms_ready"), 1)

        @block.vector
        def _(dve):
            linked = [0]

            def link(ins):
                linked[0] += 1
                ins.then_inc(S("vector_step"), 1)
                dve.wait_ge(S("vector_step"), linked[0])

            nc.vector.memset(epsc[:, :], EPS).then_inc(S("eps_ready"), 1)
            for t in range(3):
                n = ROWS[t]
                src = h[:, t, :] if t < 2 else hM[0:META, :]
                dve.wait_ge(S("rms_ready"), RMS_N1 + t + 1)
                link(nc.vector.reciprocal(stat[0:n, 3 + t:4 + t], stat[0:n, 3 + t:4 + t]))
                nc.vector.tensor_scalar(nat[0:n, t, :], src, stat[0:n, 3 + t:4 + t], None, ALU.mult).then_inc(S("n1_ready"), 1)
            dve.wait_ge(S("col_loaded"), 16)

            def gained(turned, j, n, dst, gain):
                dve.wait_ge(S(turned), j + 1)
                return nc.vector.tensor_tensor(dst, ps(j)[:, :].rearrange("p (a b) -> p a b", a=4)[:, :, 0:n],
                                               gain.unsqueeze(2).to_broadcast([P, 4, n]), ALU.mult)

            for j in range(6):
                t, k0, n = j // 2, 4 * (j % 2), ROWS[j // 2]
                gained("n1_turned", j, n, hnT[:, k0:k0 + 4, COL0[t]:COL0[t] + n],
                       col[:, C_NORM1 + k0:C_NORM1 + k0 + 4]).then_inc(S("hnT_ready"), 1)
            for job in PJ:
                name = job[0]
                n, e, k = EV[name]
                if e != "v":
                    continue
                kind, i = name
                b = ps(n % 8)
                dve.wait_ge(S("proj_made"), n + 1)
                if kind == "gq":
                    ins = nc.vector.tensor_scalar(gqT[:, i, :], b[:, 0:SEQ], DK ** -0.5, None, ALU.mult)
                elif kind == "gk":
                    ins = nc.vector.tensor_copy(gkT[:, i, :], b[:, 0:TOK])
                elif kind == "glr":
                    ins = nc.vector.tensor_copy(glrT[0:RANK, :], b[0:RANK, 0:TOK])
                else:
                    r = ROWS[i]
                    ins = nc.vector.tensor_copy(sbv[0:r, i, :], b[0:r, :])
                ins.then_inc(S("evac_v"), 1)
            dve.wait_ge(S("lg_made"), 1)
            for c in range(2):
                nc.vector.tensor_scalar(nb[:, c, :], ps(c)[:, 0:TOK], col[:, C_BG + c:C_BG + c + 1], 0.0, ALU.add, ALU.min)\
                    .then_inc(S("lg_min"), 1)
            dve.wait_ge(S("lg_min"), 2)
            dve.wait_ge(S("lg_ln"), 1)
            link(nc.vector.tensor_tensor(lgt[:, :, :], lgt[:, :, :], nb[:, :, :], ALU.subtract))
            for c in range(2):
                for t in range(3):
                    seg = slice(COL0[t], COL0[t] + ROWS[t])
                    link(nc.vector.tensor_tensor_scan(nb[:, c, seg], lgt[:, c, seg], lgt[:, c, seg], 0.0, ALU.add, ALU.max))
            nc.vector.tensor_scalar(pb[:, :, :], nb[:, :, :], -1.0 / TAU, None, ALU.mult).then_inc(S("decay_ready"), 1)
            nc.vector.tensor_scalar(nb[:, :, :], nb[:, :, :], 1.0 / TAU, None, ALU.mult).then_inc(S("decay_ready"), 1)
            for i in range(SB_HEADS):
                dve.wait_ge(S("z_ln"), i + 1)
                if i >= 2:
                    dve.wait_ge(S("s_made"), i - 1)
                nc.vector.scalar_tensor_tensor(out=sp[:, i % 2, :], in0=pairs[i % 2][:, 0:640], scalar=0.0,
                                               in1=tmp[:, i % 2, :], op0=ALU.max, op1=ALU.add).then_inc(S("sp_made"), 1)

            def state_from(c, n, upd):
                dve.wait_ge(S("klT_made"), upd + 1)
                nc.vector.tensor_copy(klnat[0:n, c, :], ps(6)[0:n, 0:P]).then_inc(S("klnat_ready"), 1)
                dve.wait_ge(S("st_prod"), upd + 1)
                if upd >= 2:
                    dve.wait_ge(S("o_made"), 2 * c + 2)
                for hp in range(2):
                    rows_ = slice(64 * hp, 64 * hp + 64)
                    new = ps(7)[rows_, hp * DV:(hp + 1) * DV]
                    if upd < 2:
                        ins = nc.vector.tensor_copy(state[rows_, c, :], new)
                    else:
                        ins = nc.vector.scalar_tensor_tensor(out=state[rows_, c, :], in0=state[rows_, c, :],
                                                             scalar=stat[rows_, 42 + c:43 + c], in1=new,
                                                             op0=ALU.mult, op1=ALU.add)
                ins.then_inc(S("state_ready"), 1)

            for c in range(2):
                dve.wait_ge(S("gex_made"), c + 1)
                nc.vector.tensor_tensor(gex[:, c, 1200:1216], gex[:, c, 1200:1216], gkT[:, c, 0:META], ALU.mult)\
                    .then_inc(S("klM_ready"), 1)
            for c in range(2):
                state_from(c, META, c)
            dve.wait_ge(S("kz_cleared"), 1)
            for u in range(4):
                t, c = divmod(u, 2)
                g = gex[:, u % 2, :]
                dve.wait_ge(S("gex_made"), 3 + u)
                a = 0
                for j in range(NSUB):
                    n = P - SUB * j
                    q0 = t * P + SUB * j
                    nc.vector.tensor_tensor(g[:, a:a + n], g[:, a:a + n], gqT[:, c, q0:q0 + n], ALU.mult)
                    a += n
                    k0 = COL0[t] + SUB * j
                    nc.vector.tensor_tensor(kzpad[:, u % 2, j, SUB * j:SUB * j + SUB], g[:, 320 + SUB * j:352 + SUB * j],
                                            gkT[:, c, k0:k0 + SUB], ALU.mult)
                nc.vector.tensor_tensor(g[:, 448:576], g[:, 448:576], gqT[:, c, t * P:t * P + P], ALU.mult)
                nc.vector.tensor_tensor(g[:, 576:704], g[:, 576:704], gkT[:, c, COL0[t]:COL0[t] + P], ALU.mult)\
                    .then_inc(S("gla_f"), 1)
                for hp in range(2):
                    v = 2 * u + hp
                    dve.wait_ge(S("att_made"), v + 1)
                    if v >= 2:
                        dve.wait_ge(S("o_made"), v - 1)
                    nc.vector.tensor_tensor(attT[:, v % 2, :], ps(4 + v % 2)[:, 0:P], causal[:, :], ALU.mult)\
                        .then_inc(S("attT_ready"), 1)
                if t == 0:
                    state_from(c, P, 2 + c)

            dve.wait_ge(S("row_loaded"), 32)
            dve.wait_ge(S("silu_made"), 2)
            dve.wait_ge(S("o_made"), 8)
            dve.wait_ge(S("pv_made"), SB_HEADS)
            for t in range(REAL):
                for part, (nh, dh, bnk, g0, s0) in enumerate(((SB_HEADS, SB_DIM, 2 + t, R_SB, 8), (GLA_HEADS, DV, t, R_GLA, 24))):
                    m = mixn[:, t, 512 * part:512 * part + 512]
                    mh = m.rearrange("p (a b) -> p a b", a=nh)
                    r0 = s0 + (8 if part == 0 else 4)
                    link(nc.vector.tensor_copy(m, ps(bnk)))
                    link(nc.vector.tensor_tensor(sqr, m, m, ALU.mult))
                    nc.vector.tensor_reduce(stat[:, s0:s0 + nh], sqr.rearrange("p (a b) -> p a b", a=nh), AX, ALU.add)\
                        .then_inc(S("ss_made"), 1)
                    dve.wait_ge(S("hrms_made"), 2 * t + part + 1)
                    link(nc.vector.reciprocal(stat[:, r0:r0 + nh], stat[:, r0:r0 + nh]))
                    link(nc.vector.tensor_tensor(mh, mh, stat[:, r0:r0 + nh].unsqueeze(2).to_broadcast([P, nh, dh]), ALU.mult))
                    if part == 0:
                        nc.vector.tensor_tensor(m, m, row[:, g0:g0 + 512], ALU.mult).then_inc(S("mixn_ready"), 1)
                    else:
                        link(nc.vector.tensor_tensor(m, m, row[:, g0:g0 + 512], ALU.mult))
                        nc.vector.tensor_tensor(m, m, gr[:, t, :], ALU.mult).then_inc(S("mixn_ready"), 1)
            for j in (0, 2):
                dve.wait_ge(S("mix_turned"), j + 1)
                nc.vector.tensor_copy(mixT[:, 0:4, (j // 2) * P:(j // 2) * P + P],
                                      ps(4 + j).rearrange("p (a b) -> p a b", a=4)).then_inc(S("mixT_v"), 1)
            for t in range(REAL):
                dve.wait_ge(S("mix_made"), t + 1)
                nc.vector.tensor_tensor(h[:, t, 0:512], h[:, t, 0:512], ps(2 * t), ALU.add)
                nc.vector.tensor_tensor(h[:, t, 512:D], h[:, t, 512:D], ps(2 * t + 1), ALU.add).then_inc(S("h_mixed"), 1)
            for t in range(REAL):
                dve.wait_ge(S("rms_ready"), RMS_N2 + t + 1)
                link(nc.vector.reciprocal(stat[:, 34 + t:35 + t], stat[:, 34 + t:35 + t]))
                nc.vector.scalar_tensor_tensor(out=hn2[:, t, :], in0=h[:, t, :], scalar=stat[:, 34 + t:35 + t],
                                               in1=row[:, R_NORM2:R_NORM2 + D], op0=ALU.mult, op1=ALU.mult)\
                    .then_inc(S("hn2_ready"), 1)
            for j in range(4):
                dve.wait_ge(S("n2_turned"), j + 1)
                nc.vector.tensor_copy(hn2T[:, 4 * (j % 2):4 * (j % 2) + 4, (j // 2) * P:(j // 2) * P + P],
                                      ps(4 + j).rearrange("p (a b) -> p a b", a=4)).then_inc(S("hn2T_ready"), 1)
            dve.wait_ge(S("n2_turned"), 4)
            nc.vector.memset(score[:, UNITS, :], 0.0).then_inc(S("score_end_set"), 1)

            dve.wait_ge(S("iota_ready"), 1)

            def route(u, p):
                step = [0]

                def done(ins):
                    step[0] += 1
                    ins.then_inc(S("route_step"), 1)
                    dve.wait_ge(S("route_step"), u * ROUTE_STEPS + step[0])

                def tick(ins):
                    step[0] += 1
                    ins.then_inc(S("route_step"), 1)

                dve.wait_ge(S("cur_ready"), u + 1)
                dve.sem_inc(S("route_turn"), 1)

                def rests():
                    dve.wait_ge(S("route_step"), u * ROUTE_STEPS + step[0])
                    dve.sem_inc(S("route_turn"), 1)

                def best16(vals, vi, idx, rest):
                    for x, v, i, r in zip(vals, vi, idx, rest):
                        tick(nc.vector.max(v[:, 0:8], x))
                    rests()
                    for x, v, i, r in zip(vals, vi, idx, rest):
                        nc.vector.max_index(i[:, 0:8], v[:, 0:8], x)
                        tick(nc.vector.match_replace(r, v[:, 0:8], x, -3.0e38))
                    rests()
                    for x, v, i, r in zip(vals, vi, idx, rest):
                        tick(nc.vector.max(v[:, 8:16], r))
                    rests()
                    for x, v, i, r in zip(vals, vi, idx, rest):
                        tick(nc.vector.max_index(i[:, 8:16], v[:, 8:16], r))
                    rests()

                side = [cur[:, p, 0:NKEYS], cur[:, p, NKEYS:2 * NKEYS]]
                best16(side, [v16[:, 0:16], v16[:, 16:32]], [i16[:, 0:16], i16[:, 16:32]],
                       [cur2[:, 0:NKEYS], cur2[:, NKEYS:2 * NKEYS]])
                ins = nc.vector.tensor_tensor(cand.rearrange("p (a b) -> p a b", a=TOPK),
                                              v16[:, 0:16].unsqueeze(2).to_broadcast([P, TOPK, TOPK]),
                                              v16[:, 16:32].unsqueeze(1).to_broadcast([P, TOPK, TOPK]), ALU.add)
                ins.then_inc(S("cur_used"), 1)
                dve.wait_ge(S("cur_used"), u + 1)
                dve.sem_inc(S("route_turn"), 1)
                best16([cand], [sc16], [pos], [pick[:, 0:256]])
                tick(nc.vector.tensor_scalar(nmx, sc16[:, 0:1], -1.0, None, ALU.mult))
                tick(nc.vector.tensor_scalar(posij[:, 0:16], pos, 4, None, ALU.logical_shift_right))
                tick(nc.vector.tensor_scalar(posij[:, 16:32], pos, 15, None, ALU.bitwise_and))
                nc.vector.tensor_copy(if16, i16).then_inc(S("sc_ready"), 1)
                dve.wait_ge(S("route_step"), u * ROUTE_STEPS + step[0])
                done(nc.vector.tensor_copy(posf, posij))
                pk = pick.rearrange("p (s k i) -> p s k i", s=2, k=TOPK)
                done(nc.vector.tensor_tensor(
                    pk, iota16.unsqueeze(1).unsqueeze(1).to_broadcast([P, 2, TOPK, TOPK]),
                    posf.rearrange("p (s k) -> p s k", s=2).unsqueeze(3).to_broadcast([P, 2, TOPK, TOPK]), ALU.is_equal))
                done(nc.vector.tensor_tensor(
                    pk, pk, if16.rearrange("p (s i) -> p s i", s=2).unsqueeze(2).to_broadcast([P, 2, TOPK, TOPK]), ALU.mult))
                done(nc.vector.tensor_reduce(eij.rearrange("p (s k) -> p s k", s=2), pk, AX, ALU.add))
                dve.wait_ge(S("v_used"), V_PRIME if isinstance(u, int) else u * TOPK)
                nc.vector.scalar_tensor_tensor(out=eidx[:, p, :], in0=eij[:, 0:16], scalar=float(NKEYS),
                                               in1=eij[:, 16:32], op0=ALU.mult, op1=ALU.add).then_inc(S("idx_ready"), 1)
                assert step[0] == ROUTE_STEPS, step[0]

            route(0, 0)
            with dve.Fori(0, REAL) as t:
                with dve.Fori(0, PASSES // REAL) as q:
                    b = t * (PASSES // REAL) + q
                    for p in range(2):
                        u = b * 2 + p
                        for k in range(TOPK):
                            s = k % RING
                            dve.wait_ge(S(f"u_row{s}"), (b * 4 + 2 * p + k // RING + 1) * 16)
                            ins = nc.vector.scalar_tensor_tensor(
                                out=uring[s], in0=uring[s], scalar=1.0, in1=hn2f[:, bass.ds(t * D, D)],
                                op0=ALU.mult, op1=ALU.mult, accum_out=dots[:, p, k:k + 1])
                            ins.then_inc(S("u_used"), 1)
                        dve.wait_ge(S("gex16_ready"), u + 1)
                        nc.vector.reciprocal(rden, den).then_inc(S("rden_ready"), 1)
                        dve.wait_ge(S("rden_ready"), u + 1)
                        dve.wait_ge(S("gelu_ready"), u + 1)
                        nc.vector.scalar_tensor_tensor(out=gw[:, p, :], in0=ex16, scalar=rden, in1=ggel[:, p, :],
                                                       op0=ALU.mult, op1=ALU.mult).then_inc(S("gw_ready"), 1)
                        route(u + 1, 1 - p)
                        dve.wait_ge(S("v_used"), u * TOPK + V_PRIME + TOPK)
                        nc.vector.tensor_tensor(hf[:, bass.ds(t * D, D)], hf[:, bass.ds(t * D, D)], pairs[p][:, :], ALU.add)\
                            .then_inc(S("y_added"), 1)
                        dve.wait_ge(S("y_added"), u + 3)

            link(nc.vector.memset(v2[:, :, :, :], 0.0))
            link(nc.vector.memset(xr[:, :, 0:CONV - 1], 0.0))
            for t in range(REAL):
                dve.wait_ge(S("rms_ready"), RMS_NF + t + 1)
                link(nc.vector.reciprocal(stat[:, 2 + t:3 + t], stat[:, 2 + t:3 + t]))
                nc.vector.scalar_tensor_tensor(out=h[:, t, :], in0=h[:, t, :], scalar=stat[:, 2 + t:3 + t],
                                               in1=row[:, R_NORMF:R_NORMF + D], op0=ALU.mult, op1=ALU.mult)\
                    .then_inc(S("hf_ready"), 1)
            for t in range(3):
                n = ROWS[t]
                dve.wait_ge(S("rms_ready"), RMS_N3 + t + 1)
                link(nc.vector.reciprocal(stat[0:n, 7 + t:8 + t], stat[0:n, 7 + t:8 + t]))
                src = h[:, t, :] if t < 2 else hM2[0:META, :]
                nc.vector.tensor_scalar(nat2[0:n, t, :], src, stat[0:n, 7 + t:8 + t], None, ALU.mult).then_inc(S("n3_ready"), 1)
            for j in range(6):
                t, k0, n = j // 2, 4 * (j % 2), ROWS[j // 2]
                gained("n3_turned", j, n, uT[:, k0:k0 + 4, COL0[t]:COL0[t] + n],
                       col[:, C_PREMIX + k0:C_PREMIX + k0 + 4]).then_inc(S("uT_ready"), 1)
            for job in PJ2:
                n, e, k = EV2[job[0]]
                if e != "v":
                    continue
                kind, i = job[0]
                dve.wait_ge(S("proj2_made"), n + 1)
                b = ps(n % 8)
                if kind == "xr":
                    ins = nc.vector.tensor_copy(xr[:, i, CONV - 1:], b[:, 0:TOK])
                elif kind == "k":
                    ins = nc.vector.tensor_copy(k2T, b[:, 0:TOK])
                else:
                    r = ROWS[i]
                    for kv in range(KVH):
                        ins = nc.vector.tensor_copy(v2[0:r, i, kv, 64 * kv:64 * kv + 64], b[0:r, 64 * kv:64 * kv + 64])
                ins.then_inc(S("evac2_v"), 1)
            dve.wait_ge(S("evac2_v"), 4)
            for c in range(4):
                w = col[:, C_CONVW + 4 * c:C_CONVW + 4 * c + 4]
                nc.vector.tensor_scalar(xc[:, c, :], xr[:, c, 3:3 + TOK], w[:, 3:4], col[:, C_CONVB + c:C_CONVB + c + 1],
                                        ALU.mult, ALU.add).then_inc(S("conv_step"), 1)
                for k in (2, 1, 0):
                    dve.wait_ge(S("conv_step"), 4 * c + 3 - k)
                    ins = nc.vector.scalar_tensor_tensor(out=xc[:, c, :], in0=xr[:, c, k:k + TOK], scalar=w[:, k:k + 1],
                                                         in1=xc[:, c, :], op0=ALU.mult, op1=ALU.add)
                    ins.then_inc(S("conv_step"), 1)
            link(nc.vector.tensor_scalar(stat[:, 60:64], col[:, C_LAM:C_LAM + 4], 0.0, None, ALU.min))
            dve.wait_ge(S("lam_ln"), 1)
            link(nc.vector.tensor_tensor(stat[:, 48:52], stat[:, 48:52], stat[:, 60:64], ALU.subtract))
            nc.vector.tensor_scalar(stat[:, 52:56], stat[:, 48:52], LRU_C, None, ALU.mult).then_inc(S("lam_ready"), 1)
            nc.vector.tensor_scalar(stat[:, 56:60], stat[:, 48:52], -LRU_C, None, ALU.mult).then_inc(S("lam_ready"), 1)
            dve.wait_ge(S("a_made"), 4)
            link(nc.vector.tensor_tensor(lt[:, :, :], lr[:, :, :], lr[:, :, :], ALU.mult))
            nc.vector.scalar_tensor_tensor(out=lm[:, :, :], in0=lt[:, :, :], scalar=1.0, in1=lm[:, :, :], op0=ALU.add, op1=ALU.mult)\
                .then_inc(S("m2_made"), 1)
            link(nc.vector.tensor_tensor(li[:, :, :], li[:, :, :], xc[:, :, :], ALU.mult))
            dve.wait_ge(S("root_made"), 1)
            link(nc.vector.tensor_tensor(li[:, :, :], li[:, :, :], lm[:, :, :], ALU.mult))
            for c in range(4):
                link(nc.vector.tensor_tensor_scan(lt[:, c, :], lr[:, c, :], li[:, c, :], 0.0, ALU.mult, ALU.add))
            dve.wait_ge(S("evac2_a"), 4)
            nc.vector.tensor_tensor(mixT2[:, 4:8, :], lt[:, :, META:TOK], geluy[:, :, :], ALU.mult).then_inc(S("rec_ready"), 1)
            dve.wait_ge(S("mask2_ready"), 4)
            for u in range(4):
                t, hf_ = divmod(u, 2)
                nk = META + P if t == 0 else SEQ
                dve.wait_ge(S("s2_made"), u + 1)
                if u >= 1:
                    dve.wait_ge(S("p_turned"), u)
                for half in range(2):
                    nc.vector.tensor_tensor(S2[:, half:4:2, 0:nk],
                                            ps(half).rearrange("p (a b) -> p a b", a=2)[:, :, 0:nk],
                                            mask2[:, t, 0:nk].unsqueeze(1).to_broadcast([P, 2, nk]), ALU.add)\
                        .then_inc(S("s2_masked"), 1)
                dve.wait_ge(S("s2_masked"), 2 * u + 2)
                nc.vector.tensor_reduce(stat[:, 8:12], S2[:, :, 0:nk], AX, ALU.max).then_inc(S("m_step"), 1)
                dve.wait_ge(S("m_step"), 5 * u + 1)
                sink = row[:, R_SINK + 4 * hf_:R_SINK + 4 * hf_ + 4]
                nc.vector.tensor_tensor(stat[:, 8:12], stat[:, 8:12], sink, ALU.max).then_inc(S("m_step"), 1)
                dve.wait_ge(S("m_step"), 5 * u + 2)
                nc.vector.tensor_tensor(stat[:, 20:24], sink, stat[:, 8:12], ALU.subtract)
                nc.vector.tensor_scalar(stat[:, 12:16], stat[:, 8:12], -1.0, None, ALU.mult).then_inc(S("nm_made"), 1)
                dve.wait_ge(S("p_made"), u + 1)
                nc.vector.tensor_tensor(stat[:, 16:20], stat[:, 16:20], stat[:, 20:24], ALU.add).then_inc(S("m_step"), 1)
                dve.wait_ge(S("m_step"), 5 * u + 3)
                nc.vector.reciprocal(stat[:, 16:20], stat[:, 16:20]).then_inc(S("m_step"), 1)
                dve.wait_ge(S("m_step"), 5 * u + 4)
                nc.vector.tensor_tensor(S2[:, :, 0:nk], S2[:, :, 0:nk],
                                        stat[:, 16:20].unsqueeze(2).to_broadcast([P, 4, nk]), ALU.mult)\
                    .then_inc(S("m_step"), 1)
                dve.wait_ge(S("p_turned"), u + 1)
                if u >= 1:
                    dve.wait_ge(S("o2_made"), u)
                for half in range(2):
                    src = ps(2 + half).rearrange("p (a k b) -> p a k b", a=2, k=2)
                    if t == 0:
                        nc.vector.tensor_copy(pT[0:META, 2 * half:2 * half + 2, 0, :], src[0:META, :, 0, :])
                        ins = nc.vector.tensor_copy(pT[:, 2 * half:2 * half + 2, 1, :], src[:, :, 1, :])
                    else:
                        ins = nc.vector.tensor_copy(pT[:, 2 * half:2 * half + 2, :, :], src)
                ins.then_inc(S("pT_ready"), 1)
                dve.wait_ge(S("o2_made"), u + 1)
                nc.vector.tensor_copy(mixT2[:, 2 * hf_:2 * hf_ + 2, t * P:t * P + P],
                                      ps(4).rearrange("p (a b) -> p a b", a=4)[:, 0:2, :]).then_inc(S("o2_ready"), 1)
            for t in range(REAL):
                dve.wait_ge(S("rms_ready"), RMS_PM + t + 1)
                link(nc.vector.reciprocal(stat[:, 26 + t:27 + t], stat[:, 26 + t:27 + t]))
                link(nc.vector.scalar_tensor_tensor(out=nat2[:, t, :], in0=pairs[t][:, :], scalar=stat[:, 26 + t:27 + t],
                                               in1=row[:, R_POSTMIX:R_POSTMIX + D], op0=ALU.mult, op1=ALU.mult))
                nc.vector.tensor_tensor(h[:, t, :], h[:, t, :], nat2[:, t, :], ALU.add).then_inc(S("h_mixed2"), 1)
            for t in range(REAL):
                dve.wait_ge(S("rms_ready"), RMS_N4 + t + 1)
                link(nc.vector.reciprocal(stat[:, 30 + t:31 + t], stat[:, 30 + t:31 + t]))
                nc.vector.tensor_scalar(nat2[:, t, :], h[:, t, :], stat[:, 30 + t:31 + t], None, ALU.mult).then_inc(S("n4_ready"), 1)
            for j in range(4):
                t, k0 = j // 2, 4 * (j % 2)
                gained("n4_turned", j, P, uF[:, k0:k0 + 4, t * P:t * P + P],
                       col[:, C_PREFFN + k0:C_PREFFN + k0 + 4]).then_inc(S("uF_ready"), 1)

            def square_pair(i):
                for s in range(2):
                    for c in range(FF_GROUP):
                        dve.wait_ge(S("relu_made"), (i * 2 + s) * FF_GROUP + c + 1)
                        nc.vector.tensor_tensor(f1T[:, s, c, :], f1T[:, s, c, :], f1T[:, s, c, :], ALU.mult)\
                            .then_inc(S("f1_ready"), 1)

            with dve.Fori(0, FF_PAIRS) as i:
                square_pair(i)
            for t in range(REAL):
                dve.wait_ge(S("rms_ready"), RMS_PF + t + 1)
                link(nc.vector.reciprocal(stat[:, 34 + t:35 + t], stat[:, 34 + t:35 + t]))
                link(nc.vector.scalar_tensor_tensor(out=nat2[:, t, :], in0=pairs[t][:, :], scalar=stat[:, 34 + t:35 + t],
                                               in1=row[:, R_POSTFFN:R_POSTFFN + D], op0=ALU.mult, op1=ALU.mult))
                nc.vector.tensor_tensor(h[:, t, :], h[:, t, :], nat2[:, t, :], ALU.add).then_inc(S("out_ready"), 1)

        @block.tensor
        def _(pe):
            pe.sem_inc(S("v_used"), V_PRIME)
            pe.sem_inc(S("u_used"), RING)
            pe.sem_inc(S("y_added"), 2)

            def turn(src, n, j, b, made):
                for k in range(4):
                    c = 4 * (j % 2) + k
                    ins = nc.tensor.transpose(ps(b)[:, k * P:k * P + n], src[:, c * P:c * P + P], ident[0:n, 0:n])
                ins.then_inc(S(made), 1)

            pe.wait_ge(S("masks_ready"), 4)
            for j in range(6):
                t, n = j // 2, ROWS[j // 2]
                pe.wait_ge(S("n1_ready"), t + 1)
                turn(nat[0:n, t, :], n, j, j, "n1_turned")
            pe.wait_ge(S("hnT_ready"), 6)
            seen = set()
            for job in PJ:
                name, kind, bi, c0, t0, n = job
                nj = EV[name][0]
                if bi not in seen:
                    seen.add(bi)
                    pe.wait_ge(S(f"w_in_loaded{bi}"), 16)
                if nj >= 8:
                    _, e, k = EV[PJ[nj - 8][0]]
                    pe.wait_ge(S(f"evac_{e}"), k)
                b = ps(nj % 8)
                for k in range(KD):
                    if kind == "T":
                        w = wlast[:, k, :] if bi == 6 else w_slice(bi, c0, P)[:, k, :]
                        m = RANK if bi == 6 else P
                        ins = nc.tensor.matmul(b[0:m, 0:n], w, hnT[:, k, t0:t0 + n], start=(k == 0), stop=(k == KD - 1))
                    else:
                        ins = nc.tensor.matmul(b[0:n, :], hnT[:, k, t0:t0 + n], w_slice(bi, 0, W_COLS)[:, k, :],
                                               start=(k == 0), stop=(k == KD - 1))
                ins.then_inc(S("proj_made"), 1)
            pe.wait_ge(S("row_loaded"), 32)
            pe.wait_ge(S("evac_v"), max(k for _, e, k in EV.values() if e == "v"))
            pe.wait_ge(S("evac_a"), max(k for _, e, k in EV.values() if e == "a"))
            for c in range(2):
                ins = nc.tensor.matmul(ps(c)[:, 0:TOK], wgate[:, c * P:c * P + P], glrT[0:RANK, :], start=True, stop=True)
            ins.then_inc(S("lg_made"), 1)

            def mm(o, a, b, start, stop):
                return nc.tensor.matmul(o, a, b, start=start, stop=stop, skip_group_check=True)

            def sb_scores(i):
                c, r = i // 2, slice(64 * (i % 2), 64 * (i % 2) + 64)
                z = pairs[i % 2]
                if i >= 2:
                    pe.wait_ge(S("aT_made"), i - 1)
                mm(z[:, 0:256], sbkT[r, c, META:META + P], sbqT[r, c, :], True, False)
                mm(z[:, 256:512], sbkT[r, c, 0:P], sbqT[r, c, :], False, False)
                mm(z[:, 512:640], sbkT[r, c, META + P:TOK], sbqT[r, c, P:SEQ], True, False).then_inc(S("z_made"), 1)

            def sb_sums(i):
                z = pairs[i % 2]
                s = sp[:, i % 2, :]
                pe.wait_ge(S("sp_masked"), i + 1)
                mm(z[:, 0:256], ntri[:, :], s[:, 0:256], False, False)
                mm(z[:, 128:256], neg1[:, :], s[:, 512:640], False, True)
                mm(z[0:META, 256:512], ntri[0:META, 0:META], s[0:META, 256:512], False, False)
                mm(z[0:META, 256:512], neg1[:, 0:META], s[:, 0:256], False, False)
                mm(z[0:META, 384:512], neg1[:, 0:META], s[:, 512:640], False, True)
                mm(z[:, 512:640], ntri[:, :], s[:, 512:640], False, True).then_inc(S("s_made"), 1)

            def sb_values(i):
                a = aT[:, i % 2, :]
                cs = slice(64 * i, 64 * i + 64)
                pe.wait_ge(S("aT_masked"), i + 1)
                mm(ps(2)[:, cs], a[0:META, 256:384], sbv[0:META, 2, cs], True, False)
                mm(ps(2)[:, cs], a[:, 0:P], sbv[:, 0, cs], False, True)
                mm(ps(3)[:, cs], a[0:META, 384:512], sbv[0:META, 2, cs], True, False)
                mm(ps(3)[:, cs], a[:, P:SEQ], sbv[:, 0, cs], False, False)
                mm(ps(3)[:, cs], a[:, 512:640], sbv[:, 1, cs], False, True).then_inc(S("pv_made"), 1)

            for i in range(SB_HEADS + 2):
                if i < SB_HEADS:
                    sb_scores(i)
                if 1 <= i <= SB_HEADS:
                    sb_sums(i - 1)
                if i >= 2:
                    sb_values(i - 2)

            def state_product(c, n, kl, v, upd):
                if upd >= 1:
                    pe.wait_ge(S("state_ready"), upd)
                nc.tensor.transpose(ps(6)[0:n, 0:P], kl, ident[:, :]).then_inc(S("klT_made"), 1)
                pe.wait_ge(S("klnat_ready"), upd + 1)
                mm(ps(7)[:, 0:256], klnat[0:n, c, :], v, True, True).then_inc(S("st_prod"), 1)

            for c in range(2):
                pe.wait_ge(S("klM_ready"), c + 1)
                state_product(c, META, gex[:, c, 1200:1216], gv[0:META, 2, 256 * c:256 * c + 256], c)
            for u in range(4):
                t, c = divmod(u, 2)
                g = gex[:, u % 2, :]
                pe.wait_ge(S("gla_f"), u + 1)
                for hp in range(2):
                    v, r = 2 * u + hp, slice(64 * hp, 64 * hp + 64)
                    if v >= 2:
                        pe.wait_ge(S("attT_ready"), v - 1)
                    a = 0
                    for j in range(NSUB):
                        n = P - SUB * j
                        ins = mm(ps(4 + v % 2)[:, SUB * j:P], kzpad[r, u % 2, j, :], g[r, a:a + n], j == 0, j == NSUB - 1)
                        a += n
                    ins.then_inc(S("att_made"), 1)
                pe.wait_ge(S("state_ready"), 2 * t + c + 1)
                for hp in range(2):
                    v, r, hd = 2 * u + hp, slice(64 * hp, 64 * hp + 64), 2 * c + hp
                    o = ps(t)[:, hd * DV:hd * DV + DV]
                    if v >= 1:
                        pe.wait_ge(S("o_made"), v)
                    mm(o, g[r, 448:576], state[r, c, :], True, False)
                    pe.wait_ge(S("attT_ready"), v + 1)
                    mm(o, attT[:, v % 2, :], gv[:, t, hd * DV:hd * DV + DV], False, True).then_inc(S("o_made"), 1)
                if t == 0:
                    pe.wait_ge(S("o_made"), 2 * u + 2)
                    state_product(c, P, g[:, 576:704], gv[:, 0, 256 * c:256 * c + 256], 2 + c)
            for j in range(4):
                pe.wait_ge(S("mixn_ready"), j + 1)
                turn(mixn[:, j // 2, :], P, j, 4 + j, "mix_turned")
            for t in range(REAL):
                pe.wait_ge(S("w_out_loaded"), 32)
                pe.wait_ge(S("mixT_v"), t + 1)
                pe.wait_ge(S("mixT_a"), t + 1)
                for i in range(2):
                    for k in range(KD):
                        ins = nc.tensor.matmul(ps(2 * t + i), mixT[:, k, t * P:t * P + P], w_slice(2 + i, 0, W_COLS)[:, k, :],
                                               start=(k == 0), stop=(k == KD - 1))
                ins.then_inc(S("mix_made"), 1)
            for j in range(4):
                pe.wait_ge(S("hn2_ready"), j // 2 + 1)
                turn(hn2[:, j // 2, :], P, j, 4 + j, "n2_turned")
            pe.wait_ge(S("hn2T_ready"), 4)
            pe.wait_ge(S("w_pq_loaded"), 32)
            for c in range(HEADS):
                if c >= 4:
                    pe.wait_ge(S("qpT_ready"), c - 3)
                for k in range(KD):
                    ins = nc.tensor.matmul(ps(c % 4)[:, 0:SEQ], w_slice(c // 4, (c % 4) * P, P)[:, k, :], hn2T[:, k, :],
                                           start=(k == 0), stop=(k == KD - 1))
                ins.then_inc(S("pq_made"), 1)
            pe.wait_ge(S("keys_loaded"), 16)
            for u in range(UNITS):
                t, hd = divmod(u, HEADS)
                pe.wait_ge(S("qpT_ready"), hd + 1)
                if u >= 2:
                    pe.wait_ge(S("score_ready"), u - 1)
                for half in range(2):
                    r = slice(64 * half, 64 * half + 64)
                    ins = mm(ps(4 + 2 * (u % 2) + half)[:, 0:P], qpT[r, hd, t * P:t * P + P], keyT[r, hd, :], True, True)
                ins.then_inc(S("score_made"), 1)
            pe.wait_ge(S("score_ready"), UNITS)
            with pe.Fori(0, PASSES) as b:
                for p in range(2):
                    pe.wait_ge(S("y_added"), b * 2 + p + 1)
                    for k in range(TOPK):
                        s = k % RING
                        pe.wait_ge(S("diag_ready"), (b * 2 + p) * TOPK + k + 1)
                        pe.wait_ge(S(f"v_row{s}"), (b * 4 + 2 * p + k // RING + 1) * 16)
                        for half in range(2):
                            ins = nc.tensor.matmul(pairs[p][:, 512 * half:512 * half + 512], diag[:, k, :],
                                                   vring[s][:, 512 * half:512 * half + 512],
                                                   start=(k == 0), stop=(k == TOPK - 1))
                        ins.then_inc(S("v_used"), 1)
            for j in range(6):
                t, n = j // 2, ROWS[j // 2]
                pe.wait_ge(S("n3_ready"), t + 1)
                turn(nat2[0:n, t, :], n, j, j, "n3_turned")
            pe.wait_ge(S("uT_ready"), 6)
            pe.wait_ge(S("w_in2_loaded"), 48)
            for job in PJ2:
                name, kind, c0, t0, n = job
                nj = EV2[name][0]
                if nj >= 8:
                    _, e, k = EV2[PJ2[nj - 8][0]]
                    pe.wait_ge(S(f"evac2_{e}"), k)
                b = ps(nj % 8)
                for k in range(KD):
                    if kind == "T":
                        ins = nc.tensor.matmul(b[:, 0:n], w2_slice(c0)[:, k, :], uT[:, k, t0:t0 + n],
                                               start=(k == 0), stop=(k == KD - 1))
                    else:
                        ins = nc.tensor.matmul(b[0:n, 0:P], uT[:, k, t0:t0 + n], w2_slice(c0)[:, k, :],
                                               start=(k == 0), stop=(k == KD - 1))
                ins.then_inc(S("proj2_made"), 1)
            pe.wait_ge(S("wbd_loaded"), 64)
            pe.wait_ge(S("evac2_v"), max(k for _, e, k in EV2.values() if e == "v"))
            pe.wait_ge(S("evac2_a"), max(k for _, e, k in EV2.values() if e == "a"))
            for c in range(4):
                pe.wait_ge(S("conv_step"), 4 * c + 4)
                if c >= 2:
                    pe.wait_ge(S("sig_made"), c - 1)
                for g in range(2):
                    ins = nc.tensor.matmul(pairs[c % 2][:, 512 * g:512 * g + TOK], wbd[:, g, c, :], xc[:, c, :],
                                           start=True, stop=True)
                ins.then_inc(S("lru_made"), 1)
            for u in range(4):
                t, hf_ = divmod(u, 2)
                k0, nk = (0, META + P) if t == 0 else (META, SEQ)
                if u >= 1:
                    pe.wait_ge(S("s2_masked"), 2 * u)
                for j in range(4):
                    c, kv = 2 * hf_ + j // 2, j % 2
                    r = slice(64 * kv, 64 * kv + 64)
                    ins = mm(ps(kv)[:, (j // 2) * 256:(j // 2) * 256 + nk], q2T[r, c, t * P:t * P + P],
                             k2T[r, k0:k0 + nk], True, True)
                ins.then_inc(S("s2_made"), 1)
                pe.wait_ge(S("m_step"), 5 * u + 5)
                if u >= 1:
                    pe.wait_ge(S("pT_ready"), u)
                kt = [(META, 0), (P, META)] if t == 0 else [(P, 0), (P, P)]
                for j in range(4):
                    for i, (n, a) in enumerate(kt):
                        ins = nc.tensor.transpose(ps(2 + j // 2)[0:n, (j % 2) * 256 + i * P:(j % 2) * 256 + i * P + P],
                                                  S2[:, j, a:a + n], ident[:, :])
                ins.then_inc(S("p_turned"), 1)
                pe.wait_ge(S("pT_ready"), u + 1)
                pe.wait_ge(S("sig_made"), 4)
                if u >= 1:
                    pe.wait_ge(S("o2_ready"), u)
                tiles = [2, 0] if t == 0 else [0, 1]
                for cc in range(2):
                    o = ps(4)[:, cc * P:cc * P + P]
                    for kv in range(2):
                        for i in range(2):
                            n = kt[i][0]
                            ins = mm(o, v2[0:n, tiles[i], kv, :], pT[0:n, 2 * cc + kv, i, :],
                                     kv == 0 and i == 0, kv == 1 and i == 1)
                ins.then_inc(S("o2_made"), 1)
            for t in range(REAL):
                pe.wait_ge(S("w_out2_loaded"), 32)
                pe.wait_ge(S("o2_ready"), 4)
                pe.wait_ge(S("rec_ready"), 1)
                for i in range(2):
                    for k in range(KD):
                        ins = nc.tensor.matmul(pairs[t][:, 512 * i:512 * i + 512], mixT2[:, k, t * P:t * P + P],
                                               w_slice(2 + i, 0, W_COLS)[:, k, :], start=(k == 0), stop=(k == KD - 1))
                ins.then_inc(S("mix2_made"), 1)
            for j in range(4):
                pe.wait_ge(S("n4_ready"), j // 2 + 1)
                turn(nat2[:, j // 2, :], P, j, j, "n4_turned")
            pe.wait_ge(S("uF_ready"), 4)

            def ff_pair(i, first, last):
                for s in range(2):
                    pe.wait_ge(S(f"w_ff1_loaded{s}"), (i + 1) * 16)
                    for c in range(FF_GROUP):
                        if not (first and s == 0):
                            pe.wait_ge(S("relu_made"), (i * 2 + s) * FF_GROUP + c - 3)
                        for k in range(KD):
                            ins = nc.tensor.matmul(ps(c)[:, 0:SEQ], w_slice(FF_AT[s], c * P, P)[:, k, :], uF[:, k, :],
                                                   start=(k == 0), stop=(k == KD - 1))
                        ins.then_inc(S("f1_made"), 1)
                for s in range(2):
                    pe.wait_ge(S(f"w_ff2_loaded{s}"), (i + 1) * 16)
                    for c in range(FF_GROUP):
                        pe.wait_ge(S("f1_ready"), (i * 2 + s) * FF_GROUP + c + 1)
                        for t in range(REAL):
                            for half in range(2):
                                ins = mm(pairs[t][:, 512 * half:512 * half + 512], f1T[:, s, c, t * P:t * P + P],
                                         blk(FF_AT[s] + 1, [FF_GROUP, D])[:, c, 512 * half:512 * half + 512],
                                         first and s == 0 and c == 0, last and s == 1 and c == FF_GROUP - 1)
                    ins.then_inc(S("f2_group"), 1)
                return ins

            ff_pair(0, True, False)
            with pe.Fori(1, FF_PAIRS - 1) as i:
                ff_pair(i, False, False)
            ff_pair(FF_PAIRS - 1, False, True)


def kernel(**inputs):
    import numpy as np
    import concourse.bacc as bacc
    from concourse.bass_utils import run_bass_kernel_spmd

    a = {k: np.asarray(v) for k, v in inputs.items()}

    def chunks(v):
        return v.reshape(-1, P).T

    cols = np.concatenate([
        chunks(a["norm1_g"][0]), chunks(a["g_pre_mix_2"][0]), chunks(a["g_pre_ffn_2"][0]), chunks(a["b_gate_up"][0]),
        a["conv_w_2"][0].reshape(CONV, 4, P).transpose(2, 1, 0).reshape(P, 16), chunks(a["conv_b_2"][0]),
        chunks(a["b_a_2"][0]), chunks(a["b_x_2"][0]), chunks(a["lru_lambda_2"][0])], axis=1)
    sinks = a["attn_sinks_2"][0].reshape(KVH, 4).T.reshape(-1)
    rows = np.concatenate([a["sb_norm_g"][0], a["gla_norm_g"][0], a["norm2_g"][0], a["norm_f_g"], a["g_post_mix_2"][0],
                           a["g_post_ffn_2"][0], sinks])
    keys = np.stack([a["sub_keys1"][0], a["sub_keys2"][0]]).transpose(0, 3, 1, 2).reshape(P, HEADS, NKEYS)
    w_in2 = a["w_in_2"][0]
    q = w_in2[:, 0:512].reshape(D, KVH, 4, 64).transpose(0, 2, 1, 3).reshape(D, 512)
    w_in2 = np.concatenate([q, w_in2[:, 512:]], axis=1)
    w_out2 = a["w_out_2"][0]
    o = w_out2[0:512].reshape(KVH, 4, 64, D).transpose(1, 0, 2, 3).reshape(512, D)
    w_out2 = np.concatenate([o, w_out2[512:]], axis=0)
    arrays = {
        "x": a["x"][0], "meta1": a["meta_tokens"], "meta2": a["meta_tokens_2"], "cols": cols, "rows": rows,
        "w_in": a["w_in"][0], "w_gate": a["w_gate_up"][0], "w_out": a["w_out"][0], "w_peer_q": a["w_peer_q"][0],
        "keys": keys, "expert_u": a["expert_u"][0], "expert_v": a["expert_v"][0], "w_in2": w_in2, "w_a": a["w_a_2"][0],
        "w_x": a["w_x_2"][0], "w_out2": w_out2, "w_ff1": a["w_ff1_2"][0], "w_ff2": a["w_ff2_2"][0],
    }
    nc = bacc.Bacc("TRN2", target_bir_lowering=False, num_devices=1)
    feed, args = {}, []
    for name, v in arrays.items():
        v = np.ascontiguousarray(v)
        feed[f"in_{name}"] = v
        args.append(nc.dram_tensor(f"in_{name}", v.shape, F32, kind="ExternalInput").ap())
    out = nc.dram_tensor("out", (SEQ, D), F32, kind="ExternalOutput").ap()
    two_blocks_kernel(nc, *args, out)
    r = run_bass_kernel_spmd(nc, [feed], core_ids=[0])
    return r.results[0]["out"].reshape(1, SEQ, D)
```

```python
from contextlib import ExitStack

import concourse.bass as bass
from concourse import mybir

ALU = mybir.AluOpType
ACT = mybir.ActivationFunctionType
F32 = mybir.dt.float32
U32 = mybir.dt.uint32
R32 = mybir.dt.float32r
AX = mybir.AxisListType.X

P = 128
D = 1024
KD = D // P
SEQ = 256
META = 16
TOK = META + SEQ
EPS = 1e-6
ROWS = [P, P, META]
COL0 = [META, META + P, 0]
REAL = 2

SB_HEADS, SB_DIM = 8, 64
GLA_HEADS, DK, DV, RANK, TAU = 4, 64, 128, 16, 16.0
SUB = 32
NSUB = P // SUB

HEADS, NKEYS, TOPK = 8, 128, 16
RING = 8
UNITS = REAL * HEADS
PASSES = UNITS // 2
RMS_N1, RMS_N2, RMS_NF, RMS_N3, RMS_PM, RMS_N4, RMS_PF = 0, 3, 5, 7, 10, 12, 14
ROUTE_STEPS = 19
V_PRIME = 16

ATT, KVH = 8, 2
CHUNKS_LRU = 4
CONV = 4
LRU_C = 8.0
NEG = -1e30
FF_GROUP = 4
FF_GROUPS = 4 * D // (FF_GROUP * P)
FF_PAIRS = FF_GROUPS // 2

W_COLS = 512
C_NORM1, C_PREMIX, C_PREFFN, C_BG, C_CONVW, C_CONVB, C_BA, C_BX, C_LAM, C_END = (
    0, 8, 16, 24, 26, 42, 46, 50, 54, 58)
R_SB, R_GLA, R_NORM2, R_NORMF, R_POSTMIX, R_POSTFFN, R_SINK, R_END = (
    0, 512, 1024, 2048, 3072, 4096, 5120, 5128)


def proj_plan():
    jobs = []
    for c in range(2):
        jobs.append((("gq", c), "T", 3, c * P, META, SEQ))
    for c in range(2):
        jobs.append((("gk", c), "T", 3, 256 + c * P, 0, TOK))
    jobs.append((("glr", 0), "T", 6, 0, 0, TOK))
    for t in range(3):
        jobs.append((("gv", t), "N", 4, 0, COL0[t], ROWS[t]))
    for t in range(3):
        jobs.append((("sbv", t), "N", 2, 0, COL0[t], ROWS[t]))
    for c in range(4):
        jobs.append((("sbq", c), "T", 0, c * P, META, SEQ))
    for c in range(4):
        jobs.append((("sbk", c), "T", 1, c * P, 0, TOK))
    for t in range(2):
        jobs.append((("gr", t), "N", 5, 0, COL0[t], ROWS[t]))
    return jobs


def proj2_plan():
    jobs = []
    for c in range(4):
        jobs.append((("xr", c), "T", 768 + c * P, 0, TOK))
    for c in range(4):
        jobs.append((("yr", c), "T", 1280 + c * P, META, SEQ))
    for c in range(4):
        jobs.append((("q", c), "T", c * P, META, SEQ))
    jobs.append((("k", 0), "T", 512, 0, TOK))
    for t in range(3):
        jobs.append((("v", t), "N", 640, COL0[t], ROWS[t]))
    return jobs


def evac_plan(jobs, engine_of):
    done = {"v": 0, "a": 0}
    out = {}
    for n, job in enumerate(jobs):
        e = engine_of(job[0])
        done[e] += 1
        out[job[0]] = (n, e, done[e])
    return out


def two_blocks_kernel(nc, x, meta1, meta2, cols, rows, w_in, w_gate, w_out, w_peer_q, keys, expert_u,
                      expert_v, w_in2, w_a, w_x, w_out2, w_ff1, w_ff2, out):
    PJ, PJ2 = proj_plan(), proj2_plan()
    EV = evac_plan(PJ, lambda n: "a" if n[0] in ("gv", "sbq", "sbk", "gr") else "v")
    EV2 = evac_plan(PJ2, lambda n: "a" if n[0] in ("yr", "q") else "v")

    with ExitStack() as ctx:
        sems = {}

        def S(name):
            if name not in sems:
                sems[name] = ctx.enter_context(nc.semaphore(name))
            return sems[name]

        def sb(name, shape, dt=F32):
            return ctx.enter_context(nc.sbuf_tensor(name, shape, dt))

        bank = [ctx.enter_context(nc.psum_tensor(f"bank{i}", [P, 512], F32)) for i in range(4)]
        pairs = [ctx.enter_context(nc.psum_tensor(f"pair{i}", [P, 1024], F32)) for i in range(2)]

        def ps(i):
            return bank[i][:, :] if i < 4 else pairs[(i - 4) // 2][:, (i % 2) * 512:(i % 2) * 512 + 512]

        with ExitStack() as first:
            wblk = [first.enter_context(nc.sbuf_tensor(f"wblk{i}", [P, KD * W_COLS], F32)) for i in range(6)]
            area = first.enter_context(nc.sbuf_tensor("area", [P, 76 * 256], F32))
        wblk_r = [sb(f"wblk_r{i}", [P, KD * W_COLS], R32) for i in range(6)]
        area_r = sb("area_r", [P, 76 * 256], R32)
        wlast = sb("wlast", [P, KD, RANK])
        row = sb("row", [P, R_END])
        col = sb("col", [P, C_END])
        ident = sb("ident", [P, P])
        ntri = sb("ntri", [P, P])
        neg1 = sb("neg1", [P, P])
        causal = sb("causal", [P, P])
        h = sb("h", [P, REAL, D])
        stat = sb("stat", [P, 64])
        epsc = sb("epsc", [P, 1])
        wgate = sb("wgate", [RANK, 2 * P])
        small = sb("small", [P, 256])
        small2 = sb("small2", [P, 256])

        def at(kb, shape, dt=F32):
            n = 1
            for s in shape:
                n *= s
            a = (area_r if dt is R32 else area)[:, int(kb * 256):int(kb * 256) + n]
            if dt is U32:
                a = a.bitcast(dt)
            if len(shape) == 1:
                return a
            names = "abcd"[:len(shape)]
            return a.rearrange(f"p ({' '.join(names)}) -> p {' '.join(names)}",
                               **{k: s for k, s in zip(names[1:], shape[1:])})

        def blk(i, shape, dt=F32):
            names = "abcd"[:len(shape)]
            return (wblk_r if dt is R32 else wblk)[i][:, :].rearrange(f"p ({' '.join(names)}) -> p {' '.join(names)}",
                                           **{k: s for k, s in zip(names[1:], shape[1:])})

        hM = at(0, [D])
        hnT = at(4, [KD, TOK])
        sbqT = at(12.5, [4, SEQ])
        sbkT = at(16.5, [4, TOK])
        gqT = at(20.75, [2, SEQ])
        gkT = at(22.75, [2, TOK])
        glrT = at(24.875, [TOK])
        nat = at(26, [3, D])
        sbv = at(26, [3, 512])
        gv = at(32, [3, 512])
        gr = at(38, [2, 512])
        sp = at(42, [2, 640])
        aT = at(47, [2, 640])
        tmp = at(52, [2, 640])
        nb = at(57, [2, TOK])
        pb = at(59.125, [2, TOK])
        lgt = at(61.25, [2, TOK])
        gex = at(63.5, [2, 1216])
        state = at(73, [2, DV])
        klnat = at(74, [2, P])
        attT = at(75, [2, P])
        kzpad = at(4, [2, NSUB, P])
        mixn = at(52, [REAL, D])
        sqr = at(60, [512])
        mixT = at(12.5, [KD, SEQ])
        hn2 = at(26, [REAL, D])
        hn2T = at(34, [KD, SEQ])
        qpT = at(0, [HEADS, SEQ])
        score = at(8, [UNITS + 1, 2 * NKEYS])
        scoref = at(8, [(UNITS + 1) * 2 * NKEYS])
        keyT = at(42, [HEADS, NKEYS])
        diag = at(34, [TOPK, P])
        cur = at(46, [2, 256])
        cur2 = at(48, [256])
        cand = at(49, [256])
        pick = at(50, [512])
        wtail = at(52, [KD, 768])

        v16 = small[:, 0:32]
        i16 = small[:, 32:64].bitcast(U32)
        if16 = small[:, 64:96]
        sc16 = small[:, 96:112]
        pos = small[:, 112:128].bitcast(U32)
        posij = small[:, 128:160].bitcast(U32)
        posf = small[:, 160:192]
        eij = small[:, 192:224]
        nmx = small[:, 224:225]
        den = small[:, 225:226]
        rden = small[:, 226:227]
        uidx = small2[:, 0:32].bitcast(U32).rearrange("p (a b) -> p a b", a=2)
        vidx = small2[:, 192:224].bitcast(U32).rearrange("p (a b) -> p a b", a=2)
        dots = small2[:, 32:64].rearrange("p (a b) -> p a b", a=2)
        gate = small2[:, 64:96].rearrange("p (a b) -> p a b", a=2)
        ggel = small2[:, 96:128].rearrange("p (a b) -> p a b", a=2)
        gw = small2[:, 128:160].rearrange("p (a b) -> p a b", a=2)
        ex16 = small2[:, 160:176]
        iota16 = small2[:, 176:192]
        uring = [blk(2 + s // 4, [4, D])[:, s % 4, :] for s in range(RING)]
        vring = [blk(4 + s // 4, [4, D])[:, s % 4, :] for s in range(RING)]

        hM2 = at(0, [D])
        nat2 = at(8, [3, D])
        uT = at(28.5, [KD, TOK])
        q2T = at(37, [4, SEQ])
        k2T = at(41, [TOK])
        v2 = at(42.25, [3, KVH, P])
        xr = at(4, [4, TOK + 3])
        xc = at(20, [4, TOK])
        geluy = at(46, [4, SEQ])
        lr = at(8.5, [4, TOK])
        li = at(12.75, [4, TOK])
        lt = at(68, [4, TOK])
        uFh, uFl = at(28, [KD, SEQ], R32), at(36, [KD, SEQ], R32)
        uF = at(36, [KD, SEQ])
        lm = at(24.25, [4, TOK])
        wbd = row[:, 0:1024].rearrange("p (g c n) -> p g c n", g=2, c=4)
        mask2 = row[:, 1024:1536].rearrange("p (t n) -> p t n", t=2)
        mixT2 = at(52, [KD, SEQ])
        S2 = at(60, [4, SEQ])
        pT = at(64, [4, 2, P])
        f1h, f1l = at(20, [2, FF_GROUP, SEQ], R32), at(8, [2, FF_GROUP, SEQ], R32)
        f1 = at(8, [2, FF_GROUP, SEQ])

        def w_slice(i, c0, n, dt=F32):
            return blk(i, [KD, W_COLS], dt)[:, :, c0:c0 + n]

        def w2_slice(c0):
            if c0 < 1024:
                return blk(c0 // 512, [KD, W_COLS])[:, :, c0 % 512:c0 % 512 + P]
            return wtail[:, :, c0 - 1024:c0 - 1024 + P]

        FF_AT = [4, 0]

        FF_STAGES = 4

        def ff_low(stage, c, dt=R32):
            s = stage % 2
            if stage < 2:
                return w_slice(FF_AT[s], c * P, P, dt)
            return blk(FF_AT[s] + 1, [FF_GROUP, D], dt)[:, c, :]

        def ff_high(stage, c):
            if stage in (0, 2):
                b = wblk_r[2 + stage // 2][:, :]
            else:
                b = at(44 + 16 * (stage // 2), [KD * W_COLS], R32)
            if stage < 2:
                return b.rearrange("p (k n) -> p k n", k=KD)[:, :, c * P:c * P + P]
            return b.rearrange("p (c n) -> p c n", c=FF_GROUP)[:, c, :]

        block = ctx.enter_context(nc.Block())

        @block.sync
        def _(sp_q):
            def block_of(src, c0):
                return src.rearrange("(k p) n -> p k n", p=P)[:, :, c0:c0 + W_COLS]

            sp_q.dma_start(h[:, 0, :], x[0:P, :]).then_inc(S("h_loaded0"), 16)
            sp_q.dma_start(h[:, 1, :], x[P:SEQ, :]).then_inc(S("h_loaded1"), 16)
            sp_q.dma_start(hM[0:META, :], meta1).then_inc(S("h_loaded2"), 16)
            sp_q.dma_start(col[:, :], cols).then_inc(S("col_loaded"), 16)
            for i in (3, 4, 2, 0, 1, 5):
                sp_q.dma_start(blk(i, [KD, W_COLS]), block_of(w_in, i * W_COLS)).then_inc(S(f"w_in_loaded{i}"), 16)
                if i == 3:
                    sp_q.dma_start(wlast[:, :, :], w_in.rearrange("(k p) n -> p k n", p=P)[:, :, 6 * W_COLS:])\
                        .then_inc(S("w_in_loaded6"), 16)
                    sp_q.dma_start(wgate[:, :], w_gate).then_inc(S("gate_loaded"), 16)
            sp_q.dma_start(row[:, :], rows.partition_broadcast(P)).then_inc(S("row_loaded"), 16)
            sp_q.wait_ge(S("proj_made"), len(PJ))
            for i in range(2):
                sp_q.dma_start(blk(2 + i, [KD, W_COLS]), block_of(w_out, i * W_COLS)).then_inc(S("w_out_loaded"), 16)
            for i in range(2):
                sp_q.dma_start(blk(i, [KD, W_COLS]), block_of(w_peer_q, i * W_COLS)).then_inc(S("w_pq_loaded"), 16)
            sp_q.wait_ge(S("mix_turned"), 4)
            sp_q.dma_start(keyT[:, :, :], keys).then_inc(S("keys_loaded"), 16)
            sp_q.wait_ge(S("pq_made"), HEADS)
            for i in range(2):
                sp_q.dma_start(blk(i, [KD, W_COLS]), block_of(w_in2, i * W_COLS)).then_inc(S("w_in2_loaded"), 16)
            sp_q.dma_start(wtail[:, :, :], w_in2.rearrange("(k p) n -> p k n", p=P)[:, :, 1024:1792])\
                .then_inc(S("w_in2_loaded"), 16)
            sp_q.wait_ge(S("u_used"), RING + UNITS * TOPK)
            for i in range(2):
                sp_q.dma_start(blk(2 + i, [KD, W_COLS]), block_of(w_out2, i * W_COLS)).then_inc(S("w_out2_loaded"), 16)
            sp_q.dma_start(hM2[0:META, :], meta2).then_inc(S("h2_loaded"), 16)
            w1v = w_ff1.rearrange("(k p) n -> p k n", p=P)
            w2v = w_ff2.rearrange("(g c p) n -> p g c n", p=P, c=FF_GROUP)

            def load_ff1(g, s):
                sp_q.dma_start(blk(FF_AT[s], [KD, W_COLS]), w1v[:, :, bass.ds(g * W_COLS, W_COLS)])\
                    .then_inc(S(f"w_ff1_loaded{s}"), 16)

            def load_ff2(g, s):
                sp_q.dma_start(blk(FF_AT[s] + 1, [FF_GROUP, D]), w2v[:, bass.ds(g, 1), :, :].rearrange("p g c n -> p (g c) n"))\
                    .then_inc(S(f"w_ff2_loaded{s}"), 16)

            sp_q.wait_ge(S("v_used"), V_PRIME + UNITS * TOPK)
            load_ff1(0, 0)
            load_ff2(0, 0)
            sp_q.wait_ge(S("proj2_made"), len(PJ2))
            load_ff1(1, 1)
            load_ff2(1, 1)
            with sp_q.Fori(1, FF_PAIRS) as i:
                for s in range(2):
                    sp_q.wait_ge(S("f1_made"), (i * 2 + s - 1) * FF_GROUP)
                    load_ff1(i * 2 + s, s)
                for s in range(2):
                    sp_q.wait_ge(S("f2_group"), i * 2 + s - 1)
                    load_ff2(i * 2 + s, s)
            for t in range(REAL):
                sp_q.wait_ge(S("out_ready"), t + 1)
                sp_q.dma_start(out[t * P:(t + 1) * P, :], h[:, t, :]).then_inc(S("out_stored"), 16)
            sp_q.wait_ge(S("out_stored"), 16 * REAL)

        @block.gpsimd
        def _(pool):
            nc.gpsimd.memset(ident[:, :], 0.0).then_inc(S("masks_cleared"), 1)
            nc.gpsimd.memset(ntri[:, :], -1.0).then_inc(S("masks_cleared"), 1)
            nc.gpsimd.memset(neg1[:, :], -1.0).then_inc(S("masks_ready"), 1)
            nc.gpsimd.memset(causal[:, :], 1.0).then_inc(S("masks_cleared"), 1)
            pool.wait_ge(S("masks_cleared"), 3)
            nc.gpsimd.affine_select(out=ident[:, :], in_=ident[:, :], compare_op=ALU.not_equal, fill=1.0, base=0,
                                    pattern=[[-1, P]], channel_multiplier=1).then_inc(S("masks_ready"), 1)
            nc.gpsimd.affine_select(out=ntri[:, :], in_=ntri[:, :], compare_op=ALU.is_ge, fill=0.0, base=0,
                                    pattern=[[-1, P]], channel_multiplier=1).then_inc(S("masks_ready"), 1)
            nc.gpsimd.affine_select(out=causal[:, :], in_=causal[:, :], compare_op=ALU.is_ge, fill=0.0, base=0,
                                    pattern=[[1, P]], channel_multiplier=-1).then_inc(S("masks_ready"), 1)
            nc.gpsimd.iota(iota16, pattern=[[1, TOPK]], base=0, channel_multiplier=0,
                           allow_small_or_imprecise_dtypes=True).then_inc(S("iota_ready"), 1)
            pool.wait_ge(S("proj_made"), len(PJ))
            nc.gpsimd.memset(kzpad[:, :, :, :], 0.0).then_inc(S("kz_cleared"), 1)

            def keep_past(view):
                return nc.gpsimd.affine_select(out=view, in_=view, compare_op=ALU.is_gt, fill=0.0, base=0,
                                               pattern=[[1, P]], channel_multiplier=-1)

            for i in range(SB_HEADS + 1):
                if i < SB_HEADS:
                    pool.wait_ge(S("sp_made"), i + 1)
                    keep_past(sp[:, i % 2, 0:P])
                    keep_past(sp[:, i % 2, 512:640]).then_inc(S("sp_masked"), 1)
                if i >= 1:
                    pool.wait_ge(S("aT_made"), i)
                    keep_past(aT[:, (i - 1) % 2, 0:P])
                    keep_past(aT[:, (i - 1) % 2, 512:640]).then_inc(S("aT_masked"), 1)

            def gather_u(u, p, k):
                s = k % RING
                pool.wait_ge(S("u_used"), u * TOPK + k + 1)
                pool.sem_inc(S("gather_turn"), 1)
                nc.gpsimd.indirect_dma_start(
                    out=uring[s], out_offset=None, in_=expert_u,
                    in_offset=bass.IndirectOffsetOnAxis(ap=uidx[:, p, k:k + 1], axis=0),
                ).then_inc(S(f"u_row{s}"), 16)

            def gather_v(u, p, k):
                s = k % RING
                pool.wait_ge(S("v_used"), u * TOPK + k + 1 + V_PRIME - RING)
                pool.sem_inc(S("gather_turn"), 1)
                nc.gpsimd.indirect_dma_start(
                    out=vring[s], out_offset=None, in_=expert_v,
                    in_offset=bass.IndirectOffsetOnAxis(ap=vidx[:, p, k:k + 1], axis=0),
                ).then_inc(S(f"v_row{s}"), 16)

            def gather_pass(b, last):
                for p in range(2):
                    u = b * 2 + p
                    ahead = not (last and p == 1)
                    if ahead:
                        pool.wait_ge(S("uidx_ready"), u + 2)
                    pool.wait_ge(S("vidx_ready"), u + 1)
                    for k in range(TOPK):
                        if ahead:
                            gather_u(u + 1, 1 - p, k)
                        gather_v(u, p, k)

            pool.wait_ge(S("mix_made"), REAL)
            pool.wait_ge(S("uidx_ready"), 1)
            for k in range(TOPK):
                gather_u(0, 0, k)
            with pool.Fori(0, PASSES - 1) as b:
                gather_pass(b, False)
            gather_pass(PASSES - 1, True)

            pool.wait_ge(S("hn2_ready"), REAL)
            nc.gpsimd.memset(mask2, 0.0).then_inc(S("mask2_cleared"), 1)
            nc.gpsimd.memset(wbd, 0.0).then_inc(S("wbd_cleared"), 1)
            pool.wait_ge(S("mask2_cleared"), 1)
            nc.gpsimd.affine_select(out=mask2[:, 0, 0:META], in_=mask2[:, 0, 0:META], compare_op=ALU.is_gt, fill=NEG,
                                    base=P - META, pattern=[[1, META]], channel_multiplier=-1).then_inc(S("mask2_ready"), 1)
            nc.gpsimd.affine_select(out=mask2[:, 0, META:META + P], in_=mask2[:, 0, META:META + P], compare_op=ALU.is_ge,
                                    fill=NEG, base=0, pattern=[[-1, P]], channel_multiplier=1).then_inc(S("mask2_ready"), 1)
            nc.gpsimd.affine_select(out=mask2[:, 1, 0:P], in_=mask2[:, 1, 0:P], compare_op=ALU.is_gt, fill=NEG,
                                    base=0, pattern=[[1, P]], channel_multiplier=-1).then_inc(S("mask2_ready"), 1)
            nc.gpsimd.affine_select(out=mask2[:, 1, P:SEQ], in_=mask2[:, 1, P:SEQ], compare_op=ALU.is_ge, fill=NEG,
                                    base=0, pattern=[[-1, P]], channel_multiplier=1).then_inc(S("mask2_ready"), 1)
            pool.wait_ge(S("wbd_cleared"), 1)
            for g, w in enumerate((w_a, w_x)):
                for half in range(2):
                    src = w.rearrange("(c a) i o -> a i c o", a=2)[half]
                    pool.dma_start(wbd[64 * half:64 * half + 64, g, :, 64 * half:64 * half + 64], src)\
                        .then_inc(S("wbd_loaded"), 16)
        @block.scalar
        def _(act):
            linked = [0]

            def link(ins):
                linked[0] += 1
                ins.then_inc(S("scalar_step"), 1)
                act.wait_ge(S("scalar_step"), linked[0])

            for t in range(3):
                n = ROWS[t]
                src = h[:, t, :] if t < 2 else hM[0:META, :]
                act.wait_ge(S(f"h_loaded{t}"), 16)
                link(nc.scalar.activation(nat[0:n, t, :], src, ACT.Square, accum_out=stat[0:n, t:t + 1]))
            act.wait_ge(S("eps_ready"), 1)
            for t in range(3):
                n = ROWS[t]
                nc.scalar.activation(stat[0:n, 3 + t:4 + t], stat[0:n, t:t + 1], ACT.Sqrt, scale=1.0 / D,
                                     bias=epsc[0:n, :]).then_inc(S("rms_ready"), 1)

            def evac(job):
                name = job[0]
                n, e, k = EV[name]
                if e != "a":
                    return
                b = ps(n % 8)
                act.wait_ge(S("proj_made"), n + 1)
                kind, i = name
                if kind == "gv":
                    r = ROWS[i]
                    ins = nc.scalar.activation(gv[0:r, i, :], b[0:r, :], ACT.Copy)
                elif kind == "gr":
                    ins = nc.scalar.activation(gr[:, i, :], b, ACT.Copy)
                elif kind == "sbq":
                    ins = nc.scalar.activation(sbqT[:, i, :], b[:, 0:SEQ], ACT.Copy, scale=SB_DIM ** -0.5)
                elif kind == "sbk":
                    ins = nc.scalar.activation(sbkT[:, i, :], b[:, 0:TOK], ACT.Copy)
                ins.then_inc(S("evac_a"), 1)

            for job in PJ:
                evac(job)
            act.wait_ge(S("lg_min"), 2)
            link(nc.scalar.activation(lgt[:, 0, :], ps(0)[:, 0:TOK], ACT.Abs, bias=col[:, C_BG:C_BG + 1]))
            link(nc.scalar.activation(lgt[:, 1, :], ps(1)[:, 0:TOK], ACT.Abs, bias=col[:, C_BG + 1:C_BG + 2]))
            link(nc.scalar.activation(lgt[:, :, :], lgt[:, :, :], ACT.Exp, scale=-1.0))
            nc.scalar.activation(lgt[:, :, :], lgt[:, :, :], ACT.Ln, bias=1.0).then_inc(S("lg_ln"), 1)

            def sb_soft(i):
                z = pairs[i % 2][:, 0:640]
                act.wait_ge(S("z_made"), i + 1)
                link(nc.scalar.activation(tmp[:, i % 2, :], z, ACT.Abs))
                link(nc.scalar.activation(tmp[:, i % 2, :], tmp[:, i % 2, :], ACT.Exp, scale=-1.0))
                nc.scalar.activation(tmp[:, i % 2, :], tmp[:, i % 2, :], ACT.Ln, bias=1.0).then_inc(S("z_ln"), 1)

            def sb_weights(i):
                act.wait_ge(S("s_made"), i + 1)
                if i >= 2:
                    act.wait_ge(S("pv_made"), i - 1)
                nc.scalar.activation(aT[:, i % 2, :], pairs[i % 2][:, 0:640], ACT.Exp).then_inc(S("aT_made"), 1)

            for i in range(SB_HEADS + 1):
                if i < SB_HEADS:
                    if i >= 2:
                        act.wait_ge(S("sp_made"), i - 1)
                    sb_soft(i)
                if i >= 1:
                    sb_weights(i - 1)

            act.wait_ge(S("decay_ready"), 2)

            def factors_M(c):
                nc.scalar.activation(gex[:, c, 1200:1216], pb[:, c, 0:META], ACT.Exp, scale=-1.0,
                                     bias=pb[:, c, META - 1:META])
                last = COL0[0] + P - 1
                nc.scalar.activation(stat[:, 42 + c:43 + c], pb[:, c, last:last + 1], ACT.Exp).then_inc(S("gex_made"), 1)

            def factors(t, c):
                u = t * 2 + c
                g = gex[:, u % 2, :]
                o = COL0[t]
                if u >= 2:
                    act.wait_ge(S("o_made"), 2 * u - 2)
                    act.wait_ge(S("klT_made"), u + 1)
                at_ = 0
                for j in range(NSUB):
                    n = P - SUB * j
                    e = o + SUB * j + SUB - 1
                    nc.scalar.activation(g[:, at_:at_ + n], pb[:, c, o + SUB * j:o + P], ACT.Exp,
                                         bias=nb[:, c, e:e + 1])
                    at_ += n
                for j in range(NSUB):
                    e = o + SUB * j + SUB - 1
                    nc.scalar.activation(g[:, 320 + SUB * j:352 + SUB * j], pb[:, c, o + SUB * j:o + SUB * j + SUB],
                                         ACT.Exp, scale=-1.0, bias=pb[:, c, e:e + 1])
                nc.scalar.activation(g[:, 448:576], pb[:, c, o:o + P], ACT.Exp)
                nc.scalar.activation(g[:, 576:704], pb[:, c, o:o + P], ACT.Exp, scale=-1.0,
                                     bias=pb[:, c, o + P - 1:o + P]).then_inc(S("gex_made"), 1)

            factors_M(0)
            factors_M(1)
            for t in range(REAL):
                for c in range(2):
                    factors(t, c)
            act.wait_ge(S("evac_a"), EV[("gr", 1)][2])
            for t in range(REAL):
                nc.scalar.activation(gr[:, t, :], gr[:, t, :], ACT.Silu).then_inc(S("silu_made"), 1)
            for t in range(REAL):
                act.wait_ge(S("ss_made"), 2 * t + 1)
                nc.scalar.activation(stat[:, 16:24], stat[:, 8:16], ACT.Sqrt, scale=1.0 / SB_DIM,
                                     bias=epsc[:, :]).then_inc(S("hrms_made"), 1)
                act.wait_ge(S("ss_made"), 2 * t + 2)
                nc.scalar.activation(stat[:, 28:32], stat[:, 24:28], ACT.Sqrt, scale=1.0 / DV,
                                     bias=epsc[:, :]).then_inc(S("hrms_made"), 1)
            for j in range(4):
                if j % 2 == 1:
                    act.wait_ge(S("mix_turned"), j + 1)
                    nc.scalar.activation(mixT[:, 4:8, (j // 2) * P:(j // 2) * P + P],
                                         ps(4 + j).rearrange("p (a b) -> p a b", a=4), ACT.Copy).then_inc(S("mixT_a"), 1)
            for t in range(REAL):
                act.wait_ge(S("h_mixed"), t + 1)
                link(nc.scalar.activation(hn2[:, t, :], h[:, t, :], ACT.Square, accum_out=stat[:, 32 + t:33 + t]))
                nc.scalar.activation(stat[:, 34 + t:35 + t], stat[:, 32 + t:33 + t], ACT.Sqrt, scale=1.0 / D,
                                     bias=epsc[:, :]).then_inc(S("rms_ready"), 1)
            for c in range(HEADS):
                act.wait_ge(S("pq_made"), c + 1)
                nc.scalar.activation(qpT[:, c, :], ps(c % 4)[:, 0:SEQ], ACT.Copy).then_inc(S("qpT_ready"), 1)
            for u in range(UNITS):
                act.wait_ge(S("score_made"), u + 1)
                nc.scalar.activation(score[:, u, :].rearrange("p (a b) -> p a b", a=2),
                                     pairs[u % 2][:, :].rearrange("p (a b) -> p a b", a=2)[:, :, 0:P], ACT.Copy).then_inc(S("score_ready"), 1)

            act.wait_ge(S("score_ready"), UNITS)
            act.wait_ge(S("score_end_set"), 1)

            def unit_scores(u, p):
                if not isinstance(u, int) or u >= 2:
                    act.wait_ge(S("cur_used"), u - 1)
                nc.scalar.activation(cur[:, p, :], scoref[:, bass.ds(u * 256, 256)], ACT.Copy)\
                    .then_inc(S("cur_ready"), 1)

            def gate_exps(u):
                act.wait_ge(S("sc_ready"), u + 1)
                nc.scalar.activation(ex16, sc16, ACT.Exp, bias=nmx, accum_out=den).then_inc(S("gex16_ready"), 1)

            def gelu_dots(u, p):
                act.wait_ge(S("u_used"), (u + 1) * TOPK + RING)
                nc.scalar.activation(ggel[:, p, :], dots[:, p, :], ACT.Gelu).then_inc(S("gelu_ready"), 1)

            def weights_pass(b, last):
                for p in range(2):
                    u = b * 2 + p
                    act.wait_ge(S("gw_ready"), u + 1)
                    for k in range(TOPK):
                        act.wait_ge(S("v_used"), u * TOPK + k + 1)
                        nc.scalar.activation(diag[:, k, :], ident[:, :], ACT.Copy, scale=gw[:, p, k:k + 1])\
                            .then_inc(S("diag_ready"), 1)
                    if not last:
                        unit_scores(u + 3, 1 - p)
                        gate_exps(u + 2)
                    if not (last and p == 1):
                        gelu_dots(u + 1, 1 - p)

            unit_scores(0, 0)
            unit_scores(1, 1)
            gate_exps(0)
            unit_scores(2, 0)
            gate_exps(1)
            gelu_dots(0, 0)
            with act.Fori(0, PASSES - 1) as b:
                weights_pass(b, False)
            weights_pass(PASSES - 1, True)

            for t in range(REAL):
                act.wait_ge(S("y_added"), 2 + UNITS)
                link(nc.scalar.activation(nat2[:, t, :], h[:, t, :], ACT.Square, accum_out=stat[:, t:t + 1]))
                nc.scalar.activation(stat[:, 2 + t:3 + t], stat[:, t:t + 1], ACT.Sqrt, scale=1.0 / D,
                                     bias=epsc[:, :]).then_inc(S("rms_ready"), 1)
            for t in range(3):
                n = ROWS[t]
                if t < 2:
                    act.wait_ge(S("hf_ready"), t + 1)
                else:
                    act.wait_ge(S("h2_loaded"), 16)
                src = h[:, t, :] if t < 2 else hM2[0:META, :]
                link(nc.scalar.activation(nat2[0:n, t, :], src, ACT.Square, accum_out=stat[0:n, 4 + t:5 + t]))
                nc.scalar.activation(stat[0:n, 7 + t:8 + t], stat[0:n, 4 + t:5 + t], ACT.Sqrt, scale=1.0 / D,
                                     bias=epsc[0:n, :]).then_inc(S("rms_ready"), 1)
            for job in PJ2:
                n, e, k = EV2[job[0]]
                if e != "a":
                    continue
                kind, i = job[0]
                act.wait_ge(S("proj2_made"), n + 1)
                if kind == "yr":
                    nc.scalar.activation(geluy[:, i, :], ps(n % 8)[:, 0:SEQ], ACT.Gelu_apprx_tanh).then_inc(S("evac2_a"), 1)
                else:
                    nc.scalar.activation(q2T[:, i, :], ps(n % 8)[:, 0:SEQ], ACT.Copy, scale=64 ** -0.5)\
                        .then_inc(S("evac2_a"), 1)
            link(nc.scalar.activation(stat[:, 48:52], col[:, C_LAM:C_LAM + 4], ACT.Abs))
            link(nc.scalar.activation(stat[:, 48:52], stat[:, 48:52], ACT.Exp, scale=-1.0))
            nc.scalar.activation(stat[:, 48:52], stat[:, 48:52], ACT.Ln, bias=1.0).then_inc(S("lam_ln"), 1)
            for c in range(4):
                act.wait_ge(S("lru_made"), c + 1)
                b2 = pairs[c % 2]
                nc.scalar.activation(lr[:, c, :], b2[:, 0:TOK], ACT.Sigmoid, bias=col[:, C_BA + c:C_BA + c + 1])
                nc.scalar.activation(li[:, c, :], b2[:, 512:512 + TOK], ACT.Sigmoid, bias=col[:, C_BX + c:C_BX + c + 1])\
                    .then_inc(S("sig_made"), 1)
            act.wait_ge(S("sig_made"), 4)
            act.wait_ge(S("lam_ready"), 2)
            for c in range(4):
                nc.scalar.activation(lm[:, c, :], lr[:, c, :], ACT.Tanh, scale=stat[:, 52 + c:53 + c]).then_inc(S("tanh_made"), 1)
                nc.scalar.activation(lr[:, c, :], lr[:, c, :], ACT.Exp, scale=stat[:, 56 + c:57 + c]).then_inc(S("a_made"), 1)
            act.wait_ge(S("m2_made"), 1)
            nc.scalar.activation(lm[:, :, :], lm[:, :, :], ACT.Sqrt).then_inc(S("root_made"), 1)
            for u in range(4):
                act.wait_ge(S("nm_made"), u + 1)
                nk = META + P if u // 2 == 0 else SEQ
                for j in range(4):
                    nc.scalar.activation(S2[:, j, 0:nk], S2[:, j, 0:nk], ACT.Exp, bias=stat[:, 12 + j:13 + j],
                                         accum_out=stat[:, 16 + j:17 + j])
                nc.scalar.activation(stat[:, 20:24], stat[:, 20:24], ACT.Exp).then_inc(S("p_made"), 1)
            for t in range(REAL):
                act.wait_ge(S("mix2_made"), t + 1)
                link(nc.scalar.activation(nat2[:, t, :], pairs[t][:, :], ACT.Square, accum_out=stat[:, 24 + t:25 + t]))
                nc.scalar.activation(stat[:, 26 + t:27 + t], stat[:, 24 + t:25 + t], ACT.Sqrt, scale=1.0 / D,
                                     bias=epsc[:, :]).then_inc(S("rms_ready"), 1)
            def w_high(i, stage, c):
                if c == 0:
                    act.wait_ge(S(f"w_ff{1 + stage // 2}_loaded{stage % 2}"), (i + 1) * 16)
                nc.scalar.activation(ff_high(stage, c), ff_low(stage, c, F32), ACT.Copy).then_inc(S("w_high"), 1)

            for t in range(REAL):
                act.wait_ge(S("h_mixed2"), t + 1)
                link(nc.scalar.activation(nat2[:, t, :], h[:, t, :], ACT.Square, accum_out=stat[:, 28 + t:29 + t]))
                nc.scalar.activation(stat[:, 30 + t:31 + t], stat[:, 28 + t:29 + t], ACT.Sqrt, scale=1.0 / D,
                                     bias=epsc[:, :]).then_inc(S("rms_ready"), 1)

            act.wait_ge(S("mix2_made"), REAL)
            for c in range(FF_GROUP):
                w_high(0, 0, c)
            for j in range(4):
                act.wait_ge(S("uF_ready"), j + 1)
                k0, cs = 4 * (j % 2), slice(j // 2 * P, j // 2 * P + P)
                nc.scalar.activation(uFh[:, k0:k0 + 4, cs], uF[:, k0:k0 + 4, cs], ACT.Copy)\
                    .then_inc(S("uF_high"), 1)

            def f1_high(i, e):
                act.wait_ge(S("f1_squared"), i * 2 * FF_GROUP + e + 1)
                s, c = divmod(e, FF_GROUP)
                nc.scalar.activation(f1h[:, s, c, :], f1[:, s, c, :], ACT.Copy).then_inc(S("f1_high"), 1)

            def hidden_pair(i, first, last):
                for stage in range(FF_STAGES):
                    for c in range(FF_GROUP):
                        if not (last and stage == FF_STAGES - 1):
                            w_high(i + (stage + 1) // FF_STAGES, (stage + 1) % FF_STAGES, c)
                        e = stage * FF_GROUP + c
                        if stage < 2:
                            if c == 0 and not first:
                                act.wait_ge(S("f2_group"), i * 2 + stage - 1)
                            act.wait_ge(S("f1_made"), i * 2 * FF_GROUP + e + 1)
                            nc.scalar.activation(f1[:, stage, c, :], ps(c)[:, 0:SEQ], ACT.Relu).then_inc(S("relu_made"), 1)
                        if 1 <= e <= 2 * FF_GROUP:
                            f1_high(i, e - 1)

            hidden_pair(0, True, False)
            with act.Fori(1, FF_PAIRS - 1) as i:
                hidden_pair(i, False, False)
            hidden_pair(FF_PAIRS - 1, False, True)
            for t in range(REAL):
                act.wait_ge(S("f2_group"), FF_GROUPS)
                link(nc.scalar.activation(nat2[:, t, :], pairs[t][:, :], ACT.Square, accum_out=stat[:, 32 + t:33 + t]))
                nc.scalar.activation(stat[:, 34 + t:35 + t], stat[:, 32 + t:33 + t], ACT.Sqrt, scale=1.0 / D,
                                     bias=epsc[:, :]).then_inc(S("rms_ready"), 1)

        @block.vector
        def _(dve):
            linked = [0]

            def link(ins):
                linked[0] += 1
                ins.then_inc(S("vector_step"), 1)
                dve.wait_ge(S("vector_step"), linked[0])

            nc.vector.memset(epsc[:, :], EPS).then_inc(S("eps_ready"), 1)
            for t in range(3):
                n = ROWS[t]
                src = h[:, t, :] if t < 2 else hM[0:META, :]
                dve.wait_ge(S("rms_ready"), RMS_N1 + t + 1)
                link(nc.vector.reciprocal(stat[0:n, 3 + t:4 + t], stat[0:n, 3 + t:4 + t]))
                nc.vector.tensor_scalar(nat[0:n, t, :], src, stat[0:n, 3 + t:4 + t], None, ALU.mult).then_inc(S("n1_ready"), 1)
            dve.wait_ge(S("col_loaded"), 16)

            def gained(turned, j, n, dst, gain):
                dve.wait_ge(S(turned), j + 1)
                return nc.vector.tensor_tensor(dst, ps(j)[:, :].rearrange("p (a b) -> p a b", a=4)[:, :, 0:n],
                                               gain.unsqueeze(2).to_broadcast([P, 4, n]), ALU.mult)

            for j in range(6):
                t, k0, n = j // 2, 4 * (j % 2), ROWS[j // 2]
                gained("n1_turned", j, n, hnT[:, k0:k0 + 4, COL0[t]:COL0[t] + n],
                       col[:, C_NORM1 + k0:C_NORM1 + k0 + 4]).then_inc(S("hnT_ready"), 1)
            for job in PJ:
                name = job[0]
                n, e, k = EV[name]
                if e != "v":
                    continue
                kind, i = name
                b = ps(n % 8)
                dve.wait_ge(S("proj_made"), n + 1)
                if kind == "gq":
                    ins = nc.vector.tensor_scalar(gqT[:, i, :], b[:, 0:SEQ], DK ** -0.5, None, ALU.mult)
                elif kind == "gk":
                    ins = nc.vector.tensor_copy(gkT[:, i, :], b[:, 0:TOK])
                elif kind == "glr":
                    ins = nc.vector.tensor_copy(glrT[0:RANK, :], b[0:RANK, 0:TOK])
                else:
                    r = ROWS[i]
                    ins = nc.vector.tensor_copy(sbv[0:r, i, :], b[0:r, :])
                ins.then_inc(S("evac_v"), 1)
            dve.wait_ge(S("lg_made"), 1)
            for c in range(2):
                nc.vector.tensor_scalar(nb[:, c, :], ps(c)[:, 0:TOK], col[:, C_BG + c:C_BG + c + 1], 0.0, ALU.add, ALU.min)\
                    .then_inc(S("lg_min"), 1)
            dve.wait_ge(S("lg_min"), 2)
            dve.wait_ge(S("lg_ln"), 1)
            link(nc.vector.tensor_tensor(lgt[:, :, :], lgt[:, :, :], nb[:, :, :], ALU.subtract))
            for c in range(2):
                for t in range(3):
                    seg = slice(COL0[t], COL0[t] + ROWS[t])
                    link(nc.vector.tensor_tensor_scan(nb[:, c, seg], lgt[:, c, seg], lgt[:, c, seg], 0.0, ALU.add, ALU.max))
            nc.vector.tensor_scalar(pb[:, :, :], nb[:, :, :], -1.0 / TAU, None, ALU.mult).then_inc(S("decay_ready"), 1)
            nc.vector.tensor_scalar(nb[:, :, :], nb[:, :, :], 1.0 / TAU, None, ALU.mult).then_inc(S("decay_ready"), 1)
            for i in range(SB_HEADS):
                dve.wait_ge(S("z_ln"), i + 1)
                if i >= 2:
                    dve.wait_ge(S("s_made"), i - 1)
                nc.vector.scalar_tensor_tensor(out=sp[:, i % 2, :], in0=pairs[i % 2][:, 0:640], scalar=0.0,
                                               in1=tmp[:, i % 2, :], op0=ALU.max, op1=ALU.add).then_inc(S("sp_made"), 1)

            def state_from(c, n, upd):
                dve.wait_ge(S("klT_made"), upd + 1)
                nc.vector.tensor_copy(klnat[0:n, c, :], ps(6)[0:n, 0:P]).then_inc(S("klnat_ready"), 1)
                dve.wait_ge(S("st_prod"), upd + 1)
                if upd >= 2:
                    dve.wait_ge(S("o_made"), 2 * c + 2)
                for hp in range(2):
                    rows_ = slice(64 * hp, 64 * hp + 64)
                    new = ps(7)[rows_, hp * DV:(hp + 1) * DV]
                    if upd < 2:
                        ins = nc.vector.tensor_copy(state[rows_, c, :], new)
                    else:
                        ins = nc.vector.scalar_tensor_tensor(out=state[rows_, c, :], in0=state[rows_, c, :],
                                                             scalar=stat[rows_, 42 + c:43 + c], in1=new,
                                                             op0=ALU.mult, op1=ALU.add)
                ins.then_inc(S("state_ready"), 1)

            for c in range(2):
                dve.wait_ge(S("gex_made"), c + 1)
                nc.vector.tensor_tensor(gex[:, c, 1200:1216], gex[:, c, 1200:1216], gkT[:, c, 0:META], ALU.mult)\
                    .then_inc(S("klM_ready"), 1)
            for c in range(2):
                state_from(c, META, c)
            dve.wait_ge(S("kz_cleared"), 1)
            for u in range(4):
                t, c = divmod(u, 2)
                g = gex[:, u % 2, :]
                dve.wait_ge(S("gex_made"), 3 + u)
                a = 0
                for j in range(NSUB):
                    n = P - SUB * j
                    q0 = t * P + SUB * j
                    nc.vector.tensor_tensor(g[:, a:a + n], g[:, a:a + n], gqT[:, c, q0:q0 + n], ALU.mult)
                    a += n
                    k0 = COL0[t] + SUB * j
                    nc.vector.tensor_tensor(kzpad[:, u % 2, j, SUB * j:SUB * j + SUB], g[:, 320 + SUB * j:352 + SUB * j],
                                            gkT[:, c, k0:k0 + SUB], ALU.mult)
                nc.vector.tensor_tensor(g[:, 448:576], g[:, 448:576], gqT[:, c, t * P:t * P + P], ALU.mult)
                nc.vector.tensor_tensor(g[:, 576:704], g[:, 576:704], gkT[:, c, COL0[t]:COL0[t] + P], ALU.mult)\
                    .then_inc(S("gla_f"), 1)
                for hp in range(2):
                    v = 2 * u + hp
                    dve.wait_ge(S("att_made"), v + 1)
                    if v >= 2:
                        dve.wait_ge(S("o_made"), v - 1)
                    nc.vector.tensor_tensor(attT[:, v % 2, :], ps(4 + v % 2)[:, 0:P], causal[:, :], ALU.mult)\
                        .then_inc(S("attT_ready"), 1)
                if t == 0:
                    state_from(c, P, 2 + c)

            dve.wait_ge(S("row_loaded"), 16)
            dve.wait_ge(S("silu_made"), 2)
            dve.wait_ge(S("o_made"), 8)
            dve.wait_ge(S("pv_made"), SB_HEADS)
            for t in range(REAL):
                for part, (nh, dh, bnk, g0, s0) in enumerate(((SB_HEADS, SB_DIM, 2 + t, R_SB, 8), (GLA_HEADS, DV, t, R_GLA, 24))):
                    m = mixn[:, t, 512 * part:512 * part + 512]
                    mh = m.rearrange("p (a b) -> p a b", a=nh)
                    r0 = s0 + (8 if part == 0 else 4)
                    link(nc.vector.tensor_copy(m, ps(bnk)))
                    link(nc.vector.tensor_tensor(sqr, m, m, ALU.mult))
                    nc.vector.tensor_reduce(stat[:, s0:s0 + nh], sqr.rearrange("p (a b) -> p a b", a=nh), AX, ALU.add)\
                        .then_inc(S("ss_made"), 1)
                    dve.wait_ge(S("hrms_made"), 2 * t + part + 1)
                    link(nc.vector.reciprocal(stat[:, r0:r0 + nh], stat[:, r0:r0 + nh]))
                    link(nc.vector.tensor_tensor(mh, mh, stat[:, r0:r0 + nh].unsqueeze(2).to_broadcast([P, nh, dh]), ALU.mult))
                    if part == 0:
                        nc.vector.tensor_tensor(m, m, row[:, g0:g0 + 512], ALU.mult).then_inc(S("mixn_ready"), 1)
                    else:
                        link(nc.vector.tensor_tensor(m, m, row[:, g0:g0 + 512], ALU.mult))
                        nc.vector.tensor_tensor(m, m, gr[:, t, :], ALU.mult).then_inc(S("mixn_ready"), 1)
            for j in (0, 2):
                dve.wait_ge(S("mix_turned"), j + 1)
                nc.vector.tensor_copy(mixT[:, 0:4, (j // 2) * P:(j // 2) * P + P],
                                      ps(4 + j).rearrange("p (a b) -> p a b", a=4)).then_inc(S("mixT_v"), 1)
            for t in range(REAL):
                dve.wait_ge(S("mix_made"), t + 1)
                nc.vector.tensor_tensor(h[:, t, 0:512], h[:, t, 0:512], ps(2 * t), ALU.add)
                nc.vector.tensor_tensor(h[:, t, 512:D], h[:, t, 512:D], ps(2 * t + 1), ALU.add).then_inc(S("h_mixed"), 1)
            for t in range(REAL):
                dve.wait_ge(S("rms_ready"), RMS_N2 + t + 1)
                link(nc.vector.reciprocal(stat[:, 34 + t:35 + t], stat[:, 34 + t:35 + t]))
                nc.vector.scalar_tensor_tensor(out=hn2[:, t, :], in0=h[:, t, :], scalar=stat[:, 34 + t:35 + t],
                                               in1=row[:, R_NORM2:R_NORM2 + D], op0=ALU.mult, op1=ALU.mult)\
                    .then_inc(S("hn2_ready"), 1)
            for j in range(4):
                dve.wait_ge(S("n2_turned"), j + 1)
                nc.vector.tensor_copy(hn2T[:, 4 * (j % 2):4 * (j % 2) + 4, (j // 2) * P:(j // 2) * P + P],
                                      ps(4 + j).rearrange("p (a b) -> p a b", a=4)).then_inc(S("hn2T_ready"), 1)
            dve.wait_ge(S("n2_turned"), 4)
            nc.vector.memset(score[:, UNITS, :], 0.0).then_inc(S("score_end_set"), 1)

            dve.wait_ge(S("iota_ready"), 1)

            def route(u, p):
                step = [0]

                def done(ins):
                    step[0] += 1
                    ins.then_inc(S("route_step"), 1)
                    dve.wait_ge(S("route_step"), u * ROUTE_STEPS + step[0])

                def tick(ins):
                    step[0] += 1
                    ins.then_inc(S("route_step"), 1)

                dve.wait_ge(S("cur_ready"), u + 1)
                dve.sem_inc(S("route_turn"), 1)

                def rests():
                    dve.wait_ge(S("route_step"), u * ROUTE_STEPS + step[0])
                    dve.sem_inc(S("route_turn"), 1)

                def best16(vals, vi, idx, rest):
                    for x, v, i, r in zip(vals, vi, idx, rest):
                        tick(nc.vector.max(v[:, 0:8], x))
                    rests()
                    for x, v, i, r in zip(vals, vi, idx, rest):
                        nc.vector.max_index(i[:, 0:8], v[:, 0:8], x)
                        tick(nc.vector.match_replace(r, v[:, 0:8], x, -3.0e38))
                    rests()
                    for x, v, i, r in zip(vals, vi, idx, rest):
                        tick(nc.vector.max(v[:, 8:16], r))
                    rests()
                    for x, v, i, r in zip(vals, vi, idx, rest):
                        tick(nc.vector.max_index(i[:, 8:16], v[:, 8:16], r))
                    rests()

                side = [cur[:, p, 0:NKEYS], cur[:, p, NKEYS:2 * NKEYS]]
                best16(side, [v16[:, 0:16], v16[:, 16:32]], [i16[:, 0:16], i16[:, 16:32]],
                       [cur2[:, 0:NKEYS], cur2[:, NKEYS:2 * NKEYS]])
                ins = nc.vector.tensor_tensor(cand.rearrange("p (a b) -> p a b", a=TOPK),
                                              v16[:, 0:16].unsqueeze(2).to_broadcast([P, TOPK, TOPK]),
                                              v16[:, 16:32].unsqueeze(1).to_broadcast([P, TOPK, TOPK]), ALU.add)
                ins.then_inc(S("cur_used"), 1)
                dve.wait_ge(S("cur_used"), u + 1)
                dve.sem_inc(S("route_turn"), 1)
                best16([cand], [sc16], [pos], [pick[:, 0:256]])
                tick(nc.vector.tensor_scalar(nmx, sc16[:, 0:1], -1.0, None, ALU.mult))
                tick(nc.vector.tensor_scalar(posij[:, 0:16], pos, 4, None, ALU.logical_shift_right))
                tick(nc.vector.tensor_scalar(posij[:, 16:32], pos, 15, None, ALU.bitwise_and))
                nc.vector.tensor_copy(if16, i16).then_inc(S("sc_ready"), 1)
                dve.wait_ge(S("route_step"), u * ROUTE_STEPS + step[0])
                done(nc.vector.tensor_copy(posf, posij))
                pk = pick.rearrange("p (s k i) -> p s k i", s=2, k=TOPK)
                done(nc.vector.tensor_tensor(
                    pk, iota16.unsqueeze(1).unsqueeze(1).to_broadcast([P, 2, TOPK, TOPK]),
                    posf.rearrange("p (s k) -> p s k", s=2).unsqueeze(3).to_broadcast([P, 2, TOPK, TOPK]), ALU.is_equal))
                done(nc.vector.tensor_tensor(
                    pk, pk, if16.rearrange("p (s i) -> p s i", s=2).unsqueeze(2).to_broadcast([P, 2, TOPK, TOPK]), ALU.mult))
                done(nc.vector.tensor_reduce(eij.rearrange("p (s k) -> p s k", s=2), pk, AX, ALU.add))
                nc.vector.scalar_tensor_tensor(out=uidx[:, p, :], in0=eij[:, 0:16], scalar=float(NKEYS),
                                               in1=eij[:, 16:32], op0=ALU.mult, op1=ALU.add).then_inc(S("uidx_ready"), 1)
                assert step[0] == ROUTE_STEPS, step[0]

            def keep_idx(u, p):
                dve.wait_ge(S("uidx_ready"), u + 1)
                nc.vector.tensor_copy(vidx[:, p, :], uidx[:, p, :]).then_inc(S("vidx_ready"), 1)

            def gates(u, p):
                dve.wait_ge(S("gex16_ready"), u + 1)
                nc.vector.reciprocal(rden, den).then_inc(S("rden_ready"), 1)
                dve.wait_ge(S("rden_ready"), u + 1)
                nc.vector.tensor_scalar(gate[:, p, :], ex16, rden, None, ALU.mult).then_inc(S("gate_ready"), 1)

            def unit_dots(u, p, turn_, tile, ks):
                for k in ks:
                    s = k % RING
                    dve.wait_ge(S(f"u_row{s}"), (turn_ + k // RING + 1) * 16)
                    nc.vector.scalar_tensor_tensor(
                        out=uring[s], in0=uring[s], scalar=1.0, in1=hn2[:, tile, :],
                        op0=ALU.mult, op1=ALU.mult, accum_out=dots[:, p, k:k + 1]).then_inc(S("u_used"), 1)

            def unit_weights(u, p):
                dve.wait_ge(S("gate_ready"), u + 1)
                dve.wait_ge(S("gelu_ready"), u + 1)
                nc.vector.tensor_tensor(gw[:, p, :], gate[:, p, :], ggel[:, p, :], ALU.mult).then_inc(S("gw_ready"), 1)

            def experts_pass(b, tile, next_tile, last):
                for p in range(2):
                    u = b * 2 + p
                    ahead = not (last and p == 1)
                    if ahead:
                        keep_idx(u + 1, 1 - p)
                        if not last:
                            route(u + 2, p)
                        of = tile if p == 0 else next_tile
                        unit_dots(u + 1, 1 - p, b * 4 + 2 * p + 2, of, range(4))
                        if not last:
                            gates(u + 2, p)
                        unit_dots(u + 1, 1 - p, b * 4 + 2 * p + 2, of, range(4, TOPK))
                        unit_weights(u + 1, 1 - p)
                    dve.wait_ge(S("v_used"), u * TOPK + V_PRIME + TOPK)
                    nc.vector.tensor_tensor(h[:, tile, :], h[:, tile, :], pairs[p][:, :], ALU.add).then_inc(S("y_added"), 1)
                    dve.wait_ge(S("y_added"), u + 3)

            route(0, 0)
            keep_idx(0, 0)
            gates(0, 0)
            route(1, 1)
            unit_dots(0, 0, 0, 0, range(4))
            gates(1, 1)
            unit_dots(0, 0, 0, 0, range(4, TOPK))
            unit_weights(0, 0)
            per = PASSES // REAL
            for t in range(REAL):
                with dve.Fori(t * per, (t + 1) * per - 1) as b:
                    experts_pass(b, t, t, False)
                experts_pass((t + 1) * per - 1, t, t + 1, t == REAL - 1)

            link(nc.vector.memset(v2[:, :, :, :], 0.0))
            link(nc.vector.memset(xr[:, :, 0:CONV - 1], 0.0))
            for t in range(REAL):
                dve.wait_ge(S("rms_ready"), RMS_NF + t + 1)
                link(nc.vector.reciprocal(stat[:, 2 + t:3 + t], stat[:, 2 + t:3 + t]))
                nc.vector.scalar_tensor_tensor(out=h[:, t, :], in0=h[:, t, :], scalar=stat[:, 2 + t:3 + t],
                                               in1=row[:, R_NORMF:R_NORMF + D], op0=ALU.mult, op1=ALU.mult)\
                    .then_inc(S("hf_ready"), 1)
            for t in range(3):
                n = ROWS[t]
                dve.wait_ge(S("rms_ready"), RMS_N3 + t + 1)
                link(nc.vector.reciprocal(stat[0:n, 7 + t:8 + t], stat[0:n, 7 + t:8 + t]))
                src = h[:, t, :] if t < 2 else hM2[0:META, :]
                nc.vector.tensor_scalar(nat2[0:n, t, :], src, stat[0:n, 7 + t:8 + t], None, ALU.mult).then_inc(S("n3_ready"), 1)
            for j in range(6):
                t, k0, n = j // 2, 4 * (j % 2), ROWS[j // 2]
                gained("n3_turned", j, n, uT[:, k0:k0 + 4, COL0[t]:COL0[t] + n],
                       col[:, C_PREMIX + k0:C_PREMIX + k0 + 4]).then_inc(S("uT_ready"), 1)
            for job in PJ2:
                n, e, k = EV2[job[0]]
                if e != "v":
                    continue
                kind, i = job[0]
                dve.wait_ge(S("proj2_made"), n + 1)
                b = ps(n % 8)
                if kind == "xr":
                    ins = nc.vector.tensor_copy(xr[:, i, CONV - 1:], b[:, 0:TOK])
                elif kind == "k":
                    ins = nc.vector.tensor_copy(k2T, b[:, 0:TOK])
                else:
                    r = ROWS[i]
                    for kv in range(KVH):
                        ins = nc.vector.tensor_copy(v2[0:r, i, kv, 64 * kv:64 * kv + 64], b[0:r, 64 * kv:64 * kv + 64])
                ins.then_inc(S("evac2_v"), 1)
            dve.wait_ge(S("evac2_v"), 4)
            for c in range(4):
                w = col[:, C_CONVW + 4 * c:C_CONVW + 4 * c + 4]
                nc.vector.tensor_scalar(xc[:, c, :], xr[:, c, 3:3 + TOK], w[:, 3:4], col[:, C_CONVB + c:C_CONVB + c + 1],
                                        ALU.mult, ALU.add).then_inc(S("conv_step"), 1)
                for k in (2, 1, 0):
                    dve.wait_ge(S("conv_step"), 4 * c + 3 - k)
                    ins = nc.vector.scalar_tensor_tensor(out=xc[:, c, :], in0=xr[:, c, k:k + TOK], scalar=w[:, k:k + 1],
                                                         in1=xc[:, c, :], op0=ALU.mult, op1=ALU.add)
                    ins.then_inc(S("conv_step"), 1)
            link(nc.vector.tensor_scalar(stat[:, 60:64], col[:, C_LAM:C_LAM + 4], 0.0, None, ALU.min))
            dve.wait_ge(S("lam_ln"), 1)
            link(nc.vector.tensor_tensor(stat[:, 48:52], stat[:, 48:52], stat[:, 60:64], ALU.subtract))
            nc.vector.tensor_scalar(stat[:, 52:56], stat[:, 48:52], LRU_C, None, ALU.mult).then_inc(S("lam_ready"), 1)
            nc.vector.tensor_scalar(stat[:, 56:60], stat[:, 48:52], -LRU_C, None, ALU.mult).then_inc(S("lam_ready"), 1)
            dve.wait_ge(S("a_made"), 4)
            link(nc.vector.tensor_tensor(lt[:, :, :], lr[:, :, :], lr[:, :, :], ALU.mult))
            nc.vector.scalar_tensor_tensor(out=lm[:, :, :], in0=lt[:, :, :], scalar=1.0, in1=lm[:, :, :], op0=ALU.add, op1=ALU.mult)\
                .then_inc(S("m2_made"), 1)
            link(nc.vector.tensor_tensor(li[:, :, :], li[:, :, :], xc[:, :, :], ALU.mult))
            dve.wait_ge(S("root_made"), 1)
            link(nc.vector.tensor_tensor(li[:, :, :], li[:, :, :], lm[:, :, :], ALU.mult))
            for c in range(4):
                link(nc.vector.tensor_tensor_scan(lt[:, c, :], lr[:, c, :], li[:, c, :], 0.0, ALU.mult, ALU.add))
            dve.wait_ge(S("evac2_a"), 4)
            nc.vector.tensor_tensor(mixT2[:, 4:8, :], lt[:, :, META:TOK], geluy[:, :, :], ALU.mult).then_inc(S("rec_ready"), 1)
            dve.wait_ge(S("mask2_ready"), 4)
            for u in range(4):
                t, hf_ = divmod(u, 2)
                nk = META + P if t == 0 else SEQ
                dve.wait_ge(S("s2_made"), u + 1)
                if u >= 1:
                    dve.wait_ge(S("p_turned"), u)
                for half in range(2):
                    nc.vector.tensor_tensor(S2[:, half:4:2, 0:nk],
                                            ps(half).rearrange("p (a b) -> p a b", a=2)[:, :, 0:nk],
                                            mask2[:, t, 0:nk].unsqueeze(1).to_broadcast([P, 2, nk]), ALU.add)\
                        .then_inc(S("s2_masked"), 1)
                dve.wait_ge(S("s2_masked"), 2 * u + 2)
                nc.vector.tensor_reduce(stat[:, 8:12], S2[:, :, 0:nk], AX, ALU.max).then_inc(S("m_step"), 1)
                dve.wait_ge(S("m_step"), 5 * u + 1)
                sink = row[:, R_SINK + 4 * hf_:R_SINK + 4 * hf_ + 4]
                nc.vector.tensor_tensor(stat[:, 8:12], stat[:, 8:12], sink, ALU.max).then_inc(S("m_step"), 1)
                dve.wait_ge(S("m_step"), 5 * u + 2)
                nc.vector.tensor_tensor(stat[:, 20:24], sink, stat[:, 8:12], ALU.subtract)
                nc.vector.tensor_scalar(stat[:, 12:16], stat[:, 8:12], -1.0, None, ALU.mult).then_inc(S("nm_made"), 1)
                dve.wait_ge(S("p_made"), u + 1)
                nc.vector.tensor_tensor(stat[:, 16:20], stat[:, 16:20], stat[:, 20:24], ALU.add).then_inc(S("m_step"), 1)
                dve.wait_ge(S("m_step"), 5 * u + 3)
                nc.vector.reciprocal(stat[:, 16:20], stat[:, 16:20]).then_inc(S("m_step"), 1)
                dve.wait_ge(S("m_step"), 5 * u + 4)
                nc.vector.tensor_tensor(S2[:, :, 0:nk], S2[:, :, 0:nk],
                                        stat[:, 16:20].unsqueeze(2).to_broadcast([P, 4, nk]), ALU.mult)\
                    .then_inc(S("m_step"), 1)
                dve.wait_ge(S("p_turned"), u + 1)
                if u >= 1:
                    dve.wait_ge(S("o2_made"), u)
                for half in range(2):
                    src = ps(2 + half).rearrange("p (a k b) -> p a k b", a=2, k=2)
                    if t == 0:
                        nc.vector.tensor_copy(pT[0:META, 2 * half:2 * half + 2, 0, :], src[0:META, :, 0, :])
                        ins = nc.vector.tensor_copy(pT[:, 2 * half:2 * half + 2, 1, :], src[:, :, 1, :])
                    else:
                        ins = nc.vector.tensor_copy(pT[:, 2 * half:2 * half + 2, :, :], src)
                ins.then_inc(S("pT_ready"), 1)
                dve.wait_ge(S("o2_made"), u + 1)
                nc.vector.tensor_copy(mixT2[:, 2 * hf_:2 * hf_ + 2, t * P:t * P + P],
                                      ps(4).rearrange("p (a b) -> p a b", a=4)[:, 0:2, :]).then_inc(S("o2_ready"), 1)
            for t in range(REAL):
                dve.wait_ge(S("rms_ready"), RMS_PM + t + 1)
                link(nc.vector.reciprocal(stat[:, 26 + t:27 + t], stat[:, 26 + t:27 + t]))
                link(nc.vector.scalar_tensor_tensor(out=nat2[:, t, :], in0=pairs[t][:, :], scalar=stat[:, 26 + t:27 + t],
                                               in1=row[:, R_POSTMIX:R_POSTMIX + D], op0=ALU.mult, op1=ALU.mult))
                nc.vector.tensor_tensor(h[:, t, :], h[:, t, :], nat2[:, t, :], ALU.add).then_inc(S("h_mixed2"), 1)
            for t in range(REAL):
                dve.wait_ge(S("rms_ready"), RMS_N4 + t + 1)
                link(nc.vector.reciprocal(stat[:, 30 + t:31 + t], stat[:, 30 + t:31 + t]))
                nc.vector.tensor_scalar(nat2[:, t, :], h[:, t, :], stat[:, 30 + t:31 + t], None, ALU.mult).then_inc(S("n4_ready"), 1)
            def w_low(i, stage, c):
                dve.wait_ge(S("w_high"), (i * FF_STAGES + stage) * FF_GROUP + c + 1)
                nc.vector.tensor_tensor(ff_low(stage, c), ff_low(stage, c, F32), ff_high(stage, c), ALU.subtract).then_inc(S("w_split"), 1)

            for j in range(4):
                t, k0 = j // 2, 4 * (j % 2)
                gained("n4_turned", j, P, uF[:, k0:k0 + 4, t * P:t * P + P],
                       col[:, C_PREFFN + k0:C_PREFFN + k0 + 4]).then_inc(S("uF_ready"), 1)
            w_low(0, 0, 0)
            for j in range(4):
                dve.wait_ge(S("uF_high"), j + 1)
                k0, cs = 4 * (j % 2), slice(j // 2 * P, j // 2 * P + P)
                nc.vector.tensor_tensor(uFl[:, k0:k0 + 4, cs], uF[:, k0:k0 + 4, cs], uFh[:, k0:k0 + 4, cs],
                                        ALU.subtract).then_inc(S("uF_split"), 1)
            for c in range(1, FF_GROUP):
                w_low(0, 0, c)

            def f1_low(i, e):
                dve.wait_ge(S("f1_high"), i * 2 * FF_GROUP + e + 1)
                s, c = divmod(e, FF_GROUP)
                nc.vector.tensor_tensor(f1l[:, s, c, :], f1[:, s, c, :], f1h[:, s, c, :], ALU.subtract)\
                    .then_inc(S("f1_ready"), 1)

            def square_pair(i, last):
                for stage in range(FF_STAGES):
                    for c in range(FF_GROUP):
                        if not (last and stage == FF_STAGES - 1):
                            w_low(i + (stage + 1) // FF_STAGES, (stage + 1) % FF_STAGES, c)
                        e = stage * FF_GROUP + c
                        if stage < 2:
                            dve.wait_ge(S("relu_made"), i * 2 * FF_GROUP + e + 1)
                            nc.vector.tensor_tensor(f1[:, stage, c, :], f1[:, stage, c, :], f1[:, stage, c, :], ALU.mult)\
                                .then_inc(S("f1_squared"), 1)
                        if 1 <= e <= 2 * FF_GROUP:
                            f1_low(i, e - 1)

            with dve.Fori(0, FF_PAIRS - 1) as i:
                square_pair(i, False)
            square_pair(FF_PAIRS - 1, True)
            for t in range(REAL):
                dve.wait_ge(S("rms_ready"), RMS_PF + t + 1)
                link(nc.vector.reciprocal(stat[:, 34 + t:35 + t], stat[:, 34 + t:35 + t]))
                link(nc.vector.scalar_tensor_tensor(out=nat2[:, t, :], in0=pairs[t][:, :], scalar=stat[:, 34 + t:35 + t],
                                               in1=row[:, R_POSTFFN:R_POSTFFN + D], op0=ALU.mult, op1=ALU.mult))
                nc.vector.tensor_tensor(h[:, t, :], h[:, t, :], nat2[:, t, :], ALU.add).then_inc(S("out_ready"), 1)

        @block.tensor
        def _(pe):
            pe.sem_inc(S("v_used"), V_PRIME)
            pe.sem_inc(S("u_used"), RING)
            pe.sem_inc(S("y_added"), 2)

            def turn(src, n, j, b, made):
                for k in range(4):
                    c = 4 * (j % 2) + k
                    ins = nc.tensor.transpose(ps(b)[:, k * P:k * P + n], src[:, c * P:c * P + P], ident[0:n, 0:n])
                ins.then_inc(S(made), 1)

            pe.wait_ge(S("masks_ready"), 4)
            for j in range(6):
                t, n = j // 2, ROWS[j // 2]
                pe.wait_ge(S("n1_ready"), t + 1)
                turn(nat[0:n, t, :], n, j, j, "n1_turned")
            pe.wait_ge(S("hnT_ready"), 6)
            seen = set()
            for job in PJ:
                name, kind, bi, c0, t0, n = job
                nj = EV[name][0]
                if bi not in seen:
                    seen.add(bi)
                    pe.wait_ge(S(f"w_in_loaded{bi}"), 16)
                if nj >= 8:
                    _, e, k = EV[PJ[nj - 8][0]]
                    pe.wait_ge(S(f"evac_{e}"), k)
                b = ps(nj % 8)
                for k in range(KD):
                    if kind == "T":
                        w = wlast[:, k, :] if bi == 6 else w_slice(bi, c0, P)[:, k, :]
                        m = RANK if bi == 6 else P
                        ins = nc.tensor.matmul(b[0:m, 0:n], w, hnT[:, k, t0:t0 + n], start=(k == 0), stop=(k == KD - 1))
                    else:
                        ins = nc.tensor.matmul(b[0:n, :], hnT[:, k, t0:t0 + n], w_slice(bi, 0, W_COLS)[:, k, :],
                                               start=(k == 0), stop=(k == KD - 1))
                ins.then_inc(S("proj_made"), 1)
            pe.wait_ge(S("gate_loaded"), 16)
            pe.wait_ge(S("evac_v"), max(k for _, e, k in EV.values() if e == "v"))
            pe.wait_ge(S("evac_a"), max(k for _, e, k in EV.values() if e == "a"))
            for c in range(2):
                ins = nc.tensor.matmul(ps(c)[:, 0:TOK], wgate[:, c * P:c * P + P], glrT[0:RANK, :], start=True, stop=True)
            ins.then_inc(S("lg_made"), 1)

            def mm(o, a, b, start, stop):
                return nc.tensor.matmul(o, a, b, start=start, stop=stop, skip_group_check=True)

            def sb_scores(i):
                c, r = i // 2, slice(64 * (i % 2), 64 * (i % 2) + 64)
                z = pairs[i % 2]
                if i >= 2:
                    pe.wait_ge(S("aT_made"), i - 1)
                mm(z[:, 0:256], sbkT[r, c, META:META + P], sbqT[r, c, :], True, False)
                mm(z[:, 256:512], sbkT[r, c, 0:P], sbqT[r, c, :], False, False)
                mm(z[:, 512:640], sbkT[r, c, META + P:TOK], sbqT[r, c, P:SEQ], True, False).then_inc(S("z_made"), 1)

            def sb_sums(i):
                z = pairs[i % 2]
                s = sp[:, i % 2, :]
                pe.wait_ge(S("sp_masked"), i + 1)
                mm(z[:, 0:256], ntri[:, :], s[:, 0:256], False, False)
                mm(z[:, 128:256], neg1[:, :], s[:, 512:640], False, True)
                mm(z[0:META, 256:512], ntri[0:META, 0:META], s[0:META, 256:512], False, False)
                mm(z[0:META, 256:512], neg1[:, 0:META], s[:, 0:256], False, False)
                mm(z[0:META, 384:512], neg1[:, 0:META], s[:, 512:640], False, True)
                mm(z[:, 512:640], ntri[:, :], s[:, 512:640], False, True).then_inc(S("s_made"), 1)

            def sb_values(i):
                a = aT[:, i % 2, :]
                cs = slice(64 * i, 64 * i + 64)
                pe.wait_ge(S("aT_masked"), i + 1)
                mm(ps(2)[:, cs], a[0:META, 256:384], sbv[0:META, 2, cs], True, False)
                mm(ps(2)[:, cs], a[:, 0:P], sbv[:, 0, cs], False, True)
                mm(ps(3)[:, cs], a[0:META, 384:512], sbv[0:META, 2, cs], True, False)
                mm(ps(3)[:, cs], a[:, P:SEQ], sbv[:, 0, cs], False, False)
                mm(ps(3)[:, cs], a[:, 512:640], sbv[:, 1, cs], False, True).then_inc(S("pv_made"), 1)

            for i in range(SB_HEADS + 2):
                if i < SB_HEADS:
                    sb_scores(i)
                if 1 <= i <= SB_HEADS:
                    sb_sums(i - 1)
                if i >= 2:
                    sb_values(i - 2)

            def state_product(c, n, kl, v, upd):
                if upd >= 1:
                    pe.wait_ge(S("state_ready"), upd)
                nc.tensor.transpose(ps(6)[0:n, 0:P], kl, ident[:, :]).then_inc(S("klT_made"), 1)
                pe.wait_ge(S("klnat_ready"), upd + 1)
                mm(ps(7)[:, 0:256], klnat[0:n, c, :], v, True, True).then_inc(S("st_prod"), 1)

            for c in range(2):
                pe.wait_ge(S("klM_ready"), c + 1)
                state_product(c, META, gex[:, c, 1200:1216], gv[0:META, 2, 256 * c:256 * c + 256], c)
            for u in range(4):
                t, c = divmod(u, 2)
                g = gex[:, u % 2, :]
                pe.wait_ge(S("gla_f"), u + 1)
                for hp in range(2):
                    v, r = 2 * u + hp, slice(64 * hp, 64 * hp + 64)
                    if v >= 2:
                        pe.wait_ge(S("attT_ready"), v - 1)
                    a = 0
                    for j in range(NSUB):
                        n = P - SUB * j
                        ins = mm(ps(4 + v % 2)[:, SUB * j:P], kzpad[r, u % 2, j, :], g[r, a:a + n], j == 0, j == NSUB - 1)
                        a += n
                    ins.then_inc(S("att_made"), 1)
                pe.wait_ge(S("state_ready"), 2 * t + c + 1)
                for hp in range(2):
                    v, r, hd = 2 * u + hp, slice(64 * hp, 64 * hp + 64), 2 * c + hp
                    o = ps(t)[:, hd * DV:hd * DV + DV]
                    if v >= 1:
                        pe.wait_ge(S("o_made"), v)
                    mm(o, g[r, 448:576], state[r, c, :], True, False)
                    pe.wait_ge(S("attT_ready"), v + 1)
                    mm(o, attT[:, v % 2, :], gv[:, t, hd * DV:hd * DV + DV], False, True).then_inc(S("o_made"), 1)
                if t == 0:
                    pe.wait_ge(S("o_made"), 2 * u + 2)
                    state_product(c, P, g[:, 576:704], gv[:, 0, 256 * c:256 * c + 256], 2 + c)
            for j in range(4):
                pe.wait_ge(S("mixn_ready"), j + 1)
                turn(mixn[:, j // 2, :], P, j, 4 + j, "mix_turned")
            for t in range(REAL):
                pe.wait_ge(S("w_out_loaded"), 32)
                pe.wait_ge(S("mixT_v"), t + 1)
                pe.wait_ge(S("mixT_a"), t + 1)
                for i in range(2):
                    for k in range(KD):
                        ins = nc.tensor.matmul(ps(2 * t + i), mixT[:, k, t * P:t * P + P], w_slice(2 + i, 0, W_COLS)[:, k, :],
                                               start=(k == 0), stop=(k == KD - 1))
                ins.then_inc(S("mix_made"), 1)
            for j in range(4):
                pe.wait_ge(S("hn2_ready"), j // 2 + 1)
                turn(hn2[:, j // 2, :], P, j, 4 + j, "n2_turned")
            pe.wait_ge(S("hn2T_ready"), 4)
            pe.wait_ge(S("w_pq_loaded"), 32)
            for c in range(HEADS):
                if c >= 4:
                    pe.wait_ge(S("qpT_ready"), c - 3)
                for k in range(KD):
                    ins = nc.tensor.matmul(ps(c % 4)[:, 0:SEQ], w_slice(c // 4, (c % 4) * P, P)[:, k, :], hn2T[:, k, :],
                                           start=(k == 0), stop=(k == KD - 1))
                ins.then_inc(S("pq_made"), 1)
            pe.wait_ge(S("keys_loaded"), 16)
            for u in range(UNITS):
                t, hd = divmod(u, HEADS)
                pe.wait_ge(S("qpT_ready"), hd + 1)
                if u >= 2:
                    pe.wait_ge(S("score_ready"), u - 1)
                for half in range(2):
                    r = slice(64 * half, 64 * half + 64)
                    ins = mm(ps(4 + 2 * (u % 2) + half)[:, 0:P], qpT[r, hd, t * P:t * P + P], keyT[r, hd, :], True, True)
                ins.then_inc(S("score_made"), 1)
            pe.wait_ge(S("score_ready"), UNITS)
            with pe.Fori(0, PASSES) as b:
                for p in range(2):
                    pe.wait_ge(S("y_added"), b * 2 + p + 1)
                    for k in range(TOPK):
                        s = k % RING
                        pe.wait_ge(S("diag_ready"), (b * 2 + p) * TOPK + k + 1)
                        pe.wait_ge(S(f"v_row{s}"), (b * 4 + 2 * p + k // RING + 1) * 16)
                        for half in range(2):
                            ins = nc.tensor.matmul(pairs[p][:, 512 * half:512 * half + 512], diag[:, k, :],
                                                   vring[s][:, 512 * half:512 * half + 512],
                                                   start=(k == 0), stop=(k == TOPK - 1))
                        ins.then_inc(S("v_used"), 1)
            for j in range(6):
                t, n = j // 2, ROWS[j // 2]
                pe.wait_ge(S("n3_ready"), t + 1)
                turn(nat2[0:n, t, :], n, j, j, "n3_turned")
            pe.wait_ge(S("uT_ready"), 6)
            pe.wait_ge(S("w_in2_loaded"), 48)
            for job in PJ2:
                name, kind, c0, t0, n = job
                nj = EV2[name][0]
                if nj >= 8:
                    _, e, k = EV2[PJ2[nj - 8][0]]
                    pe.wait_ge(S(f"evac2_{e}"), k)
                b = ps(nj % 8)
                for k in range(KD):
                    if kind == "T":
                        ins = nc.tensor.matmul(b[:, 0:n], w2_slice(c0)[:, k, :], uT[:, k, t0:t0 + n],
                                               start=(k == 0), stop=(k == KD - 1))
                    else:
                        ins = nc.tensor.matmul(b[0:n, 0:P], uT[:, k, t0:t0 + n], w2_slice(c0)[:, k, :],
                                               start=(k == 0), stop=(k == KD - 1))
                ins.then_inc(S("proj2_made"), 1)
            pe.wait_ge(S("wbd_loaded"), 64)
            pe.wait_ge(S("evac2_v"), max(k for _, e, k in EV2.values() if e == "v"))
            pe.wait_ge(S("evac2_a"), max(k for _, e, k in EV2.values() if e == "a"))
            for c in range(4):
                pe.wait_ge(S("conv_step"), 4 * c + 4)
                if c >= 2:
                    pe.wait_ge(S("sig_made"), c - 1)
                for g in range(2):
                    ins = nc.tensor.matmul(pairs[c % 2][:, 512 * g:512 * g + TOK], wbd[:, g, c, :], xc[:, c, :],
                                           start=True, stop=True)
                ins.then_inc(S("lru_made"), 1)
            for u in range(4):
                t, hf_ = divmod(u, 2)
                k0, nk = (0, META + P) if t == 0 else (META, SEQ)
                if u >= 1:
                    pe.wait_ge(S("s2_masked"), 2 * u)
                for j in range(4):
                    c, kv = 2 * hf_ + j // 2, j % 2
                    r = slice(64 * kv, 64 * kv + 64)
                    ins = mm(ps(kv)[:, (j // 2) * 256:(j // 2) * 256 + nk], q2T[r, c, t * P:t * P + P],
                             k2T[r, k0:k0 + nk], True, True)
                ins.then_inc(S("s2_made"), 1)
                pe.wait_ge(S("m_step"), 5 * u + 5)
                if u >= 1:
                    pe.wait_ge(S("pT_ready"), u)
                kt = [(META, 0), (P, META)] if t == 0 else [(P, 0), (P, P)]
                for j in range(4):
                    for i, (n, a) in enumerate(kt):
                        ins = nc.tensor.transpose(ps(2 + j // 2)[0:n, (j % 2) * 256 + i * P:(j % 2) * 256 + i * P + P],
                                                  S2[:, j, a:a + n], ident[:, :])
                ins.then_inc(S("p_turned"), 1)
                pe.wait_ge(S("pT_ready"), u + 1)
                pe.wait_ge(S("sig_made"), 4)
                if u >= 1:
                    pe.wait_ge(S("o2_ready"), u)
                tiles = [2, 0] if t == 0 else [0, 1]
                for cc in range(2):
                    o = ps(4)[:, cc * P:cc * P + P]
                    for kv in range(2):
                        for i in range(2):
                            n = kt[i][0]
                            ins = mm(o, v2[0:n, tiles[i], kv, :], pT[0:n, 2 * cc + kv, i, :],
                                     kv == 0 and i == 0, kv == 1 and i == 1)
                ins.then_inc(S("o2_made"), 1)
            for t in range(REAL):
                pe.wait_ge(S("w_out2_loaded"), 32)
                pe.wait_ge(S("o2_ready"), 4)
                pe.wait_ge(S("rec_ready"), 1)
                for i in range(2):
                    for k in range(KD):
                        ins = nc.tensor.matmul(pairs[t][:, 512 * i:512 * i + 512], mixT2[:, k, t * P:t * P + P],
                                               w_slice(2 + i, 0, W_COLS)[:, k, :], start=(k == 0), stop=(k == KD - 1))
                ins.then_inc(S("mix2_made"), 1)
            for j in range(4):
                pe.wait_ge(S("n4_ready"), j // 2 + 1)
                turn(nat2[:, j // 2, :], P, j, j, "n4_turned")
            pe.wait_ge(S("uF_split"), 4)

            def ff_pair(i, first, last):
                for stage in range(FF_STAGES):
                    s = stage % 2
                    for c in range(FF_GROUP):
                        e = s * FF_GROUP + c
                        pe.wait_ge(S("w_split"), (i * FF_STAGES + stage) * FF_GROUP + c + 1)
                        wh, wl = ff_high(stage, c), ff_low(stage, c)
                        if stage < 2:
                            if not (first and s == 0):
                                pe.wait_ge(S("relu_made"), (i * 2 + s) * FF_GROUP + c - 3)
                            for k in range(KD):
                                for n, (w, x_) in enumerate(((wh, uFh), (wh, uFl), (wl, uFh))):
                                    ins = nc.tensor.matmul(ps(c)[:, 0:SEQ], w[:, k, :], x_[:, k, :],
                                                           start=(k == 0 and n == 0), stop=(k == KD - 1 and n == 2))
                            ins.then_inc(S("f1_made"), 1)
                        else:
                            pe.wait_ge(S("f1_ready"), i * 2 * FF_GROUP + e + 1)
                            for t in range(REAL):
                                for n, (f, w) in enumerate(((f1h, wh), (f1h, wl), (f1l, wh))):
                                    for half in range(2):
                                        ins = mm(pairs[t][:, 512 * half:512 * half + 512],
                                                 f[:, s, c, t * P:t * P + P], w[:, 512 * half:512 * half + 512],
                                                 first and e == 0 and n == 0, last and e == 2 * FF_GROUP - 1 and n == 2)
                    if stage >= 2:
                        ins.then_inc(S("f2_group"), 1)

            ff_pair(0, True, False)
            with pe.Fori(1, FF_PAIRS - 1) as i:
                ff_pair(i, False, False)
            ff_pair(FF_PAIRS - 1, False, True)


def kernel(**inputs):
    import numpy as np
    import concourse.bacc as bacc
    from concourse.bass_utils import run_bass_kernel_spmd

    a = {k: np.asarray(v) for k, v in inputs.items()}

    def chunks(v):
        return v.reshape(-1, P).T

    cols = np.concatenate([
        chunks(a["norm1_g"][0]), chunks(a["g_pre_mix_2"][0]), chunks(a["g_pre_ffn_2"][0]), chunks(a["b_gate_up"][0]),
        a["conv_w_2"][0].reshape(CONV, 4, P).transpose(2, 1, 0).reshape(P, 16), chunks(a["conv_b_2"][0]),
        chunks(a["b_a_2"][0]), chunks(a["b_x_2"][0]), chunks(a["lru_lambda_2"][0])], axis=1)
    sinks = a["attn_sinks_2"][0].reshape(KVH, 4).T.reshape(-1)
    rows = np.concatenate([a["sb_norm_g"][0], a["gla_norm_g"][0], a["norm2_g"][0], a["norm_f_g"], a["g_post_mix_2"][0],
                           a["g_post_ffn_2"][0], sinks])
    keys = np.stack([a["sub_keys1"][0], a["sub_keys2"][0]]).transpose(0, 3, 1, 2).reshape(P, HEADS, NKEYS)
    w_in2 = a["w_in_2"][0]
    q = w_in2[:, 0:512].reshape(D, KVH, 4, 64).transpose(0, 2, 1, 3).reshape(D, 512)
    w_in2 = np.concatenate([q, w_in2[:, 512:]], axis=1)
    w_out2 = a["w_out_2"][0]
    o = w_out2[0:512].reshape(KVH, 4, 64, D).transpose(1, 0, 2, 3).reshape(512, D)
    w_out2 = np.concatenate([o, w_out2[512:]], axis=0)
    arrays = {
        "x": a["x"][0], "meta1": a["meta_tokens"], "meta2": a["meta_tokens_2"], "cols": cols, "rows": rows,
        "w_in": a["w_in"][0], "w_gate": a["w_gate_up"][0], "w_out": a["w_out"][0], "w_peer_q": a["w_peer_q"][0],
        "keys": keys, "expert_u": a["expert_u"][0], "expert_v": a["expert_v"][0], "w_in2": w_in2, "w_a": a["w_a_2"][0],
        "w_x": a["w_x_2"][0], "w_out2": w_out2, "w_ff1": a["w_ff1_2"][0], "w_ff2": a["w_ff2_2"][0],
    }
    nc = bacc.Bacc("TRN2", target_bir_lowering=False, num_devices=1)
    feed, args = {}, []
    for name, v in arrays.items():
        v = np.ascontiguousarray(v)
        feed[f"in_{name}"] = v
        args.append(nc.dram_tensor(f"in_{name}", v.shape, F32, kind="ExternalInput").ap())
    out = nc.dram_tensor("out", (SEQ, D), F32, kind="ExternalOutput").ap()
    two_blocks_kernel(nc, *args, out)
    r = run_bass_kernel_spmd(nc, [feed], core_ids=[0])
    return r.results[0]["out"].reshape(1, SEQ, D)
```

```python
from contextlib import ExitStack

import concourse.bass as bass
from concourse import mybir

ALU = mybir.AluOpType
ACT = mybir.ActivationFunctionType
F32 = mybir.dt.float32
U32 = mybir.dt.uint32
R32 = mybir.dt.float32r
AX = mybir.AxisListType.X

P = 128
D = 1024
KD = D // P
SEQ = 256
META = 16
TOK = META + SEQ
EPS = 1e-6
ROWS = [P, P, META]
COL0 = [META, META + P, 0]
REAL = 2

SB_HEADS, SB_DIM = 8, 64
GLA_HEADS, DK, DV, RANK, TAU = 4, 64, 128, 16, 16.0
SUB = 32
NSUB = P // SUB

HEADS, NKEYS, TOPK = 8, 128, 16
RING = 8
UNITS = REAL * HEADS
PASSES = UNITS // 2
A_PASSES = PASSES // REAL + 1
RMS_N1, RMS_N2, RMS_PF = 0, 3, 14
RMS_NF, RMS_N3 = (5, 8), (6, 9, 7)
RMS_PM, RMS_N4 = (10, 12), (11, 13)
N3_ORDER = (0, 2, 1)
ROUTE_STEPS = 19
V_PRIME = 16

ATT, KVH = 8, 2
CHUNKS_LRU = 4
CONV = 4
LRU_C = 8.0
NEG = -1e30
FF_GROUP = 4
FF_GROUPS = 4 * D // (FF_GROUP * P)
FF_PAIRS = FF_GROUPS // 2

W_COLS = 512
C_NORM1, C_PREMIX, C_PREFFN, C_BG, C_CONVW, C_CONVB, C_BA, C_BX, C_LAM, C_END = (
    0, 8, 16, 24, 26, 42, 46, 50, 54, 58)
R_SB, R_GLA, R_NORM2, R_NORMF, R_POSTMIX, R_POSTFFN, R_SINK, R_END = (
    0, 512, 1024, 2048, 3072, 4096, 5120, 5128)


GLA_FACTORS = {1: 0, 2: 1, 3: 2, 4: 3}
GLA_UNITS = 4


def proj_plan():
    jobs = []
    for c in range(2):
        jobs.append((("gq", c), "T", 3, c * P, META, SEQ))
    for c in range(2):
        jobs.append((("gk", c), "T", 3, 256 + c * P, 0, TOK))
    jobs.append((("glr", 0), "T", 6, 0, 0, TOK))
    for t in range(3):
        jobs.append((("gv", t), "N", 4, 0, COL0[t], ROWS[t]))
    for t in range(3):
        jobs.append((("sbv", t), "N", 2, 0, COL0[t], ROWS[t]))
    for c in range(4):
        jobs.append((("sbq", c), "T", 0, c * P, META, SEQ))
        jobs.append((("sbk", c), "T", 1, c * P, 0, TOK))
    for t in range(2):
        jobs.append((("gr", t), "N", 5, 0, COL0[t], ROWS[t]))
    return jobs


W_IN_ORDER = (3, 4, 2, 0, 1, 5)
PJ_FIRST = 13
PJ_LATER = {0: 13, 1: 14, 2: 15, 3: 16, 4: 17, 5: 18, 7: 19, 8: 20}
GR_SPLIT = {5: (0, 1), 6: (2, 3)}
W_HELD = 4


def w_in_step(bi):
    return 0 if bi == 6 else W_IN_ORDER.index(bi)


def proj2_plan():
    jobs = []
    for c in range(4):
        jobs.append((("xr", c), "T", 768 + c * P, 0, TOK))
    for c in range(4):
        jobs.append((("q", c), "T", c * P, META, SEQ))
    jobs.append((("k", 0), "T", 512, 0, TOK))
    for t in range(3):
        jobs.append((("v", t), "N", 640, COL0[t], ROWS[t]))
    for c in range(4):
        jobs.append((("yr", c), "T", 1280 + c * P, META, SEQ))
    return jobs


def evac_plan(jobs, engine_of):
    done = {"v": 0, "a": 0}
    out = {}
    for n, job in enumerate(jobs):
        e = engine_of(job[0])
        done[e] += 1
        out[job[0]] = (n, e, done[e])
    return out


def two_blocks_kernel(nc, x, meta1, meta2, cols, rows, w_in, w_gate, w_out, w_peer_q, keys, expert_u,
                      expert_v, w_in2, w_a, w_x, w_out2, w_ff1, w_ff2, out):
    PJ, PJ2 = proj_plan(), proj2_plan()
    STEP_END = [1 + max(n for n, job in enumerate(PJ) if w_in_step(job[2]) == q) for q in range(len(W_IN_ORDER))]
    EV = evac_plan(PJ, lambda n: "a" if n[0] in ("gv", "sbq", "sbk", "gr") else "v")
    EV2 = evac_plan(PJ2, lambda n: "a" if n[0] in ("yr", "q") else "v")

    with ExitStack() as ctx:
        sems = {}

        def S(name):
            if name not in sems:
                sems[name] = ctx.enter_context(nc.semaphore(name))
            return sems[name]

        def sb(name, shape, dt=F32):
            return ctx.enter_context(nc.sbuf_tensor(name, shape, dt))

        banks2 = [ctx.enter_context(nc.psum_tensor(f"banks{2 * i}", [P, 1024], F32)) for i in range(4)]
        pairs = banks2[2:]

        def ps(i):
            return banks2[i // 2][:, (i % 2) * 512:(i % 2) * 512 + 512]

        with ExitStack() as first:
            wblk = [first.enter_context(nc.sbuf_tensor(f"wblk{i}", [P, KD * W_COLS], F32)) for i in range(6)]
            area = first.enter_context(nc.sbuf_tensor("area", [P, 76 * 256], F32))
        wblk_r = [sb(f"wblk_r{i}", [P, KD * W_COLS], R32) for i in range(6)]
        area_r = sb("area_r", [P, 76 * 256], R32)
        wlast = sb("wlast", [P, KD, RANK])
        row = sb("row", [P, R_END])
        col = sb("col", [P, C_END])
        ident = sb("ident", [P, P])
        ntri = sb("ntri", [P, P])
        neg1 = sb("neg1", [P, P])
        causal = sb("causal", [P, P])
        h = sb("h", [P, REAL, D])
        stat = sb("stat", [P, 64])
        epsc = sb("epsc", [P, 1])
        wgate = sb("wgate", [RANK, 2 * P])
        small = sb("small", [P, 256])
        small2 = sb("small2", [P, 256])

        def at(kb, shape, dt=F32):
            n = 1
            for s in shape:
                n *= s
            a = (area_r if dt is R32 else area)[:, int(kb * 256):int(kb * 256) + n]
            if dt is U32:
                a = a.bitcast(dt)
            if len(shape) == 1:
                return a
            names = "abcd"[:len(shape)]
            return a.rearrange(f"p ({' '.join(names)}) -> p {' '.join(names)}",
                               **{k: s for k, s in zip(names[1:], shape[1:])})

        def blk(i, shape, dt=F32):
            names = "abcd"[:len(shape)]
            return (wblk_r if dt is R32 else wblk)[i][:, :].rearrange(f"p ({' '.join(names)}) -> p {' '.join(names)}",
                                           **{k: s for k, s in zip(names[1:], shape[1:])})

        hM = at(0, [D])
        hnT = at(4, [KD, TOK])
        sbqT = at(12.5, [4, SEQ])
        sbkT = at(16.5, [4, TOK])
        gqT = at(20.75, [2, SEQ])
        gkT = at(22.75, [2, TOK])
        glrT = at(24.875, [TOK])
        hnTh, hnTl = at(42, [KD, TOK], R32), at(50.5, [KD, TOK], R32)
        wlasth, wlastl = at(59.5, [KD, RANK], R32), at(60, [KD, RANK], R32)
        nat = at(26, [3, D])
        sbv = at(26, [3, 512])
        gv = at(32, [3, 512])
        gr = at(38, [2, 512])
        sp, aT, tmp = (wblk[2][:, 1280 * i:1280 * i + 1280].rearrange("p (a b) -> p a b", a=2) for i in range(3))
        lgt = wblk[2][:, 1280:1280 + 2 * TOK].rearrange("p (a b) -> p a b", a=2)
        nb = at(59, [2, TOK])
        pb = at(61.25, [2, TOK])
        gex = at(63.5, [3, 704])
        gexM = at(72, [2, META])
        state = at(73, [2, DV])
        klnat = at(74, [2, P])
        attT = at(75, [2, P])
        kzpad = at(4, [2, NSUB, P])
        os = at(0, [REAL, 512])
        og = at(8, [REAL, 512])
        mixn = at(52, [REAL, D])
        sqr = [at(60, [REAL * 512]), at(64, [REAL * 512])]
        mixT = at(12.5, [KD, SEQ])
        hn2 = at(26, [REAL, D])
        hn2T = at(34, [KD, SEQ])
        qpT = at(0, [HEADS, SEQ])
        score = at(8, [UNITS + 1, 2 * NKEYS])
        scoref = at(8, [(UNITS + 1) * 2 * NKEYS])
        keyT = at(42, [HEADS, NKEYS])
        diag = at(34, [TOPK, P])
        cur = at(46, [2, 256])
        cur2 = at(48, [256])
        cand = at(49, [256])
        pick = at(50, [512])
        wtail = at(52, [KD, 768])

        v16 = small[:, 0:32]
        i16 = small[:, 32:64].bitcast(U32)
        if16 = small[:, 64:96]
        sc16 = small[:, 96:112]
        pos = small[:, 112:128].bitcast(U32)
        posij = small[:, 128:160].bitcast(U32)
        posf = small[:, 160:192]
        eij = small[:, 192:224]
        nmx = small[:, 224:225]
        den = small[:, 225:226]
        rden = small[:, 226:227]
        uidx = small2[:, 0:32].bitcast(U32).rearrange("p (a b) -> p a b", a=2)
        vidx = small2[:, 192:224].bitcast(U32).rearrange("p (a b) -> p a b", a=2)
        dots = small2[:, 32:64].rearrange("p (a b) -> p a b", a=2)
        gate = small2[:, 64:96].rearrange("p (a b) -> p a b", a=2)
        ggel = small2[:, 96:128].rearrange("p (a b) -> p a b", a=2)
        gw = small2[:, 128:160].rearrange("p (a b) -> p a b", a=2)
        ex16 = small2[:, 160:176]
        iota16 = small2[:, 176:192]
        uring = [blk(2 + s // 4, [4, D])[:, s % 4, :] for s in range(RING)]
        vring = [blk(4 + s // 4, [4, D])[:, s % 4, :] for s in range(RING)]

        hM2 = at(0, [D])
        nat2 = at(8, [3, D])
        uT = at(28.5, [KD, TOK])
        q2T = at(37, [4, SEQ])
        k2T = at(41, [TOK])
        v2 = at(42.25, [3, KVH, P])
        xr = at(4, [4, TOK + 3])
        xc = at(20, [4, TOK])
        geluy = at(46, [4, SEQ])
        lr = at(8.5, [4, TOK])
        li = at(12.75, [4, TOK])
        lt = at(4, [4, TOK])
        uFh, uFl = at(28, [KD, SEQ], R32), at(36, [KD, SEQ], R32)
        uF = at(36, [KD, SEQ])
        lm = at(24.25, [4, TOK])
        wbd = row[:, 0:1024].rearrange("p (g c n) -> p g c n", g=2, c=4)
        mask2 = row[:, 1024:1536].rearrange("p (t n) -> p t n", t=2)
        mixT2 = at(52, [KD, SEQ])
        S2 = wblk[5][:, 0:8 * SEQ].rearrange("p (u j n) -> p u j n", u=2, j=4)
        pT = wblk[5][:, 8 * SEQ:16 * SEQ].rearrange("p (u j i n) -> p u j i n", u=2, j=4, i=2)
        att_max, att_nmax, att_sum, att_sink = (
            small[:, 8 * i:8 * i + 8].rearrange("p (u j) -> p u j", u=2) for i in range(4))
        f1h, f1l = at(20, [2, FF_GROUP, SEQ], R32), at(8, [2, FF_GROUP, SEQ], R32)
        f1 = at(8, [2, FF_GROUP, SEQ])

        def w_slice(i, c0, n, dt=F32):
            return blk(i, [KD, W_COLS], dt)[:, :, c0:c0 + n]

        def w2_slice(c0, dt=F32):
            if c0 < 1024:
                return blk(c0 // 512, [KD, W_COLS], dt)[:, :, c0 % 512:c0 % 512 + P]
            return at(52, [KD, 768], dt)[:, :, c0 - 1024:c0 - 1024 + P]

        W2_CHUNKS = ([(768 + i * P, 2, i) for i in range(4)] + [(i * P, 3, i) for i in range(4)]
                     + [(512, 4, 0), (640, 5, 3)] + [(1280 + i * P, 2, i) for i in range(4)])
        W2_FROM, UT_FROM = 4 * len(W_IN_ORDER), 7

        def w2_high(m):
            b, s = W2_CHUNKS[m][1:]
            return wblk_r[b][:, s * KD * P:(s + 1) * KD * P].rearrange("p (k n) -> p k n", k=KD)

        uTh = wblk_r[4][:, KD * P:KD * P + KD * TOK].rearrange("p (k n) -> p k n", k=KD)
        uTl = at(28.5, [KD, TOK], R32)

        def uT_part(j):
            t = N3_ORDER[j // 2]
            return slice(4 * (j % 2), 4 * (j % 2) + 4), slice(COL0[t], COL0[t] + ROWS[t])

        def proj_bank(n):
            return n % 8 if n < PJ_FIRST else 1

        def in_chunk(q, c, high, dt=R32):
            return w_slice(W_HELD + q % 2 if high else q % W_HELD, c * P, P, dt)

        FF_AT = [4, 0]

        FF_STAGES = 4

        def ff_low(stage, c, dt=R32):
            s = stage % 2
            if stage < 2:
                return w_slice(FF_AT[s], c * P, P, dt)
            return blk(FF_AT[s] + 1, [FF_GROUP, D], dt)[:, c, :]

        def ff_high(stage, c):
            if stage < 2:
                b = at(60 - 16 * stage, [KD * W_COLS], R32)
            else:
                b = wblk_r[stage][:, :]
            if stage < 2:
                return b.rearrange("p (k n) -> p k n", k=KD)[:, :, c * P:c * P + P]
            return b.rearrange("p (c n) -> p c n", c=FF_GROUP)[:, c, :]

        block = ctx.enter_context(nc.Block())

        @block.sync
        def _(sp_q):
            def block_of(src, c0):
                return src.rearrange("(k p) n -> p k n", p=P)[:, :, c0:c0 + W_COLS]

            sp_q.dma_start(h[:, 0, :], x[0:P, :]).then_inc(S("h_loaded0"), 16)
            sp_q.dma_start(h[:, 1, :], x[P:SEQ, :]).then_inc(S("h_loaded1"), 16)
            sp_q.dma_start(hM[0:META, :], meta1).then_inc(S("h_loaded2"), 16)
            sp_q.dma_start(col[:, :], cols).then_inc(S("col_loaded"), 16)
            for q, i in enumerate(W_IN_ORDER):
                if q == W_HELD:
                    sp_q.dma_start(row[:, :], rows.partition_broadcast(P)).then_inc(S("row_loaded"), 16)
                if q >= W_HELD:
                    sp_q.wait_ge(S("proj_made"), STEP_END[q - W_HELD])
                sp_q.dma_start(blk(q % W_HELD, [KD, W_COLS]), block_of(w_in, i * W_COLS)).then_inc(S(f"w_in_loaded{q}"), 16)
                if q == 0:
                    sp_q.dma_start(wlast[:, :, :], w_in.rearrange("(k p) n -> p k n", p=P)[:, :, 6 * W_COLS:])\
                        .then_inc(S("narrow_loaded"), 16)
                    sp_q.dma_start(wgate[:, :], w_gate).then_inc(S("narrow_loaded"), 16)
            sp_q.wait_ge(S("proj_made"), STEP_END[3])
            sp_q.dma_start(blk(3, [KD, W_COLS]), block_of(w_out, W_COLS)).then_inc(S("w_out_loaded1"), 16)
            sp_q.wait_ge(S("proj_made"), STEP_END[4])
            sp_q.dma_start(blk(4, [KD, W_COLS]), block_of(w_peer_q, 0)).then_inc(S("w_pq_loaded"), 16)
            sp_q.dma_start(blk(0, [KD, W_COLS]), block_of(w_in2, 0)).then_inc(S("w_in2_loaded"), 16)
            sp_q.wait_ge(S("pv_made"), SB_HEADS)
            sp_q.dma_start(blk(2, [KD, W_COLS]), block_of(w_out, 0)).then_inc(S("w_out_loaded0"), 16)
            sp_q.wait_ge(S("proj_made"), len(PJ))
            sp_q.dma_start(blk(5, [KD, W_COLS]), block_of(w_peer_q, W_COLS)).then_inc(S("w_pq_loaded"), 16)
            sp_q.dma_start(blk(1, [KD, W_COLS]), block_of(w_in2, W_COLS)).then_inc(S("w_in2_loaded"), 16)
            sp_q.wait_ge(S("mix_turned"), 4)
            sp_q.dma_start(keyT[:, :, :], keys).then_inc(S("keys_loaded"), 16)
            sp_q.dma_start(wtail[:, :, :], w_in2.rearrange("(k p) n -> p k n", p=P)[:, :, 1024:1792])\
                .then_inc(S("w_in2_loaded"), 16)
            sp_q.wait_ge(S("score_ready"), UNITS)
            sp_q.dma_start(hM2[0:META, :], meta2).then_inc(S("h2_loaded"), 16)
            sp_q.wait_ge(S("proj2_made"), 8)
            sp_q.dma_start(blk(3, [KD, W_COLS]), block_of(w_out2, W_COLS)).then_inc(S("w_out2_loaded"), 16)
            sp_q.wait_ge(S("proj2_made"), len(PJ2))
            sp_q.dma_start(blk(2, [KD, W_COLS]), block_of(w_out2, 0)).then_inc(S("w_out2_loaded"), 16)
            w1v = w_ff1.rearrange("(k p) n -> p k n", p=P)
            w2v = w_ff2.rearrange("(g c p) n -> p g c n", p=P, c=FF_GROUP)

            def load_ff1(g, s):
                sp_q.dma_start(blk(FF_AT[s], [KD, W_COLS]), w1v[:, :, bass.ds(g * W_COLS, W_COLS)])\
                    .then_inc(S(f"w_ff1_loaded{s}"), 16)

            def load_ff2(g, s):
                sp_q.dma_start(blk(FF_AT[s] + 1, [FF_GROUP, D]), w2v[:, bass.ds(g, 1), :, :].rearrange("p g c n -> p (g c) n"))\
                    .then_inc(S(f"w_ff2_loaded{s}"), 16)

            load_ff1(0, 0)
            load_ff1(1, 1)
            load_ff2(1, 1)
            sp_q.wait_ge(S("o2_made"), 4)
            load_ff2(0, 0)
            with sp_q.Fori(1, FF_PAIRS) as i:
                for s in range(2):
                    sp_q.wait_ge(S("f1_made"), (i * 2 + s - 1) * FF_GROUP)
                    load_ff1(i * 2 + s, s)
                for s in range(2):
                    sp_q.wait_ge(S("f2_group"), i * 2 + s - 1)
                    load_ff2(i * 2 + s, s)
            for t in range(REAL):
                sp_q.wait_ge(S("out_ready"), t + 1)
                sp_q.dma_start(out[t * P:(t + 1) * P, :], h[:, t, :]).then_inc(S("out_stored"), 16)
            sp_q.wait_ge(S("out_stored"), 16 * REAL)

        @block.gpsimd
        def _(pool):
            nc.gpsimd.memset(ident[:, :], 0.0).then_inc(S("masks_cleared"), 1)
            nc.gpsimd.memset(ntri[:, :], -1.0).then_inc(S("masks_cleared"), 1)
            nc.gpsimd.memset(neg1[:, :], -1.0).then_inc(S("masks_ready"), 1)
            nc.gpsimd.memset(causal[:, :], 1.0).then_inc(S("masks_cleared"), 1)
            pool.wait_ge(S("masks_cleared"), 3)
            nc.gpsimd.affine_select(out=ident[:, :], in_=ident[:, :], compare_op=ALU.not_equal, fill=1.0, base=0,
                                    pattern=[[-1, P]], channel_multiplier=1).then_inc(S("masks_ready"), 1)
            nc.gpsimd.affine_select(out=ntri[:, :], in_=ntri[:, :], compare_op=ALU.is_ge, fill=0.0, base=0,
                                    pattern=[[-1, P]], channel_multiplier=1).then_inc(S("masks_ready"), 1)
            nc.gpsimd.affine_select(out=causal[:, :], in_=causal[:, :], compare_op=ALU.is_ge, fill=0.0, base=0,
                                    pattern=[[1, P]], channel_multiplier=-1).then_inc(S("masks_ready"), 1)
            nc.gpsimd.iota(iota16, pattern=[[1, TOPK]], base=0, channel_multiplier=0,
                           allow_small_or_imprecise_dtypes=True).then_inc(S("masks_ready"), 1)
            pool.wait_ge(S("hnT_split"), 6)
            nc.gpsimd.memset(kzpad[:, :, :, :], 0.0).then_inc(S("masks_cleared"), 1)

            def keep_past(view):
                return nc.gpsimd.affine_select(out=view, in_=view, compare_op=ALU.is_gt, fill=0.0, base=0,
                                               pattern=[[1, P]], channel_multiplier=-1)

            for i in range(SB_HEADS + 1):
                if i < SB_HEADS:
                    pool.wait_ge(S("sp_made"), i + 1)
                    keep_past(sp[:, i % 2, 0:P])
                    keep_past(sp[:, i % 2, 512:640]).then_inc(S("sp_masked"), 1)
                if i >= 1:
                    pool.wait_ge(S("aT_made"), i)
                    keep_past(aT[:, (i - 1) % 2, 0:P])
                    keep_past(aT[:, (i - 1) % 2, 512:640]).then_inc(S("aT_masked"), 1)

            pool.wait_ge(S("row_loaded"), 16)
            for t in range(REAL):
                pool.wait_ge(S("silu_made"), t + 1)
                nc.gpsimd.tensor_tensor(gr[:, t, :], gr[:, t, :], row[:, R_GLA:R_GLA + 512], ALU.mult)\
                    .then_inc(S("gr_gained"), 1)

            def gather_u(u, p, k):
                s = k % RING
                pool.wait_ge(S("u_used"), u * TOPK + k + 1)
                pool.sem_inc(S("gather_turn"), 1)
                nc.gpsimd.indirect_dma_start(
                    out=uring[s], out_offset=None, in_=expert_u,
                    in_offset=bass.IndirectOffsetOnAxis(ap=uidx[:, p, k:k + 1], axis=0),
                ).then_inc(S(f"u_row{s}"), 16)

            def gather_v(u, p, k):
                s = k % RING
                pool.wait_ge(S("v_used"), u * TOPK + k + 1 + V_PRIME - RING)
                pool.sem_inc(S("gather_turn"), 1)
                nc.gpsimd.indirect_dma_start(
                    out=vring[s], out_offset=None, in_=expert_v,
                    in_offset=bass.IndirectOffsetOnAxis(ap=vidx[:, p, k:k + 1], axis=0),
                ).then_inc(S(f"v_row{s}"), 16)

            def gather_pass(b, last):
                for p in range(2):
                    u = b * 2 + p
                    ahead = not (last and p == 1)
                    if ahead:
                        pool.wait_ge(S("uidx_ready"), u + 2)
                    pool.wait_ge(S("vidx_ready"), u + 1)
                    for k in range(TOPK):
                        if ahead:
                            gather_u(u + 1, 1 - p, k)
                        gather_v(u, p, k)

            pool.wait_ge(S("mix_made"), REAL)
            pool.wait_ge(S("uidx_ready"), 1)
            for k in range(TOPK):
                gather_u(0, 0, k)
            pool.wait_ge(S("pq_made"), HEADS)
            with pool.Fori(0, PASSES - 1) as b:
                gather_pass(b, False)
            gather_pass(PASSES - 1, True)

            pool.wait_ge(S("hn2_ready"), REAL)
            nc.gpsimd.memset(mask2, 0.0).then_inc(S("masks_cleared"), 1)
            nc.gpsimd.memset(wbd, 0.0).then_inc(S("masks_cleared"), 1)
            pool.wait_ge(S("masks_cleared"), 6)
            nc.gpsimd.affine_select(out=mask2[:, 0, 0:META], in_=mask2[:, 0, 0:META], compare_op=ALU.is_gt, fill=NEG,
                                    base=P - META, pattern=[[1, META]], channel_multiplier=-1).then_inc(S("mask2_ready"), 1)
            nc.gpsimd.affine_select(out=mask2[:, 0, META:META + P], in_=mask2[:, 0, META:META + P], compare_op=ALU.is_ge,
                                    fill=NEG, base=0, pattern=[[-1, P]], channel_multiplier=1).then_inc(S("mask2_ready"), 1)
            nc.gpsimd.affine_select(out=mask2[:, 1, 0:P], in_=mask2[:, 1, 0:P], compare_op=ALU.is_gt, fill=NEG,
                                    base=0, pattern=[[1, P]], channel_multiplier=-1).then_inc(S("mask2_ready"), 1)
            nc.gpsimd.affine_select(out=mask2[:, 1, P:SEQ], in_=mask2[:, 1, P:SEQ], compare_op=ALU.is_ge, fill=NEG,
                                    base=0, pattern=[[-1, P]], channel_multiplier=1).then_inc(S("mask2_ready"), 1)
            for g, w in enumerate((w_a, w_x)):
                for half in range(2):
                    src = w.rearrange("(c a) i o -> a i c o", a=2)[half]
                    pool.dma_start(wbd[64 * half:64 * half + 64, g, :, 64 * half:64 * half + 64], src)\
                        .then_inc(S("wbd_loaded"), 16)
        @block.scalar
        def _(act):
            linked = [0]

            def link(ins):
                linked[0] += 1
                ins.then_inc(S("scalar_step"), 1)
                act.wait_ge(S("scalar_step"), linked[0])

            for t in range(3):
                n = ROWS[t]
                src = h[:, t, :] if t < 2 else hM[0:META, :]
                act.wait_ge(S(f"h_loaded{t}"), 16)
                link(nc.scalar.activation(nat[0:n, t, :], src, ACT.Square, accum_out=stat[0:n, t:t + 1]))
            act.wait_ge(S("eps_ready"), 1)
            for t in range(3):
                n = ROWS[t]
                nc.scalar.activation(stat[0:n, 3 + t:4 + t], stat[0:n, t:t + 1], ACT.Sqrt, scale=1.0 / D,
                                     bias=epsc[0:n, :]).then_inc(S("rms_ready"), 1)

            def evac(job):
                name = job[0]
                n, e, k = EV[name]
                if e != "a":
                    return
                b = ps(proj_bank(n))
                act.wait_ge(S("proj_made"), n + 1)
                kind, i = name
                if kind == "gv":
                    r = ROWS[i]
                    ins = nc.scalar.activation(gv[0:r, i, :], b[0:r, :], ACT.Copy)
                elif kind == "gr":
                    ins = nc.scalar.activation(gr[:, i, :], b, ACT.Copy)
                elif kind == "sbq":
                    ins = nc.scalar.activation(sbqT[:, i, :], b[:, 0:SEQ], ACT.Copy, scale=SB_DIM ** -0.5)
                elif kind == "sbk":
                    ins = nc.scalar.activation(sbkT[:, i, :], b[:, 0:TOK], ACT.Copy)
                ins.then_inc(S("evac_a"), 1)

            def in_high(q, cs=range(4)):
                if q >= 2:
                    act.wait_ge(S("proj_made"), STEP_END[q - 2])
                act.wait_ge(S(f"w_in_loaded{q}"), 16)
                for c in cs:
                    nc.scalar.activation(in_chunk(q, c, True), in_chunk(q, c, False, F32), ACT.Copy)\
                        .then_inc(S("w_in_high"), 1)

            in_high(0)
            for j in range(6):
                act.wait_ge(S("hnT_ready"), j + 1)
                t, k0 = j // 2, 4 * (j % 2)
                cs = slice(COL0[t], COL0[t] + ROWS[t])
                nc.scalar.activation(hnTh[:, k0:k0 + 4, cs], hnT[:, k0:k0 + 4, cs], ACT.Copy).then_inc(S("hnT_high"), 1)
            act.wait_ge(S("narrow_loaded"), 32)
            nc.scalar.activation(wlasth, wlast[:, :, :], ACT.Copy).then_inc(S("hnT_high"), 1)
            in_high(1)
            for q in range(3):
                for job in PJ[:PJ_FIRST]:
                    if w_in_step(job[2]) == q:
                        evac(job)
                in_high(q + 2)
            for job in PJ[PJ_FIRST - 2:PJ_FIRST]:
                evac(job)
            nc.scalar.preload_act_table_set("natural_log_exp_and_others")
            act.wait_ge(S("lg_min"), 2)
            link(nc.scalar.activation(lgt[:, 0, :], ps(0)[:, 0:TOK], ACT.Abs, bias=col[:, C_BG:C_BG + 1]))
            link(nc.scalar.activation(lgt[:, 1, :], ps(1)[:, 0:TOK], ACT.Abs, bias=col[:, C_BG + 1:C_BG + 2]))
            link(nc.scalar.activation(lgt[:, :, :], lgt[:, :, :], ACT.Exp, scale=-1.0))
            nc.scalar.activation(lgt[:, :, :], lgt[:, :, :], ACT.Ln, bias=1.0).then_inc(S("lg_ln"), 1)

            def sb_soft(i):
                z = pairs[i % 2][:, 0:640]
                act.wait_ge(S("z_made"), i + 1)
                link(nc.scalar.activation(tmp[:, i % 2, :], z, ACT.Abs))
                link(nc.scalar.activation(tmp[:, i % 2, :], tmp[:, i % 2, :], ACT.Exp, scale=-1.0))
                nc.scalar.activation(tmp[:, i % 2, :], tmp[:, i % 2, :], ACT.Ln, bias=1.0).then_inc(S("z_ln"), 1)

            def sb_weights(i):
                act.wait_ge(S("s_made"), i + 1)
                if i >= 2:
                    act.wait_ge(S("pv_made"), i - 1)
                nc.scalar.activation(aT[:, i % 2, :], pairs[i % 2][:, 0:640], ACT.Exp).then_inc(S("aT_made"), 1)


            def factors_M(c):
                nc.scalar.activation(gexM[:, c, :], pb[:, c, 0:META], ACT.Exp, scale=-1.0,
                                     bias=pb[:, c, META - 1:META])
                last = COL0[0] + P - 1
                nc.scalar.activation(stat[:, 42 + c:43 + c], pb[:, c, last:last + 1], ACT.Exp).then_inc(S("gex_made"), 1)

            def factors(t, c):
                u = t * 2 + c
                g = gex[:, u % 3, :]
                o = COL0[t]
                if u >= 3:
                    act.wait_ge(S("o_made"), 2 * (u - 3) + 2)
                    act.wait_ge(S("klT_made"), u)
                at_ = 0
                for j in range(NSUB):
                    n = P - SUB * j
                    e = o + SUB * j + SUB - 1
                    nc.scalar.activation(g[:, at_:at_ + n], pb[:, c, o + SUB * j:o + P], ACT.Exp,
                                         bias=nb[:, c, e:e + 1])
                    at_ += n
                for j in range(NSUB):
                    e = o + SUB * j + SUB - 1
                    nc.scalar.activation(g[:, 320 + SUB * j:352 + SUB * j], pb[:, c, o + SUB * j:o + SUB * j + SUB],
                                         ACT.Exp, scale=-1.0, bias=pb[:, c, e:e + 1])
                nc.scalar.activation(g[:, 448:576], pb[:, c, o:o + P], ACT.Exp)
                nc.scalar.activation(g[:, 576:704], pb[:, c, o:o + P], ACT.Exp, scale=-1.0,
                                     bias=pb[:, c, o + P - 1:o + P]).then_inc(S("gex_made"), 1)

            for i in range(SB_HEADS + 1):
                if i < SB_HEADS:
                    if i >= 2:
                        act.wait_ge(S("sp_made"), i - 1)
                    sb_soft(i)
                if i in PJ_LATER:
                    evac(PJ[PJ_LATER[i]])
                if i >= 1:
                    sb_weights(i - 1)
                if i in GR_SPLIT:
                    in_high(5, GR_SPLIT[i])
                if i == 0:
                    act.wait_ge(S("decay_ready"), 2)
                    factors_M(0)
                    factors_M(1)
                elif i in GLA_FACTORS:
                    factors(*divmod(GLA_FACTORS[i], 2))
            act.wait_ge(S("evac_a"), EV[("gr", 1)][2])
            for t in range(REAL):
                nc.scalar.activation(gr[:, t, :], gr[:, t, :], ACT.Silu).then_inc(S("silu_made"), 1)
            act.wait_ge(S("ss_made"), 1)
            nc.scalar.activation(stat[:, 24:40], stat[:, 8:24], ACT.Sqrt, scale=1.0 / SB_DIM,
                                 bias=epsc[:, :]).then_inc(S("hrms_made"), 1)
            act.wait_ge(S("ss_made"), 2)
            nc.scalar.activation(small[:, 8:16], small[:, 0:8], ACT.Sqrt, scale=1.0 / DV,
                                 bias=epsc[:, :]).then_inc(S("hrms_made"), 1)
            for t in range(REAL):
                act.wait_ge(S("mix_turned"), t + 1)
                nc.scalar.activation(mixT[:, 0:4, t * P:t * P + P],
                                     ps(4 + t).rearrange("p (a b) -> p a b", a=4), ACT.Copy).then_inc(S("mixT_a"), 1)
            for t in range(REAL):
                act.wait_ge(S("h_mixed"), t + 1)
                link(nc.scalar.activation(hn2[:, t, :], h[:, t, :], ACT.Square, accum_out=stat[:, 32 + t:33 + t]))
                nc.scalar.activation(stat[:, 34 + t:35 + t], stat[:, 32 + t:33 + t], ACT.Sqrt, scale=1.0 / D,
                                     bias=epsc[:, :]).then_inc(S("rms_ready"), 1)
            def queries_out(c):
                act.wait_ge(S("pq_made"), c + 1)
                nc.scalar.activation(qpT[:, c, :], ps(c % 4)[:, 0:SEQ], ACT.Copy).then_inc(S("qpT_ready"), 1)

            def scores_out(hd):
                for t in range(REAL):
                    act.wait_ge(S("score_made"), REAL * hd + t + 1)
                    nc.scalar.activation(score[:, t * HEADS + hd, :].rearrange("p (a b) -> p a b", a=2),
                                         pairs[t][:, :].rearrange("p (a b) -> p a b", a=2)[:, :, 0:P], ACT.Copy)\
                        .then_inc(S("score_ready"), 1)

            def unit_scores(u, p):
                if not isinstance(u, int) or u >= 2:
                    act.wait_ge(S("cur_used"), u - 1)
                nc.scalar.activation(cur[:, p, :], scoref[:, bass.ds(u * 256, 256)], ACT.Copy)\
                    .then_inc(S("cur_ready"), 1)

            def gate_exps(u):
                act.wait_ge(S("sc_ready"), u + 1)
                nc.scalar.activation(ex16, sc16, ACT.Exp, bias=nmx, accum_out=den).then_inc(S("gex16_ready"), 1)

            queries_out(0)
            for c in range(1, HEADS + 1):
                if c < HEADS:
                    queries_out(c)
                scores_out(c - 1)
                if c <= 2:
                    act.wait_ge(S("score_ready"), REAL * (c - 1) + 1)
                    unit_scores(c - 1, c - 1)
                if c == 4:
                    gate_exps(0)

            act.wait_ge(S("score_ready"), UNITS)
            act.wait_ge(S("hn2T_ready"), 5)

            def gelu_dots(u, p):
                act.wait_ge(S("u_used"), (u + 1) * TOPK + RING)
                nc.scalar.activation(ggel[:, p, :], dots[:, p, :], ACT.Gelu).then_inc(S("gelu_ready"), 1)

            def weights_pass(b, last):
                for p in range(2):
                    u = b * 2 + p
                    act.wait_ge(S("gw_ready"), u + 1)
                    for k in range(TOPK):
                        act.wait_ge(S("v_used"), u * TOPK + k + 1)
                        nc.scalar.activation(diag[:, k, :], ident[:, :], ACT.Copy, scale=gw[:, p, k:k + 1])\
                            .then_inc(S("diag_ready"), 1)
                    if not last:
                        unit_scores(u + 3, 1 - p)
                        gate_exps(u + 2)
                    if not (last and p == 1):
                        gelu_dots(u + 1, 1 - p)

            unit_scores(2, 0)
            gate_exps(1)
            gelu_dots(0, 0)
            def root(src, n, dump, a, b):
                link(nc.scalar.activation(dump, src, ACT.Square, accum_out=stat[0:n, a:a + 1]))
                nc.scalar.activation(stat[0:n, b:b + 1], stat[0:n, a:a + 1], ACT.Sqrt, scale=1.0 / D,
                                     bias=epsc[0:n, :]).then_inc(S("rms_ready"), 1)

            def w2_highs(ms):
                act.wait_ge(S("w_in2_loaded"), 48)
                for m in ms:
                    nc.scalar.activation(w2_high(m), w2_slice(W2_CHUNKS[m][0]), ACT.Copy).then_inc(S("w_in_high"), 1)

            def uT_highs(js):
                for j in js:
                    act.wait_ge(S("uT_ready"), j + 1)
                    ks, cs = uT_part(j)
                    nc.scalar.activation(uTh[:, ks, cs], uT[:, ks, cs], ACT.Copy).then_inc(S("hnT_high"), 1)

            def tile_roots(t):
                act.wait_ge(S("y_added"), 2 + HEADS * (t + 1))
                root(h[:, t, :], P, nat2[:, t, :], t, 2 + t)
                if t == 1:
                    uT_highs(range(4))
                act.wait_ge(S("hf_ready"), t + 1)
                root(h[:, t, :], P, nat2[:, t, :], 4 + t, 7 + t)

            with act.Fori(0, A_PASSES) as b:
                weights_pass(b, False)
            tile_roots(0)
            with act.Fori(A_PASSES, PASSES - 1) as b:
                weights_pass(b, False)
            weights_pass(PASSES - 1, True)
            act.wait_ge(S("u_used"), RING + UNITS * TOPK)
            w2_highs(range(8))
            link(nc.scalar.activation(stat[:, 48:52], col[:, C_LAM:C_LAM + 4], ACT.Abs))
            link(nc.scalar.activation(stat[:, 48:52], stat[:, 48:52], ACT.Exp, scale=-1.0))
            nc.scalar.activation(stat[:, 48:52], stat[:, 48:52], ACT.Ln, bias=1.0).then_inc(S("lam_ln"), 1)

            act.wait_ge(S("h2_loaded"), 16)
            root(hM2[0:META, :], META, nat2[0:META, 2, :], 6, 9)

            tile_roots(1)
            uT_highs(range(4, 6))
            w2_highs(range(8, 10))
            act.wait_ge(S("proj2_made"), 4)
            w2_highs(range(10, 14))

            def evac2(kind, i):
                n = EV2[(kind, i)][0]
                act.wait_ge(S("proj2_made"), n + 1)
                if kind == "yr":
                    ins = nc.scalar.activation(geluy[:, i, :], ps(n % 8)[:, 0:SEQ], ACT.Gelu_apprx_tanh)
                else:
                    ins = nc.scalar.activation(q2T[:, i, :], ps(n % 8)[:, 0:SEQ], ACT.Copy, scale=64 ** -0.5)
                ins.then_inc(S("evac2_a"), 1)

            def att_exps(u):
                act.wait_ge(S("nm_made"), u + 1)
                nk, b = (META + P if u // 2 == 0 else SEQ), u % 2
                for j in range(4):
                    nc.scalar.activation(S2[:, b, j, 0:nk], S2[:, b, j, 0:nk], ACT.Exp, bias=att_nmax[:, b, j:j + 1],
                                         accum_out=att_sum[:, b, j:j + 1])
                nc.scalar.activation(att_sink[:, b, :], att_sink[:, b, :], ACT.Exp).then_inc(S("p_made"), 1)

            for c in range(4):
                evac2("q", c)
            for c in range(4):
                act.wait_ge(S("lru_made"), c + 1)
                b2 = pairs[c % 2]
                nc.scalar.activation(lr[:, c, :], b2[:, 0:TOK], ACT.Sigmoid, bias=col[:, C_BA + c:C_BA + c + 1])
                nc.scalar.activation(li[:, c, :], b2[:, 512:512 + TOK], ACT.Sigmoid, bias=col[:, C_BX + c:C_BX + c + 1])\
                    .then_inc(S("sig_made"), 1)
            act.wait_ge(S("sig_made"), 4)
            act.wait_ge(S("lam_ready"), 2)
            for c in range(4):
                nc.scalar.activation(lm[:, c, :], lr[:, c, :], ACT.Tanh, scale=stat[:, 52 + c:53 + c])
                nc.scalar.activation(lr[:, c, :], lr[:, c, :], ACT.Exp, scale=stat[:, 56 + c:57 + c]).then_inc(S("a_made"), 1)
            att_exps(0)
            att_exps(1)
            for c in range(4):
                evac2("yr", c)
            act.wait_ge(S("m2_made"), 1)
            nc.scalar.activation(lm[:, :, :], lm[:, :, :], ACT.Sqrt).then_inc(S("root_made"), 1)
            att_exps(2)
            att_exps(3)

            def w_high(i, stage, c):
                if c == 0:
                    act.wait_ge(S(f"w_ff{1 + stage // 2}_loaded{stage % 2}"), (i + 1) * 16)
                nc.scalar.activation(ff_high(stage, c), ff_low(stage, c, F32), ACT.Copy).then_inc(S("w_high"), 1)

            act.wait_ge(S("proj2_made"), len(PJ2))
            for c in range(FF_GROUP):
                w_high(0, 0, c)
            for t in range(REAL):
                act.wait_ge(S("mix2_made"), t + 1)
                link(nc.scalar.activation(nat2[:, t, :], banks2[t][:, :], ACT.Square, accum_out=stat[:, 24 + t:25 + t]))
                nc.scalar.activation(stat[:, 26 + t:27 + t], stat[:, 24 + t:25 + t], ACT.Sqrt, scale=1.0 / D,
                                     bias=epsc[:, :]).then_inc(S("rms_ready"), 1)
                act.wait_ge(S("h_mixed2"), t + 1)
                link(nc.scalar.activation(nat2[:, t, :], h[:, t, :], ACT.Square, accum_out=stat[:, 28 + t:29 + t]))
                nc.scalar.activation(stat[:, 30 + t:31 + t], stat[:, 28 + t:29 + t], ACT.Sqrt, scale=1.0 / D,
                                     bias=epsc[:, :]).then_inc(S("rms_ready"), 1)

            for j in range(4):
                act.wait_ge(S("uF_ready"), j + 1)
                k0, cs = 4 * (j % 2), slice(j // 2 * P, j // 2 * P + P)
                nc.scalar.activation(uFh[:, k0:k0 + 4, cs], uF[:, k0:k0 + 4, cs], ACT.Copy)\
                    .then_inc(S("uF_high"), 1)

            def f1_high(i, e):
                act.wait_ge(S("f1_squared"), i * 2 * FF_GROUP + e + 1)
                s, c = divmod(e, FF_GROUP)
                nc.scalar.activation(f1h[:, s, c, :], f1[:, s, c, :], ACT.Copy).then_inc(S("f1_high"), 1)

            def hidden_pair(i, first, last):
                for stage in range(FF_STAGES):
                    for c in range(FF_GROUP):
                        if not (last and stage == FF_STAGES - 1):
                            w_high(i + (stage + 1) // FF_STAGES, (stage + 1) % FF_STAGES, c)
                        e = stage * FF_GROUP + c
                        if stage < 2:
                            if c == 0 and not first:
                                act.wait_ge(S("f2_group"), i * 2 + stage - 1)
                            act.wait_ge(S("f1_made"), i * 2 * FF_GROUP + e + 1)
                            nc.scalar.activation(f1[:, stage, c, :], ps(c)[:, 0:SEQ], ACT.Relu).then_inc(S("relu_made"), 1)
                        if 1 <= e <= 2 * FF_GROUP:
                            f1_high(i, e - 1)

            hidden_pair(0, True, False)
            with act.Fori(1, FF_PAIRS - 1) as i:
                hidden_pair(i, False, False)
            hidden_pair(FF_PAIRS - 1, False, True)
            for t in range(REAL):
                act.wait_ge(S("f2_group"), FF_GROUPS)
                link(nc.scalar.activation(nat2[:, t, :], pairs[t][:, :], ACT.Square, accum_out=stat[:, 32 + t:33 + t]))
                nc.scalar.activation(stat[:, 34 + t:35 + t], stat[:, 32 + t:33 + t], ACT.Sqrt, scale=1.0 / D,
                                     bias=epsc[:, :]).then_inc(S("rms_ready"), 1)

        @block.vector
        def _(dve):
            linked = [0]

            def link(ins):
                linked[0] += 1
                ins.then_inc(S("vector_step"), 1)
                dve.wait_ge(S("vector_step"), linked[0])

            nc.vector.memset(epsc[:, :], EPS).then_inc(S("eps_ready"), 1)
            for t in range(3):
                n = ROWS[t]
                src = h[:, t, :] if t < 2 else hM[0:META, :]
                dve.wait_ge(S("rms_ready"), RMS_N1 + t + 1)
                link(nc.vector.reciprocal(stat[0:n, 3 + t:4 + t], stat[0:n, 3 + t:4 + t]))
                nc.vector.tensor_scalar(nat[0:n, t, :], src, stat[0:n, 3 + t:4 + t], None, ALU.mult).then_inc(S("n1_ready"), 1)
            dve.wait_ge(S("col_loaded"), 16)

            def gained(turned, j, n, dst, gain):
                dve.wait_ge(S(turned), j + 1)
                return nc.vector.tensor_tensor(dst, ps(j)[:, :].rearrange("p (a b) -> p a b", a=4)[:, :, 0:n],
                                               gain.unsqueeze(2).to_broadcast([P, 4, n]), ALU.mult)

            for j in range(6):
                t, k0, n = j // 2, 4 * (j % 2), ROWS[j // 2]
                gained("n1_turned", j, n, hnT[:, k0:k0 + 4, COL0[t]:COL0[t] + n],
                       col[:, C_NORM1 + k0:C_NORM1 + k0 + 4]).then_inc(S("hnT_ready"), 1)
            def in_low(q, cs=range(4)):
                for c in cs:
                    dve.wait_ge(S("w_in_high"), 4 * q + c + 1)
                    nc.vector.tensor_tensor(in_chunk(q, c, False), in_chunk(q, c, False, F32), in_chunk(q, c, True),
                                            ALU.subtract).then_inc(S("w_in_split"), 1)

            in_low(0, [0])
            for j in range(6):
                dve.wait_ge(S("hnT_high"), j + 1)
                t, k0 = j // 2, 4 * (j % 2)
                cs = slice(COL0[t], COL0[t] + ROWS[t])
                nc.vector.tensor_tensor(hnTl[:, k0:k0 + 4, cs], hnT[:, k0:k0 + 4, cs], hnTh[:, k0:k0 + 4, cs],
                                        ALU.subtract).then_inc(S("hnT_split"), 1)
            in_low(0, range(1, 4))
            dve.wait_ge(S("hnT_high"), 7)
            nc.vector.tensor_tensor(wlastl, wlast[:, :, :], wlasth, ALU.subtract).then_inc(S("hnT_split"), 1)
            in_low(1)

            def evac(job):
                name = job[0]
                n, e, k = EV[name]
                if e != "v":
                    return
                kind, i = name
                b = ps(proj_bank(n))
                dve.wait_ge(S("proj_made"), n + 1)
                if kind == "gq":
                    ins = nc.vector.tensor_scalar(gqT[:, i, :], b[:, 0:SEQ], DK ** -0.5, None, ALU.mult)
                elif kind == "gk":
                    ins = nc.vector.tensor_copy(gkT[:, i, :], b[:, 0:TOK])
                elif kind == "glr":
                    ins = nc.vector.tensor_copy(glrT[0:RANK, :], b[0:RANK, 0:TOK])
                else:
                    r = ROWS[i]
                    ins = nc.vector.tensor_copy(sbv[0:r, i, :], b[0:r, :])
                ins.then_inc(S("evac_v"), 1)

            for q in range(3):
                for job in PJ[:PJ_FIRST]:
                    if w_in_step(job[2]) == q:
                        evac(job)
                in_low(q + 2)
            dve.wait_ge(S("lg_made"), 1)
            for c in range(2):
                nc.vector.tensor_scalar(nb[:, c, :], ps(c)[:, 0:TOK], col[:, C_BG + c:C_BG + c + 1], 0.0, ALU.add, ALU.min)\
                    .then_inc(S("lg_min"), 1)
            dve.wait_ge(S("lg_min"), 2)
            dve.wait_ge(S("lg_ln"), 1)
            link(nc.vector.tensor_tensor(lgt[:, :, :], lgt[:, :, :], nb[:, :, :], ALU.subtract))
            for c in range(2):
                for t in range(3):
                    seg = slice(COL0[t], COL0[t] + ROWS[t])
                    link(nc.vector.tensor_tensor_scan(nb[:, c, seg], lgt[:, c, seg], lgt[:, c, seg], 0.0, ALU.add, ALU.max))
            nc.vector.tensor_scalar(pb[:, :, :], nb[:, :, :], -1.0 / TAU, None, ALU.mult).then_inc(S("decay_ready"), 1)
            nc.vector.tensor_scalar(nb[:, :, :], nb[:, :, :], 1.0 / TAU, None, ALU.mult).then_inc(S("decay_ready"), 1)
            def sb_softplus(i):
                dve.wait_ge(S("z_ln"), i + 1)
                if i >= 2:
                    dve.wait_ge(S("s_made"), i - 1)
                nc.vector.scalar_tensor_tensor(out=sp[:, i % 2, :], in0=pairs[i % 2][:, 0:640], scalar=0.0,
                                               in1=tmp[:, i % 2, :], op0=ALU.max, op1=ALU.add).then_inc(S("sp_made"), 1)

            def sb_out(i):
                dve.wait_ge(S("pv_made"), i + 1)
                nc.vector.tensor_copy(os[:, :, SB_DIM * i:SB_DIM * i + SB_DIM],
                                      ps(2)[:, 0:2 * SB_DIM].rearrange("p (t n) -> p t n", t=2)).then_inc(S("os_ready"), 1)

            def state_from(c, n, upd):
                dve.wait_ge(S("klT_made"), upd + 1)
                nc.vector.tensor_copy(klnat[0:n, c, :], ps(0)[0:n, 256:256 + P]).then_inc(S("klnat_ready"), 1)
                dve.wait_ge(S("st_prod"), upd + 1)
                if upd >= 2:
                    dve.wait_ge(S("o_made"), 2 * c + 2)
                for hp in range(2):
                    rows_ = slice(64 * hp, 64 * hp + 64)
                    new = ps(0)[rows_, hp * DV:(hp + 1) * DV]
                    if upd < 2:
                        ins = nc.vector.tensor_copy(state[rows_, c, :], new)
                    else:
                        ins = nc.vector.scalar_tensor_tensor(out=state[rows_, c, :], in0=state[rows_, c, :],
                                                             scalar=stat[rows_, 42 + c:43 + c], in1=new,
                                                             op0=ALU.mult, op1=ALU.add)
                ins.then_inc(S("state_ready"), 1)

            def meta_keys():
                for c in range(2):
                    dve.wait_ge(S("gex_made"), c + 1)
                    nc.vector.tensor_tensor(gexM[:, c, :], gexM[:, c, :], gkT[:, c, 0:META], ALU.mult)\
                        .then_inc(S("klM_ready"), 1)

            def gla_products(u):
                t, c = divmod(u, 2)
                g = gex[:, u % 3, :]
                dve.wait_ge(S("gex_made"), 3 + u)
                a = 0
                for j in range(NSUB):
                    n = P - SUB * j
                    q0 = t * P + SUB * j
                    nc.vector.tensor_tensor(g[:, a:a + n], g[:, a:a + n], gqT[:, c, q0:q0 + n], ALU.mult)
                    a += n
                    k0 = COL0[t] + SUB * j
                    nc.vector.tensor_tensor(kzpad[:, u % 2, j, SUB * j:SUB * j + SUB], g[:, 320 + SUB * j:352 + SUB * j],
                                            gkT[:, c, k0:k0 + SUB], ALU.mult)
                nc.vector.tensor_tensor(g[:, 448:576], g[:, 448:576], gqT[:, c, t * P:t * P + P], ALU.mult)
                nc.vector.tensor_tensor(g[:, 576:704], g[:, 576:704], gkT[:, c, COL0[t]:COL0[t] + P], ALU.mult)\
                    .then_inc(S("gla_f"), 1)

            def gla_mask(u):
                dve.wait_ge(S("att_made"), 2 * u + 2)
                for hp in range(2):
                    if u >= 1:
                        dve.wait_ge(S("o_made"), 2 * u)
                    nc.vector.tensor_tensor(attT[:, hp, :], ps(0)[:, hp * P:hp * P + P], causal[:, :], ALU.mult)\
                        .then_inc(S("attT_ready"), 1)

            def gla_out(u):
                t, c = divmod(u, 2)
                dve.wait_ge(S("o_made"), 2 * u + 2)
                nc.vector.tensor_copy(og[:, t, 2 * DV * c:2 * DV * (c + 1)], ps(3)[:, 0:2 * DV]).then_inc(S("og_ready"), 1)

            dve.wait_ge(S("masks_cleared"), 4)
            for i in range(SB_HEADS + 3):
                if i < SB_HEADS:
                    sb_softplus(i)
                if 0 <= i - 4 < GLA_UNITS:
                    gla_mask(i - 4)
                if i >= 3:
                    sb_out(i - 3)
                if i == 1:
                    meta_keys()
                if i == 2:
                    for c in range(2):
                        state_from(c, META, c)
                if 0 <= i - 2 < GLA_UNITS:
                    gla_products(i - 2)
                if 0 <= i - 4 < GLA_UNITS:
                    gla_out(i - 4)
                    if i - 4 < 2:
                        state_from(i - 4, P, 2 + i - 4)
                if i in GR_SPLIT:
                    in_low(5, GR_SPLIT[i])

            dve.wait_ge(S("row_loaded"), 16)
            dve.wait_ge(S("og_ready"), GLA_UNITS)
            dve.wait_ge(S("os_ready"), SB_HEADS)
            parts = ((os, SB_HEADS, SB_DIM, R_SB, stat[:, 8:24], stat[:, 24:40]),
                     (og, GLA_HEADS, DV, R_GLA, small[:, 0:8], small[:, 8:16]))
            for (src, nh, dh, g0, ss, rr), sq in zip(parts, sqr):
                flat = src.rearrange("p t n -> p (t n)")
                link(nc.vector.tensor_tensor(sq, flat, flat, ALU.mult))
                nc.vector.tensor_reduce(ss, sq.rearrange("p (a b) -> p a b", b=dh), AX, ALU.add)\
                    .then_inc(S("ss_made"), 1)
            for part, (src, nh, dh, g0, ss, rr) in enumerate(parts):
                dve.wait_ge(S("hrms_made"), part + 1)
                link(nc.vector.reciprocal(rr, rr))
                for t in range(REAL):
                    m = mixn[:, t, 512 * part:512 * part + 512]
                    link(nc.vector.tensor_tensor(m.rearrange("p (a b) -> p a b", b=dh),
                                                 src[:, t, :].rearrange("p (a b) -> p a b", b=dh),
                                                 rr[:, nh * t:nh * t + nh].unsqueeze(2).to_broadcast([P, nh, dh]), ALU.mult))
                    if part == 1:
                        dve.wait_ge(S("gr_gained"), t + 1)
                    nc.vector.tensor_tensor(m, m, gr[:, t, :] if part == 1 else row[:, g0:g0 + 512], ALU.mult)\
                        .then_inc(S("mixn_ready"), 1)
            for t in range(REAL):
                dve.wait_ge(S("mix_turned"), REAL + t + 1)
                nc.vector.tensor_copy(mixT[:, 4:8, t * P:t * P + P],
                                      ps(6 + t).rearrange("p (a b) -> p a b", a=4)).then_inc(S("mixT_v"), 1)
            for t in range(REAL):
                dve.wait_ge(S("mix_made"), t + 1)
                nc.vector.tensor_tensor(h[:, t, 0:512], h[:, t, 0:512], ps(2 * t), ALU.add)
                nc.vector.tensor_tensor(h[:, t, 512:D], h[:, t, 512:D], ps(2 * t + 1), ALU.add).then_inc(S("h_mixed"), 1)
            for t in range(REAL):
                dve.wait_ge(S("rms_ready"), RMS_N2 + t + 1)
                link(nc.vector.reciprocal(stat[:, 34 + t:35 + t], stat[:, 34 + t:35 + t]))
                nc.vector.scalar_tensor_tensor(out=hn2[:, t, :], in0=h[:, t, :], scalar=stat[:, 34 + t:35 + t],
                                               in1=row[:, R_NORM2:R_NORM2 + D], op0=ALU.mult, op1=ALU.mult)\
                    .then_inc(S("hn2_ready"), 1)
            for j in range(4):
                dve.wait_ge(S("n2_turned"), j + 1)
                nc.vector.tensor_copy(hn2T[:, 4 * (j % 2):4 * (j % 2) + 4, (j // 2) * P:(j // 2) * P + P],
                                      ps(4 + j).rearrange("p (a b) -> p a b", a=4)).then_inc(S("hn2T_ready"), 1)
            dve.wait_ge(S("n2_turned"), 4)
            nc.vector.memset(score[:, UNITS, :], 0.0).then_inc(S("hn2T_ready"), 1)

            dve.wait_ge(S("masks_ready"), 5)

            def route(u, p):
                step = [0]

                def done(ins):
                    step[0] += 1
                    ins.then_inc(S("route_step"), 1)
                    dve.wait_ge(S("route_step"), u * ROUTE_STEPS + step[0])

                def tick(ins):
                    step[0] += 1
                    ins.then_inc(S("route_step"), 1)

                dve.wait_ge(S("cur_ready"), u + 1)
                dve.sem_inc(S("route_turn"), 1)

                def rests():
                    dve.wait_ge(S("route_step"), u * ROUTE_STEPS + step[0])
                    dve.sem_inc(S("route_turn"), 1)

                def best16(vals, vi, idx, rest):
                    for x, v, i, r in zip(vals, vi, idx, rest):
                        tick(nc.vector.max(v[:, 0:8], x))
                    rests()
                    for x, v, i, r in zip(vals, vi, idx, rest):
                        nc.vector.max_index(i[:, 0:8], v[:, 0:8], x)
                        tick(nc.vector.match_replace(r, v[:, 0:8], x, -3.0e38))
                    rests()
                    for x, v, i, r in zip(vals, vi, idx, rest):
                        tick(nc.vector.max(v[:, 8:16], r))
                    rests()
                    for x, v, i, r in zip(vals, vi, idx, rest):
                        tick(nc.vector.max_index(i[:, 8:16], v[:, 8:16], r))
                    rests()

                side = [cur[:, p, 0:NKEYS], cur[:, p, NKEYS:2 * NKEYS]]
                best16(side, [v16[:, 0:16], v16[:, 16:32]], [i16[:, 0:16], i16[:, 16:32]],
                       [cur2[:, 0:NKEYS], cur2[:, NKEYS:2 * NKEYS]])
                ins = nc.vector.tensor_tensor(cand.rearrange("p (a b) -> p a b", a=TOPK),
                                              v16[:, 0:16].unsqueeze(2).to_broadcast([P, TOPK, TOPK]),
                                              v16[:, 16:32].unsqueeze(1).to_broadcast([P, TOPK, TOPK]), ALU.add)
                ins.then_inc(S("cur_used"), 1)
                dve.wait_ge(S("cur_used"), u + 1)
                dve.sem_inc(S("route_turn"), 1)
                best16([cand], [sc16], [pos], [pick[:, 0:256]])
                tick(nc.vector.tensor_scalar(nmx, sc16[:, 0:1], -1.0, None, ALU.mult))
                tick(nc.vector.tensor_scalar(posij[:, 0:16], pos, 4, None, ALU.logical_shift_right))
                tick(nc.vector.tensor_scalar(posij[:, 16:32], pos, 15, None, ALU.bitwise_and))
                nc.vector.tensor_copy(if16, i16).then_inc(S("sc_ready"), 1)
                dve.wait_ge(S("route_step"), u * ROUTE_STEPS + step[0])
                done(nc.vector.tensor_copy(posf, posij))
                pk = pick.rearrange("p (s k i) -> p s k i", s=2, k=TOPK)
                done(nc.vector.tensor_tensor(
                    pk, iota16.unsqueeze(1).unsqueeze(1).to_broadcast([P, 2, TOPK, TOPK]),
                    posf.rearrange("p (s k) -> p s k", s=2).unsqueeze(3).to_broadcast([P, 2, TOPK, TOPK]), ALU.is_equal))
                done(nc.vector.tensor_tensor(
                    pk, pk, if16.rearrange("p (s i) -> p s i", s=2).unsqueeze(2).to_broadcast([P, 2, TOPK, TOPK]), ALU.mult))
                done(nc.vector.tensor_reduce(eij.rearrange("p (s k) -> p s k", s=2), pk, AX, ALU.add))
                nc.vector.scalar_tensor_tensor(out=uidx[:, p, :], in0=eij[:, 0:16], scalar=float(NKEYS),
                                               in1=eij[:, 16:32], op0=ALU.mult, op1=ALU.add).then_inc(S("uidx_ready"), 1)
                assert step[0] == ROUTE_STEPS, step[0]

            def keep_idx(u, p):
                dve.wait_ge(S("uidx_ready"), u + 1)
                nc.vector.tensor_copy(vidx[:, p, :], uidx[:, p, :]).then_inc(S("vidx_ready"), 1)

            def gates(u, p):
                dve.wait_ge(S("gex16_ready"), u + 1)
                nc.vector.reciprocal(rden, den).then_inc(S("rden_ready"), 1)
                dve.wait_ge(S("rden_ready"), u + 1)
                nc.vector.tensor_scalar(gate[:, p, :], ex16, rden, None, ALU.mult).then_inc(S("gate_ready"), 1)

            def unit_dots(u, p, turn_, tile, ks):
                for k in ks:
                    s = k % RING
                    dve.wait_ge(S(f"u_row{s}"), (turn_ + k // RING + 1) * 16)
                    nc.vector.scalar_tensor_tensor(
                        out=uring[s], in0=uring[s], scalar=1.0, in1=hn2[:, tile, :],
                        op0=ALU.mult, op1=ALU.mult, accum_out=dots[:, p, k:k + 1]).then_inc(S("u_used"), 1)

            def unit_weights(u, p):
                dve.wait_ge(S("gate_ready"), u + 1)
                dve.wait_ge(S("gelu_ready"), u + 1)
                nc.vector.tensor_tensor(gw[:, p, :], gate[:, p, :], ggel[:, p, :], ALU.mult).then_inc(S("gw_ready"), 1)

            def experts_pass(b, tile, next_tile, last):
                for p in range(2):
                    u = b * 2 + p
                    ahead = not (last and p == 1)
                    if ahead:
                        keep_idx(u + 1, 1 - p)
                        if not last:
                            route(u + 2, p)
                        of = tile if p == 0 else next_tile
                        unit_dots(u + 1, 1 - p, b * 4 + 2 * p + 2, of, range(4))
                        if not last:
                            gates(u + 2, p)
                        unit_dots(u + 1, 1 - p, b * 4 + 2 * p + 2, of, range(4, TOPK))
                        unit_weights(u + 1, 1 - p)
                    else:
                        before_last_sum()
                    dve.wait_ge(S("v_used"), u * TOPK + V_PRIME + TOPK)
                    nc.vector.tensor_tensor(h[:, tile, :], h[:, tile, :], pairs[p][:, :], ALU.add).then_inc(S("y_added"), 1)
                    dve.wait_ge(S("y_added"), u + 3)

            route(0, 0)
            keep_idx(0, 0)
            gates(0, 0)
            route(1, 1)
            unit_dots(0, 0, 0, 0, range(4))
            gates(1, 1)
            unit_dots(0, 0, 0, 0, range(4, TOPK))
            unit_weights(0, 0)
            def w2_lows(ms):
                for m in ms:
                    dve.wait_ge(S("w_in_high"), W2_FROM + m + 1)
                    c0 = W2_CHUNKS[m][0]
                    nc.vector.tensor_tensor(w2_slice(c0, R32), w2_slice(c0), w2_high(m), ALU.subtract)\
                        .then_inc(S("w_in_split"), 1)

            def uT_lows(js):
                for j in js:
                    dve.wait_ge(S("hnT_high"), UT_FROM + j + 1)
                    ks, cs = uT_part(j)
                    nc.vector.tensor_tensor(uTl[:, ks, cs], uT[:, ks, cs], uTh[:, ks, cs], ALU.subtract)\
                        .then_inc(S("hnT_split"), 1)

            def tile_norms(t):
                dve.wait_ge(S("rms_ready"), RMS_NF[t] + 1)
                link(nc.vector.reciprocal(stat[:, 2 + t:3 + t], stat[:, 2 + t:3 + t]))
                nc.vector.scalar_tensor_tensor(out=h[:, t, :], in0=h[:, t, :], scalar=stat[:, 2 + t:3 + t],
                                               in1=row[:, R_NORMF:R_NORMF + D], op0=ALU.mult, op1=ALU.mult)\
                    .then_inc(S("hf_ready"), 1)
                if t == 1:
                    uT_lows(range(4))
                normed3(t, h[:, t, :], P)

            def turned3(js):
                for j in js:
                    t = N3_ORDER[j // 2]
                    k0, n = 4 * (j % 2), ROWS[t]
                    gained("n3_turned", j, n, uT[:, k0:k0 + 4, COL0[t]:COL0[t] + n],
                           col[:, C_PREMIX + k0:C_PREMIX + k0 + 4]).then_inc(S("uT_ready"), 1)

            def normed3(t, src, n):
                dve.wait_ge(S("rms_ready"), RMS_N3[t] + 1)
                link(nc.vector.reciprocal(stat[0:n, 7 + t:8 + t], stat[0:n, 7 + t:8 + t]))
                nc.vector.tensor_scalar(nat2[0:n, t, :], src, stat[0:n, 7 + t:8 + t], None, ALU.mult).then_inc(S("n3_ready"), 1)

            def before_last_sum():
                w2_lows(range(8))
                normed3(2, hM2[0:META, :], META)
                link(nc.vector.memset(v2[:, :, :, :], 0.0))
                link(nc.vector.memset(xr[:, :, 0:CONV - 1], 0.0))
                link(nc.vector.tensor_scalar(stat[:, 60:64], col[:, C_LAM:C_LAM + 4], 0.0, None, ALU.min))
                dve.wait_ge(S("lam_ln"), 1)
                link(nc.vector.tensor_tensor(stat[:, 48:52], stat[:, 48:52], stat[:, 60:64], ALU.subtract))
                nc.vector.tensor_scalar(stat[:, 52:56], stat[:, 48:52], LRU_C, None, ALU.mult).then_inc(S("lam_ready"), 1)
                nc.vector.tensor_scalar(stat[:, 56:60], stat[:, 48:52], -LRU_C, None, ALU.mult).then_inc(S("lam_ready"), 1)

            per = PASSES // REAL
            with dve.Fori(0, per - 1) as b:
                experts_pass(b, 0, 0, False)
            experts_pass(per - 1, 0, 1, False)
            experts_pass(per, 1, 1, False)
            tile_norms(0)
            with dve.Fori(A_PASSES, PASSES - 1) as b:
                experts_pass(b, 1, 1, False)
            experts_pass(PASSES - 1, 1, 1, True)
            turned3(range(4))
            tile_norms(1)
            turned3(range(4, 6))
            uT_lows(range(4, 6))
            def evac2(kind, i):
                n = EV2[(kind, i)][0]
                dve.wait_ge(S("proj2_made"), n + 1)
                b = ps(n % 8)
                if kind == "xr":
                    ins = nc.vector.tensor_copy(xr[:, i, CONV - 1:], b[:, 0:TOK])
                elif kind == "k":
                    ins = nc.vector.tensor_copy(k2T, b[:, 0:TOK])
                else:
                    r = ROWS[i]
                    for kv in range(KVH):
                        ins = nc.vector.tensor_copy(v2[0:r, i, kv, 64 * kv:64 * kv + 64], b[0:r, 64 * kv:64 * kv + 64])
                ins.then_inc(S("evac2_v"), 1)

            for c in range(4):
                evac2("xr", c)
                dve.wait_ge(S("evac2_v"), c + 1)
                w = col[:, C_CONVW + 4 * c:C_CONVW + 4 * c + 4]
                nc.vector.tensor_scalar(xc[:, c, :], xr[:, c, 3:3 + TOK], w[:, 3:4], col[:, C_CONVB + c:C_CONVB + c + 1],
                                        ALU.mult, ALU.add).then_inc(S("conv_step"), 1)
                for k in (2, 1, 0):
                    dve.wait_ge(S("conv_step"), 4 * c + 3 - k)
                    ins = nc.vector.scalar_tensor_tensor(out=xc[:, c, :], in0=xr[:, c, k:k + TOK], scalar=w[:, k:k + 1],
                                                         in1=xc[:, c, :], op0=ALU.mult, op1=ALU.add)
                    ins.then_inc(S("conv_step"), 1)
            w2_lows(range(8, 14))
            evac2("k", 0)
            for t in range(3):
                evac2("v", t)

            def att_scores(u):
                t, hf_ = divmod(u, 2)
                nk, b = (META + P if t == 0 else SEQ), u % 2
                dve.wait_ge(S("s2_made"), u + 1)
                for half in range(2):
                    nc.vector.tensor_tensor(S2[:, b, half:4:2, 0:nk],
                                            ps(2 * b + half).rearrange("p (a b) -> p a b", a=2)[:, :, 0:nk],
                                            mask2[:, t, 0:nk].unsqueeze(1).to_broadcast([P, 2, nk]), ALU.add)\
                        .then_inc(S("s2_masked"), 1)
                dve.wait_ge(S("s2_masked"), 2 * u + 2)
                link(nc.vector.tensor_reduce(att_max[:, b, :], S2[:, b, :, 0:nk], AX, ALU.max))
                sink = row[:, R_SINK + 4 * hf_:R_SINK + 4 * hf_ + 4]
                link(nc.vector.tensor_tensor(att_max[:, b, :], att_max[:, b, :], sink, ALU.max))
                nc.vector.tensor_tensor(att_sink[:, b, :], sink, att_max[:, b, :], ALU.subtract)
                nc.vector.tensor_scalar(att_nmax[:, b, :], att_max[:, b, :], -1.0, None, ALU.mult).then_inc(S("nm_made"), 1)

            def att_divide(u):
                nk, b = (META + P if u // 2 == 0 else SEQ), u % 2
                dve.wait_ge(S("p_made"), u + 1)
                link(nc.vector.tensor_tensor(att_sum[:, b, :], att_sum[:, b, :], att_sink[:, b, :], ALU.add))
                link(nc.vector.reciprocal(att_sum[:, b, :], att_sum[:, b, :]))
                nc.vector.tensor_tensor(S2[:, b, :, 0:nk], S2[:, b, :, 0:nk],
                                        att_sum[:, b, :].unsqueeze(2).to_broadcast([P, 4, nk]), ALU.mult)\
                    .then_inc(S("p_divided"), 1)

            def att_turned(u):
                b = u % 2
                dve.wait_ge(S("p_turned"), u + 1)
                for half in range(2):
                    src = ps(4 + half).rearrange("p (a k b) -> p a k b", a=2, k=2)
                    if u // 2 == 0:
                        nc.vector.tensor_copy(pT[0:META, b, 2 * half:2 * half + 2, 0, :], src[0:META, :, 0, :])
                        ins = nc.vector.tensor_copy(pT[:, b, 2 * half:2 * half + 2, 1, :], src[:, :, 1, :])
                    else:
                        ins = nc.vector.tensor_copy(pT[:, b, 2 * half:2 * half + 2, :, :], src)
                ins.then_inc(S("pT_ready"), 1)

            def att_out(u):
                t, hf_ = divmod(u, 2)
                dve.wait_ge(S("o2_made"), u + 1)
                nc.vector.tensor_copy(mixT2[:, 2 * hf_:2 * hf_ + 2, t * P:t * P + P],
                                      ps(6 + u % 2).rearrange("p (a b) -> p a b", a=4)[:, 0:2, :]).then_inc(S("o2_ready"), 1)

            dve.wait_ge(S("mask2_ready"), 4)
            att_scores(0)
            att_scores(1)
            dve.wait_ge(S("a_made"), 4)
            link(nc.vector.tensor_tensor(lt[:, :, :], lr[:, :, :], lr[:, :, :], ALU.mult))
            nc.vector.scalar_tensor_tensor(out=lm[:, :, :], in0=lt[:, :, :], scalar=1.0, in1=lm[:, :, :], op0=ALU.add, op1=ALU.mult)\
                .then_inc(S("m2_made"), 1)
            att_divide(0)
            att_divide(1)
            link(nc.vector.tensor_tensor(li[:, :, :], li[:, :, :], xc[:, :, :], ALU.mult))
            att_turned(0)
            att_scores(2)
            att_turned(1)
            dve.wait_ge(S("root_made"), 1)
            link(nc.vector.tensor_tensor(li[:, :, :], li[:, :, :], lm[:, :, :], ALU.mult))
            att_scores(3)
            att_divide(2)
            for c in range(4):
                link(nc.vector.tensor_tensor_scan(lt[:, c, :], lr[:, c, :], li[:, c, :], 0.0, ALU.mult, ALU.add))
            att_out(0)
            att_out(1)
            dve.wait_ge(S("evac2_a"), 8)
            nc.vector.tensor_tensor(mixT2[:, 4:8, :], lt[:, :, META:TOK], geluy[:, :, :], ALU.mult).then_inc(S("rec_ready"), 1)
            att_turned(2)
            att_divide(3)

            def w_low(i, stage, c):
                dve.wait_ge(S("w_high"), (i * FF_STAGES + stage) * FF_GROUP + c + 1)
                nc.vector.tensor_tensor(ff_low(stage, c), ff_low(stage, c, F32), ff_high(stage, c), ALU.subtract).then_inc(S("w_split"), 1)

            for c in range(FF_GROUP):
                w_low(0, 0, c)
            att_turned(3)
            att_out(2)
            att_out(3)
            def uF_gained(t):
                for j in (2 * t, 2 * t + 1):
                    k0 = 4 * (j % 2)
                    gained("n4_turned", j, P, uF[:, k0:k0 + 4, t * P:t * P + P],
                           col[:, C_PREFFN + k0:C_PREFFN + k0 + 4]).then_inc(S("uF_ready"), 1)

            def uF_low(t):
                for j in (2 * t, 2 * t + 1):
                    dve.wait_ge(S("uF_high"), j + 1)
                    k0, cs = 4 * (j % 2), slice(t * P, t * P + P)
                    nc.vector.tensor_tensor(uFl[:, k0:k0 + 4, cs], uF[:, k0:k0 + 4, cs], uFh[:, k0:k0 + 4, cs],
                                            ALU.subtract).then_inc(S("uF_split"), 1)

            for t in range(REAL):
                dve.wait_ge(S("rms_ready"), RMS_PM[t] + 1)
                link(nc.vector.reciprocal(stat[:, 26 + t:27 + t], stat[:, 26 + t:27 + t]))
                link(nc.vector.scalar_tensor_tensor(out=nat2[:, t, :], in0=banks2[t][:, :], scalar=stat[:, 26 + t:27 + t],
                                               in1=row[:, R_POSTMIX:R_POSTMIX + D], op0=ALU.mult, op1=ALU.mult))
                nc.vector.tensor_tensor(h[:, t, :], h[:, t, :], nat2[:, t, :], ALU.add).then_inc(S("h_mixed2"), 1)
                if t == 1:
                    uF_gained(0)
                dve.wait_ge(S("rms_ready"), RMS_N4[t] + 1)
                link(nc.vector.reciprocal(stat[:, 30 + t:31 + t], stat[:, 30 + t:31 + t]))
                nc.vector.tensor_scalar(nat2[:, t, :], h[:, t, :], stat[:, 30 + t:31 + t], None, ALU.mult).then_inc(S("n4_ready"), 1)

            uF_low(0)
            uF_gained(1)
            uF_low(1)

            def f1_low(i, e):
                dve.wait_ge(S("f1_high"), i * 2 * FF_GROUP + e + 1)
                s, c = divmod(e, FF_GROUP)
                nc.vector.tensor_tensor(f1l[:, s, c, :], f1[:, s, c, :], f1h[:, s, c, :], ALU.subtract)\
                    .then_inc(S("f1_ready"), 1)

            def square_pair(i, last):
                for stage in range(FF_STAGES):
                    for c in range(FF_GROUP):
                        if not (last and stage == FF_STAGES - 1):
                            w_low(i + (stage + 1) // FF_STAGES, (stage + 1) % FF_STAGES, c)
                        e = stage * FF_GROUP + c
                        if stage < 2:
                            dve.wait_ge(S("relu_made"), i * 2 * FF_GROUP + e + 1)
                            nc.vector.tensor_tensor(f1[:, stage, c, :], f1[:, stage, c, :], f1[:, stage, c, :], ALU.mult)\
                                .then_inc(S("f1_squared"), 1)
                        if 1 <= e <= 2 * FF_GROUP:
                            f1_low(i, e - 1)

            with dve.Fori(0, FF_PAIRS - 1) as i:
                square_pair(i, False)
            square_pair(FF_PAIRS - 1, True)
            for t in range(REAL):
                dve.wait_ge(S("rms_ready"), RMS_PF + t + 1)
                link(nc.vector.reciprocal(stat[:, 34 + t:35 + t], stat[:, 34 + t:35 + t]))
                link(nc.vector.scalar_tensor_tensor(out=nat2[:, t, :], in0=pairs[t][:, :], scalar=stat[:, 34 + t:35 + t],
                                               in1=row[:, R_POSTFFN:R_POSTFFN + D], op0=ALU.mult, op1=ALU.mult))
                nc.vector.tensor_tensor(h[:, t, :], h[:, t, :], nat2[:, t, :], ALU.add).then_inc(S("out_ready"), 1)

        @block.tensor
        def _(pe):
            pe.sem_inc(S("v_used"), V_PRIME)
            pe.sem_inc(S("u_used"), RING)
            pe.sem_inc(S("y_added"), 2)

            def turn(src, n, j, b, made):
                for k in range(4):
                    c = 4 * (j % 2) + k
                    ins = nc.tensor.transpose(ps(b)[:, k * P:k * P + n], src[:, c * P:c * P + P], ident[0:n, 0:n])
                ins.then_inc(S(made), 1)

            pe.wait_ge(S("masks_ready"), 4)
            for j in range(6):
                t, n = j // 2, ROWS[j // 2]
                pe.wait_ge(S("n1_ready"), t + 1)
                turn(nat[0:n, t, :], n, j, j, "n1_turned")
            pe.wait_ge(S("hnT_split"), 6)

            def project(job):
                name, kind, bi, c0, t0, n = job
                nj = EV[name][0]
                q = w_in_step(bi)
                if bi == 6:
                    pe.wait_ge(S("hnT_split"), 7)
                else:
                    pe.wait_ge(S("w_in_split"), 4 * q + (c0 // P + 1 if kind == "T" else 4))
                if nj > PJ_FIRST or 8 <= nj < PJ_FIRST:
                    _, e, k = EV[PJ[nj - (8 if nj < PJ_FIRST else 1)][0]]
                    pe.wait_ge(S(f"evac_{e}"), k)
                b = ps(proj_bank(nj))
                low = blk(q % W_HELD, [KD, W_COLS], R32)
                high = blk(W_HELD + q % 2, [KD, W_COLS], R32)
                for k in range(KD):
                    for i, (wh, xh) in enumerate(((True, True), (True, False), (False, True))):
                        x_ = (hnTh if xh else hnTl)[:, k, t0:t0 + n]
                        if bi == 6:
                            out_, w, x_ = b[0:RANK, 0:n], (wlasth if wh else wlastl)[:, k, :], x_
                        elif kind == "T":
                            out_, w = b[:, 0:n], (high if wh else low)[:, k, c0:c0 + P]
                        else:
                            out_, w, x_ = b[0:n, :], x_, (high if wh else low)[:, k, :]
                        ins = nc.tensor.matmul(out_, w, x_, start=(k == 0 and i == 0), stop=(k == KD - 1 and i == 2))
                ins.then_inc(S("proj_made"), 1)

            for job in PJ[:PJ_FIRST]:
                project(job)
            pe.wait_ge(S("narrow_loaded"), 32)
            for eng in "va":
                pe.wait_ge(S(f"evac_{eng}"), max(k for n, e, k in EV.values() if e == eng and n < PJ_FIRST))
            for c in range(2):
                ins = nc.tensor.matmul(ps(c)[:, 0:TOK], wgate[:, c * P:c * P + P], glrT[0:RANK, :], start=True, stop=True)
            ins.then_inc(S("lg_made"), 1)

            def mm(o, a, b, start, stop):
                return nc.tensor.matmul(o, a, b, start=start, stop=stop, skip_group_check=True)

            def sb_scores(i):
                c, r = i // 2, slice(64 * (i % 2), 64 * (i % 2) + 64)
                z = pairs[i % 2]
                if i >= 2:
                    pe.wait_ge(S("aT_made"), i - 1)
                mm(z[:, 0:256], sbkT[r, c, META:META + P], sbqT[r, c, :], True, False)
                mm(z[:, 256:512], sbkT[r, c, 0:P], sbqT[r, c, :], False, False)
                mm(z[:, 512:640], sbkT[r, c, META + P:TOK], sbqT[r, c, P:SEQ], True, False).then_inc(S("z_made"), 1)

            def sb_sums(i):
                z = pairs[i % 2]
                s = sp[:, i % 2, :]
                pe.wait_ge(S("sp_masked"), i + 1)
                mm(z[:, 0:256], ntri[:, :], s[:, 0:256], False, False)
                mm(z[:, 128:256], neg1[:, :], s[:, 512:640], False, True)
                mm(z[0:META, 256:512], ntri[0:META, 0:META], s[0:META, 256:512], False, False)
                mm(z[0:META, 256:512], neg1[:, 0:META], s[:, 0:256], False, False)
                mm(z[0:META, 384:512], neg1[:, 0:META], s[:, 512:640], False, True)
                mm(z[:, 512:640], ntri[:, :], s[:, 512:640], False, True).then_inc(S("s_made"), 1)

            def sb_values(i):
                a = aT[:, i % 2, :]
                cs = slice(64 * i, 64 * i + 64)
                pe.wait_ge(S("aT_masked"), i + 1)
                if i >= 1:
                    pe.wait_ge(S("os_ready"), i)
                oA, oB = ps(2)[:, 0:SB_DIM], ps(2)[:, SB_DIM:2 * SB_DIM]
                mm(oA, a[0:META, 256:384], sbv[0:META, 2, cs], True, False)
                mm(oA, a[:, 0:P], sbv[:, 0, cs], False, True)
                mm(oB, a[0:META, 384:512], sbv[0:META, 2, cs], True, False)
                mm(oB, a[:, P:SEQ], sbv[:, 0, cs], False, False)
                mm(oB, a[:, 512:640], sbv[:, 1, cs], False, True).then_inc(S("pv_made"), 1)

            def state_keys(c, n, kl, upd):
                if upd >= 1:
                    pe.wait_ge(S("state_ready"), upd)
                nc.tensor.transpose(ps(0)[0:n, 256:256 + P], kl, ident[:, :]).then_inc(S("klT_made"), 1)

            def state_product(c, n, v, upd):
                pe.wait_ge(S("klnat_ready"), upd + 1)
                mm(ps(0)[:, 0:256], klnat[0:n, c, :], v, True, True).then_inc(S("st_prod"), 1)

            def gla_scores(u):
                g = gex[:, u % 3, :]
                pe.wait_ge(S("gla_f"), u + 1)
                if u >= 1:
                    pe.wait_ge(S("attT_ready"), 2 * u)
                pe.wait_ge(S("state_ready"), min(u + 2, 4))
                for hp in range(2):
                    if hp == 1:
                        pe.wait_ge(S("att_made"), 2 * u + 1)
                    r = slice(64 * hp, 64 * hp + 64)
                    a = 0
                    for j in range(NSUB):
                        n = P - SUB * j
                        ins = mm(ps(0)[:, hp * P + SUB * j:hp * P + P], kzpad[r, u % 2, j, :], g[r, a:a + n], j == 0, j == NSUB - 1)
                        a += n
                    ins.then_inc(S("att_made"), 1)

            def gla_values(u):
                t, c = divmod(u, 2)
                g = gex[:, u % 3, :]
                pe.wait_ge(S("state_ready"), 2 * t + c + 1)
                if u >= 1:
                    pe.wait_ge(S("og_ready"), u)
                for hp in range(2):
                    v, r, hd = 2 * u + hp, slice(64 * hp, 64 * hp + 64), 2 * c + hp
                    o = ps(3)[:, hp * DV:hp * DV + DV]
                    if v >= 1:
                        pe.wait_ge(S("o_made"), v)
                    mm(o, g[r, 448:576], state[r, c, :], True, False)
                    pe.wait_ge(S("attT_ready"), v + 1)
                    mm(o, attT[:, hp, :], gv[:, t, hd * DV:hd * DV + DV], False, True).then_inc(S("o_made"), 1)

            for i in range(SB_HEADS + 2):
                if i < SB_HEADS:
                    if i >= 2 and i % 2 == 0:
                        pe.wait_ge(S("evac_a"), EV[("sbk", i // 2)][2])
                    sb_scores(i)
                if i in PJ_LATER:
                    if i == 0:
                        pe.wait_ge(S("lg_ln"), 1)
                        pe.wait_ge(S("lg_min"), 2)
                    project(PJ[PJ_LATER[i]])
                if 1 <= i <= SB_HEADS:
                    sb_sums(i - 1)
                u = i - 4
                if 0 <= u < GLA_UNITS:
                    gla_values(u)
                    if u < 2:
                        pe.wait_ge(S("o_made"), 2 * u + 2)
                        state_keys(u, P, gex[:, u, 576:704], 2 + u)
                if i == 2:
                    for c in range(2):
                        pe.wait_ge(S("klM_ready"), c + 1)
                        state_keys(c, META, gexM[:, c, :], c)
                        state_product(c, META, gv[0:META, 2, 256 * c:256 * c + 256], c)
                if i >= 2:
                    sb_values(i - 2)
                if u in (0, 1):
                    state_product(u, P, gv[:, 0, 256 * u:256 * u + 256], 2 + u)
                if 0 <= i - 3 < GLA_UNITS:
                    gla_scores(i - 3)
            for half in range(2):
                for t in range(REAL):
                    pe.wait_ge(S("mixn_ready"), REAL * half + t + 1)
                    turn(mixn[:, t, :], P, half, 4 + REAL * half + t, "mix_turned")
            for t in range(REAL):
                pe.wait_ge(S("mixT_v"), t + 1)
                pe.wait_ge(S("mixT_a"), t + 1)
                for i in range(2):
                    pe.wait_ge(S(f"w_out_loaded{i}"), 16)
                    for k in range(KD):
                        ins = nc.tensor.matmul(ps(2 * t + i), mixT[:, k, t * P:t * P + P], w_slice(2 + i, 0, W_COLS)[:, k, :],
                                               start=(k == 0), stop=(k == KD - 1))
                ins.then_inc(S("mix_made"), 1)
            for j in range(4):
                pe.wait_ge(S("hn2_ready"), j // 2 + 1)
                turn(hn2[:, j // 2, :], P, j, 4 + j, "n2_turned")
            pe.wait_ge(S("hn2T_ready"), 4)
            pe.wait_ge(S("w_pq_loaded"), 32)
            def head_scores(hd):
                pe.wait_ge(S("qpT_ready"), hd + 1)
                for t in range(REAL):
                    if hd >= 1:
                        pe.wait_ge(S("score_ready"), REAL * (hd - 1) + t + 1)
                    for half in range(2):
                        r = slice(64 * half, 64 * half + 64)
                        ins = mm(ps(4 + 2 * t + half)[:, 0:P], qpT[r, hd, t * P:t * P + P], keyT[r, hd, :], True, True)
                    ins.then_inc(S("score_made"), 1)

            for c in range(HEADS):
                if c >= 4:
                    pe.wait_ge(S("qpT_ready"), c - 3)
                for k in range(KD):
                    ins = nc.tensor.matmul(ps(c % 4)[:, 0:SEQ], w_slice(4 + c // 4, (c % 4) * P, P)[:, k, :], hn2T[:, k, :],
                                           start=(k == 0), stop=(k == KD - 1))
                ins.then_inc(S("pq_made"), 1)
                if c == 0:
                    pe.wait_ge(S("keys_loaded"), 16)
                else:
                    head_scores(c - 1)
            head_scores(HEADS - 1)
            pe.wait_ge(S("score_ready"), UNITS)
            with pe.Fori(0, PASSES) as b:
                for p in range(2):
                    pe.wait_ge(S("y_added"), b * 2 + p + 1)
                    for k in range(TOPK):
                        s = k % RING
                        pe.wait_ge(S("diag_ready"), (b * 2 + p) * TOPK + k + 1)
                        pe.wait_ge(S(f"v_row{s}"), (b * 4 + 2 * p + k // RING + 1) * 16)
                        for half in range(2):
                            ins = nc.tensor.matmul(pairs[p][:, 512 * half:512 * half + 512], diag[:, k, :],
                                                   vring[s][:, 512 * half:512 * half + 512],
                                                   start=(k == 0), stop=(k == TOPK - 1))
                        ins.then_inc(S("v_used"), 1)
            for j in range(6):
                t = N3_ORDER[j // 2]
                n = ROWS[t]
                pe.wait_ge(S("n3_ready"), j // 2 + 1)
                turn(nat2[0:n, t, :], n, j, j, "n3_turned")
            pe.wait_ge(S("hnT_split"), UT_FROM + 6)

            def project2(job):
                name, kind, c0, t0, n = job
                nj = EV2[name][0]
                m = [c[0] for c in W2_CHUNKS].index(c0)
                pe.wait_ge(S("w_in_split"), W2_FROM + m + 1)
                if nj >= 8:
                    _, e, k = EV2[PJ2[nj - 8][0]]
                    pe.wait_ge(S(f"evac2_{e}"), k)
                b = ps(nj % 8)
                wh, wl = w2_high(m), w2_slice(c0, R32)
                for k in range(KD):
                    for i, (w, x_) in enumerate(((wh, uTh), (wh, uTl), (wl, uTh))):
                        x_ = x_[:, k, t0:t0 + n]
                        if kind == "T":
                            ins = nc.tensor.matmul(b[:, 0:n], w[:, k, :], x_, start=(k == 0 and i == 0),
                                                   stop=(k == KD - 1 and i == 2))
                        else:
                            ins = nc.tensor.matmul(b[0:n, 0:P], x_, w[:, k, :], start=(k == 0 and i == 0),
                                                   stop=(k == KD - 1 and i == 2))
                ins.then_inc(S("proj2_made"), 1)

            for job in PJ2[:12]:
                project2(job)
            pe.wait_ge(S("wbd_loaded"), 64)
            pe.wait_ge(S("evac2_a"), 4)
            for c in range(4):
                pe.wait_ge(S("conv_step"), 4 * c + 4)
                if c >= 2:
                    pe.wait_ge(S("sig_made"), c - 1)
                for g in range(2):
                    ins = nc.tensor.matmul(pairs[c % 2][:, 512 * g:512 * g + TOK], wbd[:, g, c, :], xc[:, c, :],
                                           start=True, stop=True)
                ins.then_inc(S("lru_made"), 1)

            def att2_scores(u):
                t, hf_ = divmod(u, 2)
                k0, nk = (0, META + P) if t == 0 else (META, SEQ)
                if u >= 2:
                    pe.wait_ge(S("s2_masked"), 2 * u - 2)
                for j in range(4):
                    c, kv = 2 * hf_ + j // 2, j % 2
                    r = slice(64 * kv, 64 * kv + 64)
                    ins = mm(ps(2 * (u % 2) + kv)[:, (j // 2) * 256:(j // 2) * 256 + nk], q2T[r, c, t * P:t * P + P],
                             k2T[r, k0:k0 + nk], True, True)
                ins.then_inc(S("s2_made"), 1)

            def keys_of(u):
                return [(META, 0), (P, META)] if u // 2 == 0 else [(P, 0), (P, P)]

            def att2_turn(u):
                pe.wait_ge(S("p_divided"), u + 1)
                if u >= 1:
                    pe.wait_ge(S("pT_ready"), u)
                for j in range(4):
                    for i, (n, a) in enumerate(keys_of(u)):
                        ins = nc.tensor.transpose(ps(4 + j // 2)[0:n, (j % 2) * 256 + i * P:(j % 2) * 256 + i * P + P],
                                                  S2[:, u % 2, j, a:a + n], ident[:, :])
                ins.then_inc(S("p_turned"), 1)

            def att2_values(u):
                pe.wait_ge(S("pT_ready"), u + 1)
                if u >= 2:
                    pe.wait_ge(S("o2_ready"), u - 1)
                tiles = [2, 0] if u // 2 == 0 else [0, 1]
                for cc in range(2):
                    o = ps(6 + u % 2)[:, cc * P:cc * P + P]
                    for kv in range(2):
                        for i in range(2):
                            n = keys_of(u)[i][0]
                            ins = mm(o, v2[0:n, tiles[i], kv, :], pT[0:n, u % 2, 2 * cc + kv, i, :],
                                     kv == 0 and i == 0, kv == 1 and i == 1)
                ins.then_inc(S("o2_made"), 1)

            def mix_product2(t):
                pe.wait_ge(S("w_out2_loaded"), 32)
                pe.wait_ge(S("s2_masked"), 6 + 2 * t)
                pe.wait_ge(S("o2_ready"), 2 * t + 2)
                pe.wait_ge(S("rec_ready"), 1)
                for i in range(2):
                    for k in range(KD):
                        ins = nc.tensor.matmul(banks2[t][:, 512 * i:512 * i + 512], mixT2[:, k, t * P:t * P + P],
                                               w_slice(2 + i, 0, W_COLS)[:, k, :], start=(k == 0), stop=(k == KD - 1))
                ins.then_inc(S("mix2_made"), 1)

            pe.wait_ge(S("evac2_v"), 8)
            att2_scores(0)
            att2_scores(1)
            pe.wait_ge(S("sig_made"), 4)
            for job in PJ2[12:]:
                project2(job)
            att2_scores(2)
            pe.wait_ge(S("evac2_a"), 8)
            att2_turn(0)
            att2_scores(3)
            att2_turn(1)
            att2_values(0)
            att2_values(1)
            att2_turn(2)
            mix_product2(0)
            att2_turn(3)
            att2_values(2)
            att2_values(3)
            mix_product2(1)
            for j in range(4):
                pe.wait_ge(S("n4_ready"), j // 2 + 1)
                turn(nat2[:, j // 2, :], P, j, j, "n4_turned")
            pe.wait_ge(S("uF_split"), 4)

            def ff_pair(i, first, last):
                for stage in range(FF_STAGES):
                    s = stage % 2
                    for c in range(FF_GROUP):
                        e = s * FF_GROUP + c
                        pe.wait_ge(S("w_split"), (i * FF_STAGES + stage) * FF_GROUP + c + 1)
                        wh, wl = ff_high(stage, c), ff_low(stage, c)
                        if stage < 2:
                            if not (first and s == 0):
                                pe.wait_ge(S("relu_made"), (i * 2 + s) * FF_GROUP + c - 3)
                            for k in range(KD):
                                for n, (w, x_) in enumerate(((wh, uFh), (wh, uFl), (wl, uFh))):
                                    ins = nc.tensor.matmul(ps(c)[:, 0:SEQ], w[:, k, :], x_[:, k, :],
                                                           start=(k == 0 and n == 0), stop=(k == KD - 1 and n == 2))
                            ins.then_inc(S("f1_made"), 1)
                        else:
                            pe.wait_ge(S("f1_ready"), i * 2 * FF_GROUP + e + 1)
                            for t in range(REAL):
                                for n, (f, w) in enumerate(((f1h, wh), (f1h, wl), (f1l, wh))):
                                    for half in range(2):
                                        ins = mm(pairs[t][:, 512 * half:512 * half + 512],
                                                 f[:, s, c, t * P:t * P + P], w[:, 512 * half:512 * half + 512],
                                                 first and e == 0 and n == 0, last and e == 2 * FF_GROUP - 1 and n == 2)
                    if stage >= 2:
                        ins.then_inc(S("f2_group"), 1)

            ff_pair(0, True, False)
            with pe.Fori(1, FF_PAIRS - 1) as i:
                ff_pair(i, False, False)
            ff_pair(FF_PAIRS - 1, False, True)


def kernel(**inputs):
    import numpy as np
    import concourse.bacc as bacc
    from concourse.bass_utils import run_bass_kernel_spmd

    a = {k: np.asarray(v) for k, v in inputs.items()}

    def chunks(v):
        return v.reshape(-1, P).T

    cols = np.concatenate([
        chunks(a["norm1_g"][0]), chunks(a["g_pre_mix_2"][0]), chunks(a["g_pre_ffn_2"][0]), chunks(a["b_gate_up"][0]),
        a["conv_w_2"][0].reshape(CONV, 4, P).transpose(2, 1, 0).reshape(P, 16), chunks(a["conv_b_2"][0]),
        chunks(a["b_a_2"][0]), chunks(a["b_x_2"][0]), chunks(a["lru_lambda_2"][0])], axis=1)
    sinks = a["attn_sinks_2"][0].reshape(KVH, 4).T.reshape(-1)
    rows = np.concatenate([a["sb_norm_g"][0], a["gla_norm_g"][0], a["norm2_g"][0], a["norm_f_g"], a["g_post_mix_2"][0],
                           a["g_post_ffn_2"][0], sinks])
    keys = np.stack([a["sub_keys1"][0], a["sub_keys2"][0]]).transpose(0, 3, 1, 2).reshape(P, HEADS, NKEYS)
    w_in2 = a["w_in_2"][0]
    q = w_in2[:, 0:512].reshape(D, KVH, 4, 64).transpose(0, 2, 1, 3).reshape(D, 512)
    w_in2 = np.concatenate([q, w_in2[:, 512:]], axis=1)
    w_out2 = a["w_out_2"][0]
    o = w_out2[0:512].reshape(KVH, 4, 64, D).transpose(1, 0, 2, 3).reshape(512, D)
    w_out2 = np.concatenate([o, w_out2[512:]], axis=0)
    arrays = {
        "x": a["x"][0], "meta1": a["meta_tokens"], "meta2": a["meta_tokens_2"], "cols": cols, "rows": rows,
        "w_in": a["w_in"][0], "w_gate": a["w_gate_up"][0], "w_out": a["w_out"][0], "w_peer_q": a["w_peer_q"][0],
        "keys": keys, "expert_u": a["expert_u"][0], "expert_v": a["expert_v"][0], "w_in2": w_in2, "w_a": a["w_a_2"][0],
        "w_x": a["w_x_2"][0], "w_out2": w_out2, "w_ff1": a["w_ff1_2"][0], "w_ff2": a["w_ff2_2"][0],
    }
    nc = bacc.Bacc("TRN2", target_bir_lowering=False, num_devices=1)
    feed, args = {}, []
    for name, v in arrays.items():
        v = np.ascontiguousarray(v)
        feed[f"in_{name}"] = v
        args.append(nc.dram_tensor(f"in_{name}", v.shape, F32, kind="ExternalInput").ap())
    out = nc.dram_tensor("out", (SEQ, D), F32, kind="ExternalOutput").ap()
    two_blocks_kernel(nc, *args, out)
    r = run_bass_kernel_spmd(nc, [feed], core_ids=[0])
    return r.results[0]["out"].reshape(1, SEQ, D)
```
